# Optimizing a Trainium2 kernel written in Bass

```python
import jax, jax.numpy as jnp
from jax import lax
import numpy as np
import math

D_MODEL = 1024
BATCH = 1
SEQ = 256
DEPTH = 2

N_MIXERS = 2
N_LRU = (DEPTH + 1) // 2
N_FOX = DEPTH // 2
D_RNN = D_MODEL
LRU_BLOCKS = 16
LRU_BLOCK_DIM = D_RNN // LRU_BLOCKS
CONV_WIDTH = 4
LRU_C = 8.0
N_HEADS = 16
HEAD_DIM = D_MODEL // N_HEADS
Q_BLOCK = 128
D_FF = 4 * D_MODEL
EPS = 1e-6
NEG_INF = -1e30


def rms_norm(x, g):
    xf = x.astype(jnp.float32)
    y = xf * lax.rsqrt(jnp.mean(xf * xf, axis=-1, keepdims=True) + EPS)
    return (y * g.astype(jnp.float32)).astype(x.dtype)

def causal_depthwise_conv(x, w, b):
    S = x.shape[1]
    xp = jnp.pad(x, ((0, 0), (CONV_WIDTH - 1, 0), (0, 0)))
    y = b
    for k in range(CONV_WIDTH):
        y = y + xp[:, k:k + S] * w[k]
    return y

def rglru_mixer(h, w_in, conv_w, conv_b, w_r, b_r, w_i, b_i, lam, w_out):
    B, S, _ = h.shape
    u = h @ w_in
    gate_branch, x_branch = jnp.split(u, 2, axis=-1)
    gate_branch = jax.nn.gelu(gate_branch)
    xc = causal_depthwise_conv(x_branch, conv_w, conv_b)
    xb = xc.reshape(B, S, LRU_BLOCKS, LRU_BLOCK_DIM)
    r = jax.nn.sigmoid((jnp.einsum('bsnd,nde->bsne', xb, w_r) + b_r).astype(jnp.float32))
    i = jax.nn.sigmoid((jnp.einsum('bsnd,nde->bsne', xb, w_i) + b_i).astype(jnp.float32))
    r = r.reshape(B, S, D_RNN)
    i = i.reshape(B, S, D_RNN)
    log_a = LRU_C * r * jax.nn.log_sigmoid(lam.astype(jnp.float32))
    a = jnp.exp(log_a)
    mult = jnp.sqrt(-jnp.expm1(2.0 * log_a))
    bt = mult * (i * xc.astype(jnp.float32))

    def combine(left, right):
        a_l, b_l = left
        a_r, b_r_ = right
        return a_l * a_r, a_r * b_l + b_r_

    _, hs = lax.associative_scan(combine, (a, bt), axis=1)
    y = gate_branch * hs.astype(h.dtype)
    return y @ w_out

def fox_mixer(h, w_in, b_f, q_gain, k_gain, w_out):
    B, S, _ = h.shape
    u = h @ w_in
    q, k, v, f_logit = jnp.split(u, [D_MODEL, 2 * D_MODEL, 3 * D_MODEL], axis=-1)

    def heads(t):
        return t.reshape(B, S, N_HEADS, HEAD_DIM).transpose(0, 2, 1, 3)

    q = rms_norm(heads(q), q_gain)
    k = rms_norm(heads(k), k_gain)
    v = heads(v)
    log_f = jax.nn.log_sigmoid((f_logit + b_f).astype(jnp.float32))
    c = jnp.cumsum(log_f, axis=1).transpose(0, 2, 1)
    scale = HEAD_DIM ** -0.5
    nb = S // Q_BLOCK
    q_blocks = q.reshape(B, N_HEADS, nb, Q_BLOCK, HEAD_DIM).transpose(2, 0, 1, 3, 4)
    c_blocks = c.reshape(B, N_HEADS, nb, Q_BLOCK).transpose(2, 0, 1, 3)
    k_pos = jnp.arange(S)

    def attend(args):
        qb, cb, blk = args
        q_pos = blk * Q_BLOCK + jnp.arange(Q_BLOCK)
        s = jnp.einsum('bhqd,bhkd->bhqk', qb, k).astype(jnp.float32) * scale
        s = s + cb[..., :, None] - c[:, :, None, :]
        s = jnp.where(k_pos[None, :] <= q_pos[:, None], s, NEG_INF)
        p = jax.nn.softmax(s, axis=-1)
        return jnp.einsum('bhqk,bhkd->bhqd', p.astype(v.dtype), v)

    o = lax.map(attend, (q_blocks, c_blocks, jnp.arange(nb)))
    o = o.transpose(1, 0, 3, 2, 4).reshape(B, S, D_MODEL)
    return o @ w_out

def sq_relu_mlp(h, w1, w2):
    return jnp.square(jax.nn.relu(h @ w1)) @ w2

def first_inputs(seed: int = 0) -> dict:
    key = jax.random.key(seed)
    ks = jax.random.split(key, 20)
    f32 = jnp.float32
    nrm = lambda k, shape, fan_in: jax.random.normal(k, shape, f32) * (fan_in ** -0.5)
    a0 = jax.random.uniform(ks[12], (N_LRU, D_RNN), f32, minval=0.9, maxval=0.999)
    return {
        "x": jax.random.normal(ks[0], (BATCH, SEQ, D_MODEL), f32),
        "mix_norm": 1.0 + 0.02 * jax.random.normal(ks[1], (DEPTH, D_MODEL), f32),
        "mlp_norm": 1.0 + 0.02 * jax.random.normal(ks[2], (DEPTH, D_MODEL), f32),
        "mlp_w1": nrm(ks[3], (DEPTH, D_MODEL, D_FF), D_MODEL),
        "mlp_w2": nrm(ks[4], (DEPTH, D_FF, D_MODEL), D_FF),
        "lru_w_in": nrm(ks[5], (N_LRU, D_MODEL, 2 * D_RNN), D_MODEL),
        "lru_conv_w": nrm(ks[6], (N_LRU, CONV_WIDTH, D_RNN), CONV_WIDTH),
        "lru_conv_b": 0.02 * jax.random.normal(ks[7], (N_LRU, D_RNN), f32),
        "lru_w_r": nrm(ks[8], (N_LRU, LRU_BLOCKS, LRU_BLOCK_DIM, LRU_BLOCK_DIM), LRU_BLOCK_DIM),
        "lru_b_r": 0.1 * jax.random.normal(ks[9], (N_LRU, LRU_BLOCKS, LRU_BLOCK_DIM), f32),
        "lru_w_i": nrm(ks[10], (N_LRU, LRU_BLOCKS, LRU_BLOCK_DIM, LRU_BLOCK_DIM), LRU_BLOCK_DIM),
        "lru_b_i": 0.1 * jax.random.normal(ks[11], (N_LRU, LRU_BLOCKS, LRU_BLOCK_DIM), f32),
        "lru_lambda": jnp.log(a0) - jnp.log1p(-a0),
        "lru_w_out": nrm(ks[13], (N_LRU, D_RNN, D_MODEL), D_RNN),
        "fox_w_in": nrm(ks[14], (N_FOX, D_MODEL, 3 * D_MODEL + N_HEADS), D_MODEL),
        "fox_b_f": jax.random.uniform(ks[15], (N_FOX, N_HEADS), f32, minval=1.0, maxval=6.0),
        "fox_q_gain": 1.0 + 0.02 * jax.random.normal(ks[16], (N_FOX, HEAD_DIM), f32),
        "fox_k_gain": 1.0 + 0.02 * jax.random.normal(ks[17], (N_FOX, HEAD_DIM), f32),
        "fox_w_out": nrm(ks[18], (N_FOX, D_MODEL, D_MODEL), D_MODEL),
    }

def first_block(x, mix_norm, mlp_norm, mlp_w1, mlp_w2, lru_w_in, lru_conv_w, lru_conv_b,
              lru_w_r, lru_b_r, lru_w_i, lru_b_i, lru_lambda, lru_w_out,
              fox_w_in, fox_b_f, fox_q_gain, fox_k_gain, fox_w_out):
    for layer in range(DEPTH):
        h = rms_norm(x, mix_norm[layer])
        j = layer // N_MIXERS
        if layer % N_MIXERS == 0:
            mixed = rglru_mixer(h, lru_w_in[j], lru_conv_w[j], lru_conv_b[j], lru_w_r[j],
                                lru_b_r[j], lru_w_i[j], lru_b_i[j], lru_lambda[j], lru_w_out[j])
        else:
            mixed = fox_mixer(h, fox_w_in[j], fox_b_f[j], fox_q_gain[j], fox_k_gain[j],
                              fox_w_out[j])
        x = x + mixed
        x = x + sq_relu_mlp(rms_norm(x, mlp_norm[layer]), mlp_w1[layer], mlp_w2[layer])
    return x


DEPTH_2 = 1

SB_WIDTH = D_MODEL // 2
SB_HEAD_DIM = 64
SB_HEADS = SB_WIDTH // SB_HEAD_DIM
SB_BLOCK = 128
HGRN_WIDTH = D_MODEL // 2
HGRN_HEAD_DIM = 128
HGRN_HEADS = HGRN_WIDTH // HGRN_HEAD_DIM
HGRN_CHUNK = 64
N_EXPERTS = 32
TOP_K = 4
D_FF_2 = D_MODEL
SWIGLU_ALPHA = 1.702
SWIGLU_LIMIT = 7.0
EXPERT_BLOCK = 128
DEEPNORM_ALPHA = (2 * DEPTH_2) ** 0.25
DEEPNORM_BETA = (8 * DEPTH_2) ** -0.25
LN_EPS = 1e-5
RMS_EPS = 1e-6
IN_SPLITS = (SB_WIDTH, SB_WIDTH, SB_WIDTH, HGRN_WIDTH, HGRN_WIDTH, HGRN_WIDTH, HGRN_WIDTH, D_MODEL, D_MODEL)
IN_WIDTH = sum(IN_SPLITS)


def layer_norm(x, g, b):
    xf = x.astype(jnp.float32)
    mu = jnp.mean(xf, axis=-1, keepdims=True)
    var = jnp.mean(jnp.square(xf - mu), axis=-1, keepdims=True)
    return ((xf - mu) * lax.rsqrt(var + LN_EPS) * g + b).astype(x.dtype)

def stick_breaking_attention(q, k, v):
    T = q.shape[2]
    scale = SB_HEAD_DIM ** -0.5
    qf, kf, vf = q.astype(jnp.float32), k.astype(jnp.float32), v.astype(jnp.float32)
    outs = []
    for blk in range(T // SB_BLOCK):
        t0 = blk * SB_BLOCK
        t1 = t0 + SB_BLOCK
        z = jnp.einsum('bhtd,bhsd->bhts', qf[:, :, t0:t1], kf[:, :, :t1]) * scale
        mask = jnp.arange(t1)[None, :] < (t0 + jnp.arange(SB_BLOCK))[:, None]
        log_keep = jnp.where(mask, jax.nn.log_sigmoid(-z), 0.0)
        log_after = lax.cumsum(log_keep, axis=3, reverse=True) - log_keep
        weights = jnp.where(mask, jnp.exp(jax.nn.log_sigmoid(z) + log_after), 0.0)
        outs.append(jnp.einsum('bhts,bhsd->bhtd', weights, vf[:, :, :t1]))
    return jnp.concatenate(outs, axis=2).astype(q.dtype)

def hgrn2_recurrence(q, k, logf, v):
    B, T, H, dk = q.shape
    dv = v.shape[-1]
    n_chunks = T // HGRN_CHUNK

    def to_chunks(a):
        return a.reshape(B, n_chunks, HGRN_CHUNK, H, a.shape[-1]).transpose(1, 0, 3, 2, 4)

    causal = jnp.tril(jnp.ones((HGRN_CHUNK, HGRN_CHUNK), dtype=bool))

    def step(S, xs):
        qc, kc, gc, vc = xs
        b = jnp.cumsum(gc, axis=2)
        o_inter = jnp.einsum('bhtk,bhkv->bhtv', qc * jnp.exp(b), S)
        diff = b[:, :, :, None, :] - b[:, :, None, :, :]
        decay = jnp.exp(jnp.where(causal[:, :, None], diff, -jnp.inf))
        scores = jnp.einsum('bhtsk,bhsk->bhts', qc[:, :, :, None, :] * decay, kc)
        o = o_inter + jnp.einsum('bhts,bhsv->bhtv', scores, vc)
        b_last = b[:, :, -1:, :]
        S_new = jnp.exp(b_last[:, :, 0, :])[..., None] * S + jnp.einsum(
            'bhsk,bhsv->bhkv', kc * jnp.exp(b_last - b), vc)
        return S_new, o

    S0 = jnp.zeros((B, H, dk, dv), jnp.float32)
    _, o = lax.scan(step, S0, (to_chunks(q), to_chunks(k), to_chunks(logf), to_chunks(v)))
    return o.transpose(1, 0, 3, 2, 4).reshape(B, T, H, dv)

def hybrid_mixer(x, w_in, lower_bound, hgrn_norm_g, w_branch_sb, w_branch_hgrn, w_out):
    B, T, _ = x.shape
    proj = x @ w_in
    offsets = np.cumsum(IN_SPLITS)[:-1].tolist()
    sq, sk, sv, hq, hf, hi, hg, gate_sb, gate_hg = jnp.split(proj, offsets, axis=-1)

    def heads(a):
        return a.reshape(B, T, SB_HEADS, SB_HEAD_DIM).transpose(0, 2, 1, 3)
    o_sb = stick_breaking_attention(heads(sq), heads(sk), heads(sv))
    o_sb = o_sb.transpose(0, 2, 1, 3).reshape(B, T, SB_WIDTH)

    f = lower_bound + (1.0 - lower_bound) * jax.nn.sigmoid(hf.astype(jnp.float32))
    shp = (B, T, HGRN_HEADS, HGRN_HEAD_DIM)
    o_hg = hgrn2_recurrence(jax.nn.silu(hq.astype(jnp.float32)).reshape(shp),
                            (1.0 - f).reshape(shp),
                            jnp.log(f).reshape(shp),
                            hi.astype(jnp.float32).reshape(shp))
    o_hg = o_hg * lax.rsqrt(jnp.mean(jnp.square(o_hg), axis=-1, keepdims=True) + RMS_EPS)
    o_hg = (o_hg.reshape(B, T, HGRN_WIDTH) * hgrn_norm_g * jax.nn.sigmoid(hg.astype(jnp.float32))).astype(x.dtype)

    merged = jax.nn.sigmoid(gate_sb) * (o_sb @ w_branch_sb) + jax.nn.sigmoid(gate_hg) * (o_hg @ w_branch_hgrn)
    return merged @ w_out

def moe(h, router_w, router_b, w_up, b_up, w_down, b_down):
    B, T, D = h.shape
    N = B * T
    xt = h.reshape(N, D)
    logits = (xt @ router_w + router_b).astype(jnp.float32)
    top_vals, top_idx = lax.top_k(logits, TOP_K)
    gates = jax.nn.softmax(top_vals, axis=-1)

    e_flat = top_idx.reshape(-1)
    tok_flat = jnp.arange(N * TOP_K, dtype=jnp.int32) // TOP_K
    order = jnp.argsort(e_flat)
    e_sorted = e_flat[order]
    tok_sorted = tok_flat[order]
    gate_sorted = gates.reshape(-1)[order].astype(h.dtype)

    counts = jnp.bincount(e_flat, length=N_EXPERTS)
    padded = (counts + EXPERT_BLOCK - 1) // EXPERT_BLOCK * EXPERT_BLOCK
    start = jnp.cumsum(counts) - counts
    pad_end = jnp.cumsum(padded)
    pad_start = pad_end - padded
    dest = pad_start[e_sorted] + (jnp.arange(N * TOP_K) - start[e_sorted])

    cap = N * TOP_K + N_EXPERTS * (EXPERT_BLOCK - 1)
    n_blocks = -(-cap // EXPERT_BLOCK)
    n_slots = n_blocks * EXPERT_BLOCK
    slot_tok = jnp.full((n_slots,), N, dtype=jnp.int32).at[dest].set(tok_sorted)
    x_pad = jnp.concatenate([xt, jnp.zeros((1, D), xt.dtype)], axis=0)
    xb = x_pad[slot_tok].reshape(n_blocks, EXPERT_BLOCK, D)
    block_e = jnp.minimum(jnp.searchsorted(pad_end, jnp.arange(n_blocks) * EXPERT_BLOCK, side='right'),
                          N_EXPERTS - 1)

    def expert_block(args):
        xblk, e = args
        hcat = xblk @ w_up[e] + b_up[e]
        x_glu = jnp.minimum(hcat[:, 0::2], SWIGLU_LIMIT)
        x_lin = jnp.clip(hcat[:, 1::2], -SWIGLU_LIMIT, SWIGLU_LIMIT)
        act = x_glu * jax.nn.sigmoid(SWIGLU_ALPHA * x_glu) * (x_lin + 1.0)
        return act @ w_down[e] + b_down[e]

    y_slots = lax.map(expert_block, (xb, block_e)).reshape(n_slots, D)
    contrib = y_slots[dest] * gate_sorted[:, None]
    out = jax.ops.segment_sum(contrib, tok_sorted, num_segments=N)
    return out.reshape(B, T, D).astype(h.dtype)

def second_inputs(seed: int = 0) -> dict:
    key = jax.random.key(seed)
    ks = jax.random.split(key, 18)
    nrm = jax.random.normal
    beta = DEEPNORM_BETA
    col_scale = jnp.concatenate([jnp.full((w,), s, jnp.float32) for w, s in
                                 zip(IN_SPLITS, (1.0, 1.0, beta, 1.0, 1.0, beta, 1.0, 1.0, 1.0))])
    x = nrm(ks[0], (BATCH, SEQ, D_MODEL), jnp.float32)
    w_in = nrm(ks[1], (DEPTH_2, D_MODEL, IN_WIDTH), jnp.float32) * D_MODEL ** -0.5 * col_scale
    hgrn_lb_logits = 1.0 + 0.1 * nrm(ks[2], (DEPTH_2 + 1, HGRN_WIDTH), jnp.float32)
    hgrn_norm_g = 1.0 + 0.05 * nrm(ks[3], (DEPTH_2, HGRN_WIDTH), jnp.float32)
    w_branch_sb = nrm(ks[4], (DEPTH_2, SB_WIDTH, D_MODEL), jnp.float32) * SB_WIDTH ** -0.5
    w_branch_hgrn = nrm(ks[5], (DEPTH_2, HGRN_WIDTH, D_MODEL), jnp.float32) * HGRN_WIDTH ** -0.5
    w_out = nrm(ks[6], (DEPTH_2, D_MODEL, D_MODEL), jnp.float32) * D_MODEL ** -0.5 * beta
    ln1_g = 1.0 + 0.05 * nrm(ks[7], (DEPTH_2, D_MODEL), jnp.float32)
    ln1_b = 0.02 * nrm(ks[8], (DEPTH_2, D_MODEL), jnp.float32)
    router_w = nrm(ks[9], (DEPTH_2, D_MODEL, N_EXPERTS), jnp.float32) * D_MODEL ** -0.5
    router_b = 0.01 * nrm(ks[10], (DEPTH_2, N_EXPERTS), jnp.float32)
    expert_w_up = nrm(ks[11], (DEPTH_2, N_EXPERTS, D_MODEL, 2 * D_FF_2), jnp.float32) * D_MODEL ** -0.5 * beta
    expert_b_up = 0.01 * nrm(ks[12], (DEPTH_2, N_EXPERTS, 2 * D_FF_2), jnp.float32)
    expert_w_down = nrm(ks[13], (DEPTH_2, N_EXPERTS, D_FF_2, D_MODEL), jnp.float32) * D_FF_2 ** -0.5 * beta
    expert_b_down = 0.01 * nrm(ks[14], (DEPTH_2, N_EXPERTS, D_MODEL), jnp.float32)
    ln2_g = 1.0 + 0.05 * nrm(ks[15], (DEPTH_2, D_MODEL), jnp.float32)
    ln2_b = 0.02 * nrm(ks[16], (DEPTH_2, D_MODEL), jnp.float32)
    return {'x': x, 'w_in': w_in, 'hgrn_lb_logits': hgrn_lb_logits, 'hgrn_norm_g': hgrn_norm_g,
            'w_branch_sb': w_branch_sb, 'w_branch_hgrn': w_branch_hgrn, 'w_out': w_out,
            'ln1_g': ln1_g, 'ln1_b': ln1_b, 'router_w': router_w, 'router_b': router_b,
            'expert_w_up': expert_w_up, 'expert_b_up': expert_b_up,
            'expert_w_down': expert_w_down, 'expert_b_down': expert_b_down,
            'ln2_g': ln2_g, 'ln2_b': ln2_b}

def second_block(x, w_in, hgrn_lb_logits, hgrn_norm_g, w_branch_sb, w_branch_hgrn, w_out,
              ln1_g, ln1_b, router_w, router_b, expert_w_up, expert_b_up,
              expert_w_down, expert_b_down, ln2_g, ln2_b):
    lower_bounds = jnp.cumsum(jax.nn.softmax(hgrn_lb_logits.astype(jnp.float32), axis=0), axis=0)
    h = x
    for l in range(DEPTH_2):
        mix = hybrid_mixer(h, w_in[l], lower_bounds[l], hgrn_norm_g[l],
                           w_branch_sb[l], w_branch_hgrn[l], w_out[l])
        h = layer_norm(DEEPNORM_ALPHA * h + mix, ln1_g[l], ln1_b[l])
        ffn = moe(h, router_w[l], router_b[l], expert_w_up[l], expert_b_up[l],
                  expert_w_down[l], expert_b_down[l])
        h = layer_norm(DEEPNORM_ALPHA * h + ffn, ln2_g[l], ln2_b[l])
    return h


def setup_inputs(seed=0):
    out = dict(first_inputs(seed))
    for name, value in second_inputs(seed + 1).items():
        if name != "x":
            out[name + "_2"] = value
    return out


def reference(
    x, mix_norm, mlp_norm, mlp_w1, mlp_w2, lru_w_in, lru_conv_w, lru_conv_b, lru_w_r, lru_b_r,
    lru_w_i, lru_b_i, lru_lambda, lru_w_out, fox_w_in, fox_b_f, fox_q_gain, fox_k_gain,
    fox_w_out, w_in_2, hgrn_lb_logits_2, hgrn_norm_g_2, w_branch_sb_2, w_branch_hgrn_2, w_out_2,
    ln1_g_2, ln1_b_2, router_w_2, router_b_2, expert_w_up_2, expert_b_up_2, expert_w_down_2,
    expert_b_down_2, ln2_g_2, ln2_b_2,
):
    x = first_block(
        x, mix_norm, mlp_norm, mlp_w1, mlp_w2, lru_w_in, lru_conv_w, lru_conv_b, lru_w_r,
        lru_b_r, lru_w_i, lru_b_i, lru_lambda, lru_w_out, fox_w_in, fox_b_f, fox_q_gain,
        fox_k_gain, fox_w_out,
    )
    return second_block(
        x, w_in_2, hgrn_lb_logits_2, hgrn_norm_g_2, w_branch_sb_2, w_branch_hgrn_2, w_out_2,
        ln1_g_2, ln1_b_2, router_w_2, router_b_2, expert_w_up_2, expert_b_up_2, expert_w_down_2,
        expert_b_down_2, ln2_g_2, ln2_b_2,
    )


_drawn_inputs = setup_inputs


def setup_inputs(seed=0):
    import zlib

    import numpy as np

    out = dict(_drawn_inputs(seed))
    spreads = {}
    factors = {'mix_norm': 3.349,
     'lru_b_r': 3.881,
     'lru_b_i': 2.952,
     'fox_q_gain': 8.0,
     'fox_k_gain': 7.45,
     'hgrn_lb_logits_2': 28.173,
     'hgrn_norm_g_2': 29.556,
     'router_b_2': 16.643,
     'expert_b_up_2': 26.175,
     'expert_b_down_2': 8.0,
     'ln2_b_2': 2.738}
    for name, (base, spread) in spreads.items():
        noise = np.random.default_rng([zlib.crc32(name.encode()), seed]).standard_normal(out[name].shape)
        drawn = base * np.exp(spread * noise) if base else spread * noise
        out[name] = __import__('jax').numpy.asarray(drawn.astype(out[name].dtype))
    for name, factor in factors.items():
        out[name] = (out[name] * factor).astype(out[name].dtype)
    return out
```

```python
from contextlib import ExitStack

import concourse.bass as bass
import concourse.mybir as mybir

F32 = mybir.dt.float32
I32 = mybir.dt.int32
U32 = mybir.dt.uint32
ALU = mybir.AluOpType
ACT = mybir.ActivationFunctionType
AX = mybir.AxisListType

P = 128
T = 256
TT = T // P
D = 1024
KD = D // P
DFF = 4 * D
NH, HD = 16, 64
SBH, SBW = 8, 512
HGH, HGD, HGW = 4, 128, 512
NE, TOPK = 32, 4
SLOTS = 128
NARROW = 64
RING = 4
XRING = 6
PANEL = 4096
EPS = 1e-6
LN_EPS = 1e-5
NEG = -1e30
ALPHA = 2.0 ** 0.25
SWIGLU_ALPHA, SWIGLU_LIMIT = 1.702, 7.0


class Count:

    def __init__(self, sem, step=1):
        self.sem, self.step, self.n, self.loop = sem, step, 0, None

    def add(self, instruction):
        instruction.then_inc(self.sem, self.step)
        self.n += 1
        return self.now()

    def now(self):
        return (self, self.n, self.loop)

    def before_iteration(self):
        return (self, self.loop[2], self.loop)


class Engine:

    def __init__(self, engine, sem):
        self.engine, self.done = engine, Count(sem) if sem is not None else None
        self.waited = {}

    def after(self, *marks):
        for mark in marks:
            if mark is None:
                continue
            count, n, loop = mark
            if n <= self.waited.get((count, loop), 0 if loop is None else -RING * 16):
                continue
            assert loop is None or loop is count.loop, "a mark of a loop is used outside of it"
            self.waited[count, loop] = n
            value = n * count.step
            if loop is not None:
                value = value + loop[0] * (loop[1] * count.step)
            self.engine.wait_ge(count.sem, value)
        return self

    def do(self, instruction):
        return self.done.add(instruction)

    def settle(self, sem):
        self.engine.sem_inc(sem, 1)


class Share(tuple):

    __hash__ = object.__hash__

    def __eq__(self, other):
        return self is other


class Loop:

    def __init__(self, nc, trips, shares):
        self.nc, self.trips, self.shares = nc, trips, shares

    def __enter__(self):
        self.fori = self.nc.Fori(0, self.trips)
        i = self.fori.__enter__()
        for count, share in self.shares.items():
            count.loop = Share((i, share, count.n))
        return i

    def __exit__(self, *exc):
        if exc[0] is None:
            for count, share in self.shares.items():
                grown = count.n - count.loop[2]
                assert grown == share, f"{count.sem}: {grown} in an iteration, {share} stated"
                count.n = count.loop[2] + self.trips * share
                count.loop = None
        return self.fori.__exit__(*exc)


class Kernel:
    def __init__(self, nc, ctx, a, out):
        self.nc, self.ctx, self.a, self.out = nc, ctx, a, out
        sem = lambda name: ctx.enter_context(nc.semaphore(name))
        self.sem, self.made = sem, 0
        self.pe = Engine(nc.tensor, sem("pe_done"))
        self.dve = Engine(nc.vector, sem("dve_done"))
        self.act = Engine(nc.scalar, sem("act_done"))
        self.pool = Engine(nc.gpsimd, sem("pool_done"))
        self.sp = Engine(nc.sync, None)
        self.compute = (self.pe, self.dve, self.act, self.pool)
        self.arrived = [Count(sem(f"panel_in_slot{s}"), 16) for s in range(XRING)]
        self.freed = Count(sem("panels_consumed"))
        self.small = Count(sem("small_loads"), 16)
        self.late = Count(sem("late_loads"), 16)
        self.stored = Count(sem("stored"), 16)
        self.settled = sem("waits_settled")
        self.panels = 0
        self.ring = self.sb("panel_ring", [P, XRING, PANEL])
        self.psA = self.ps("psA", [P, 4, 512])
        self.psB = [self.ps(f"psB{j}", [P, 2, 512]) for j in range(2)]
        self.x = self.sb("x", [P, TT, D])
        self.hT = self.sb("hT", [P, KD, T])

    def sb(self, name, shape, dt=F32, ctx=None):
        self.made = self.made + 1
        return (ctx or self.ctx).enter_context(self.nc.sbuf_tensor(f"{name}_{self.made}", shape, dt))

    def ps(self, name, shape, dt=F32):
        return self.ctx.enter_context(self.nc.psum_tensor(name, shape, dt))

    def join(self):
        for e in self.compute:
            for other in self.compute:
                e.after(other.done.now())
            e.after(self.freed.now())


    def load_panel(self, source, parts):
        slot = self.panels % RING
        self.panels += 1
        view = self.ring[:, slot, :].rearrange("p (k n) -> p k n", k=parts)
        count, n, loop = self.freed, self.panels - RING, self.freed.loop
        self.sp.after((count, n, loop))
        if loop is not None:
            self.sp.settle(self.settled)
        mark = self.arrived[slot].add(self.nc.sync.dma_start(view, source))
        return view, mark

    def columns(self, w, j):
        return self.load_panel(w[:, j * 512:(j + 1) * 512].rearrange("(k p) n -> p k n", p=P), KD)

    def rows(self, w, j):
        return self.load_panel(w[j * 512:(j + 1) * 512, :].rearrange("(k p) n -> p k n", p=P), 4)

    def project_T(self, panel, hT, ps, *ready):
        w, arrived = panel
        self.pe.after(arrived, *ready)
        out = ps[:].rearrange("p a b -> p (a b)").rearrange("p (m t) -> p m t", t=T)
        for m in range(4):
            for k in range(KD):
                last = self.nc.tensor.matmul(out[:, m, :], w[:, k, m * P:(m + 1) * P], hT[:, k, :],
                                             start=(k == 0), stop=(k == KD - 1))
        return out, self.freed.add(last)

    def project_nat(self, panel, hT, ps, *ready):
        w, arrived = panel
        self.pe.after(arrived, *ready)
        for tt in range(TT):
            for k in range(KD):
                last = self.nc.tensor.matmul(ps[:, tt, :], hT[:, k, tt * P:(tt + 1) * P], w[:, k, :],
                                             start=(k == 0), stop=(k == KD - 1))
        return self.freed.add(last)

    def accumulate_nat(self, panel, aT, first, last, ps, *ready):
        w, arrived = panel
        self.pe.after(arrived, *ready)
        for k in range(4):
            for tt in range(TT):
                for half in range(2):
                    mm = self.nc.tensor.matmul(ps[:, 2 * tt + half, :], aT[:, k, tt * P:(tt + 1) * P],
                                               w[:, k, half * 512:(half + 1) * 512],
                                               start=first and k == 0, stop=last and k == 3)
        return self.freed.add(mm)


    def transpose_to(self, src, j0, n, ps, *ready):
        self.pe.after(*ready)
        out = ps[:].rearrange("p a b -> p (a b)").rearrange("p (m t) -> p m t", t=T)
        for m in range(n):
            for tt in range(TT):
                last = self.nc.tensor.transpose(out[:, m, tt * P:(tt + 1) * P],
                                                src[:, tt, (j0 + m) * P:(j0 + m + 1) * P], self.ident[:])
        return out, self.pe.do(last)

    def to_T(self, src, dst, *ready, scale=None):
        n, V = src.shape[2] // P, self.nc.vector
        marks = [None, None]
        for g in range((n + 3) // 4):
            m = min(4, n - 4 * g)
            out, done = self.transpose_to(src, 4 * g, m, self.psB[g % 2], *ready, marks[g % 2])
            to = dst[:, 4 * g:4 * g + m, :]
            self.dve.after(done)
            if scale is None:
                marks[g % 2] = self.dve.do(V.tensor_copy(to, out[:, 0:m, :]))
            else:
                s = scale[:, 4 * g:4 * g + m].unsqueeze(2).to_broadcast([P, m, T])
                marks[g % 2] = self.dve.do(V.tensor_tensor(to, out[:, 0:m, :], s, ALU.mult))
        return self.dve.done.now()

    def rsqrt(self, ms, y, t, *ready):
        V, dve, act = self.nc.vector, self.dve, self.act
        a = act.after(*ready).do(self.nc.scalar.activation(y, ms, ACT.Ln))
        a = act.after(a).do(self.nc.scalar.activation(y, y, ACT.Exp, scale=-0.5))
        m = dve.after(a).do(V.tensor_tensor(t, y, y, ALU.mult))
        m = dve.after(m).do(V.tensor_tensor(t, t, ms, ALU.mult))
        m = dve.after(m).do(V.tensor_scalar(t, t, -0.5, 1.5, ALU.mult, ALU.add))
        return dve.after(m).do(V.tensor_tensor(y, y, t, ALU.mult))

    def rms_to_hT(self, gain):
        V, dve, act = self.nc.vector, self.dve, self.act
        self.join()
        with ExitStack() as c:
            xn = self.sb("x_normed", [P, TT, D], ctx=c)
            st = self.sb("rms_stats", [P, 4, TT], ctx=c)
            for tt in range(TT):
                act.do(self.nc.scalar.activation(xn[:, tt, :], self.x[:, tt, :], ACT.Square,
                                                 accum_out=st[:, 0, tt:tt + 1]))
            m = dve.after(act.done.now()).do(
                V.tensor_scalar(st[:, 1, :], st[:, 0, :], 1.0 / D, EPS, ALU.mult, ALU.add))
            r = self.rsqrt(st[:, 1, :], st[:, 2, :], st[:, 3, :], m)
            for tt in range(TT):
                m = dve.after(r).do(V.tensor_scalar(xn[:, tt, :], self.x[:, tt, :], st[:, 2, tt:tt + 1],
                                                    None, ALU.mult))
            self.to_T(xn, self.hT, m, scale=gain)
            self.join()


    def setup(self):
        nc, G, pool = self.nc, self.nc.gpsimd, self.pool
        a = self.a
        for tt in range(TT):
            self.small.add(nc.scalar.dma_start(self.x[:, tt, :], a["x"][0, tt * P:(tt + 1) * P, :]))
        rows = self.sb("param_rows", [P, P])
        z = pool.do(G.memset(rows[:], 0.0))
        at, self.col_of = 0, {}
        nc.scalar.wait_ge(self.pool.done.sem, 1)

        def put(name, src, n):
            nonlocal at
            self.small.add(nc.scalar.dma_start(rows[at:at + n, :], src))
            self.col_of[name] = at
            at += n

        put("mix", a["mix_norm"].rearrange("l (c p) -> (l c) p", p=P), 16)
        put("mlp", a["mlp_norm"].rearrange("l (c p) -> (l c) p", p=P), 16)
        put("conv_w", a["lru_conv_w"][0].rearrange("l (c p) -> (l c) p", p=P), 32)
        put("conv_b", a["lru_conv_b"][0].rearrange("(c p) -> c p", p=P), 8)
        put("b_r", a["lru_b_r"][0].rearrange("(c n) p -> c (n p)", n=2), 8)
        put("b_i", a["lru_b_i"][0].rearrange("(c n) p -> c (n p)", n=2), 8)
        put("lam", a["lru_lambda"][0].rearrange("(c p) -> c p", p=P), 8)
        put("lb", a["hgrn_lb_logits_2"].rearrange("l (c p) -> (l c) p", p=P), 8)
        for name in ("q_gain", "k_gain"):
            for half in range(2):
                self.small.add(nc.scalar.dma_start(rows[at:at + 1, half * HD:(half + 1) * HD],
                                                   a["fox_" + name]))
            self.col_of[name] = at
            at += 1
        self.ident = self.sb("ident", [P, P])
        self.ones = self.sb("ones", [P, P])
        self.before = self.sb("before", [P, P])
        self.after_ = self.sb("after_", [P, P])
        m0 = pool.do(G.memset(self.ident[:], 0.0))
        m1 = pool.do(G.memset(self.ones[:], 1.0))
        pool.after(m0).do(G.affine_select(out=self.ident[:], in_=self.ident[:], compare_op=ALU.not_equal,
                                          fill=1.0, base=0, pattern=[[-1, P]], channel_multiplier=1))
        pool.after(m1).do(G.affine_select(out=self.before[:], in_=self.ones[:], compare_op=ALU.is_gt,
                                          fill=0.0, base=0, pattern=[[1, P]], channel_multiplier=-1))
        pool.do(G.affine_select(out=self.after_[:], in_=self.ones[:], compare_op=ALU.is_gt,
                                fill=0.0, base=0, pattern=[[-1, P]], channel_multiplier=1))
        self.cols = self.sb("param_cols", [P, P])
        self.pe.after(pool.done.now(), self.small.now())
        t = self.pe.do(nc.tensor.transpose(self.psB[0][:, 0, 0:P], rows[:], self.ident[:]))
        self.dve.after(t).do(nc.vector.tensor_copy(self.cols[:], self.psB[0][:, 0, 0:P]))
        for e in self.compute:
            e.after(self.small.now())
        self.join()

    def col(self, name, n, skip=0):
        at = self.col_of[name] + skip
        return self.cols[:, at:at + n]


    def griffin(self):
        nc, V, A, G = self.nc, self.nc.vector, self.nc.scalar, self.nc.gpsimd
        pe, dve, act, pool = self.compute
        a = self.a
        self.rms_to_hT(self.col("mix", KD))
        with ExitStack() as c:
            sb = lambda n, s: self.sb(n, s, ctx=c)
            gate = sb("gate", [P, KD, T])
            xpad = sb("x_branch", [P, KD, T + 3])
            xc = sb("x_conv", [P, KD, T])
            wri = sb("w_ri", [P, 2, KD, P])
            ra = sb("r_then_a", [P, KD, T])
            ib = sb("i_then_b", [P, KD, T])
            th = sb("tanh_then_h", [P, KD, T])
            lam = sb("lam_work", [P, 5, KD])
            z0 = pool.do(G.memset(wri[:], 0.0))
            z1 = pool.do(G.memset(xpad[:, :, 0:3], 0.0))
            act.after(z0)
            for n, name in enumerate(("lru_w_r", "lru_w_i")):
                w = a[name][0].rearrange("(c n) d e -> d n c e", n=2)
                for half in range(2):
                    self.late.add(A.dma_start(wri[half * 64:half * 64 + 64, n, :, half * 64:half * 64 + 64],
                                              w[:, half, :, :]))
            u, s, s2, acc, ls = (lam[:, i, :] for i in range(5))
            L = self.col("lam", KD)
            k = act.do(A.activation(u, L, ACT.Abs))
            k = act.after(k).do(A.activation(u, u, ACT.Exp, scale=-1.0))
            m = dve.after(k).do(V.tensor_scalar(s2, u, 2.0, None, ALU.add))
            m = dve.after(m).do(V.reciprocal(s, s2))
            m = dve.after(m).do(V.tensor_tensor(s, s, u, ALU.mult))
            m = dve.after(m).do(V.tensor_tensor(s2, s, s, ALU.mult))
            m = dve.after(m).do(V.tensor_scalar(acc, s2, 2.0 / 17, 2.0 / 15, ALU.mult, ALU.add))
            for odd in (13, 11, 9, 7, 5, 3, 1):
                m = dve.after(m).do(V.tensor_tensor(acc, acc, s2, ALU.mult))
                m = dve.after(m).do(V.tensor_scalar(acc, acc, 2.0 / odd, None, ALU.add))
            m = dve.after(m).do(V.tensor_tensor(acc, acc, s, ALU.mult))
            m = dve.after(m).do(V.tensor_scalar(ls, L, 0.0, None, ALU.min))
            m = dve.after(m).do(V.tensor_tensor(ls, ls, acc, ALU.subtract))
            c8 = dve.after(m).do(V.tensor_scalar(ls, ls, 8.0, None, ALU.mult))

            w_in = a["lru_w_in"][0]
            free = [None, None]
            for j in range(4):
                out, done = self.project_T(self.columns(w_in, j), self.hT, self.psB[j % 2], free[j % 2])
                if j < 2:
                    free[j % 2] = act.after(done).do(
                        A.activation(gate[:, 4 * j:4 * j + 4, :], out, ACT.Gelu_apprx_tanh))
                    continue
                t0 = 4 * (j - 2)
                copied = dve.after(done, z1).do(V.tensor_copy(xpad[:, t0:t0 + 4, 3:3 + T], out))
                free[j % 2] = copied
                w = lambda k, t: self.col("conv_w", 1, 8 * k + t)
                tiles = range(t0, t0 + 4)
                m = {}
                for t in tiles:
                    m[t] = dve.after(copied).do(V.tensor_scalar(
                        xc[:, t, :], xpad[:, t, 0:T], w(0, t), self.col("conv_b", 1, t), ALU.mult, ALU.add))
                for k in range(1, 4):
                    for t in tiles:
                        m[t] = dve.after(m[t]).do(V.scalar_tensor_tensor(
                            xc[:, t, :], xpad[:, t, k:k + T], w(k, t), xc[:, t, :], ALU.mult, ALU.add))
            conv = dve.done.now()
            pe.after(conv, self.late.now(), *free)
            rps = self.psA[:].rearrange("p a (b t) -> p (a b) t", t=T)
            for t in range(KD):
                r_done = nc.tensor.matmul(rps[:, t, :], wri[:, 0, t, :], xc[:, t, :], start=True, stop=True)
            r_done = pe.do(r_done)
            ips = [self.psB[j][:].rearrange("p a (b t) -> p (a b) t", t=T) for j in range(2)]
            for t in range(KD):
                i_done = nc.tensor.matmul(ips[t // 4][:, t % 4, :], wri[:, 1, t, :], xc[:, t, :],
                                          start=True, stop=True)
            i_done = pe.do(i_done)
            act.after(r_done)
            for t in range(KD):
                act.do(A.activation(ra[:, t, :], rps[:, t, :], ACT.Sigmoid, bias=self.col("b_r", 1, t)))
            r_ready = act.done.now()
            act.after(i_done)
            for t in range(KD):
                act.do(A.activation(ib[:, t, :], ips[t // 4][:, t % 4, :], ACT.Sigmoid,
                                    bias=self.col("b_i", 1, t)))
            i_ready = act.done.now()
            c8b = ls.unsqueeze(2).to_broadcast([P, KD, T])
            m = dve.after(r_ready, c8).do(V.tensor_tensor(ra[:], ra[:], c8b, ALU.mult))
            k1 = act.after(m).do(A.activation(th[:], ra[:], ACT.Tanh))
            k2 = act.after(k1).do(A.activation(ra[:], ra[:], ACT.Exp))
            b = dve.after(i_ready).do(V.tensor_tensor(ib[:], ib[:], xc[:], ALU.mult))
            m = dve.after(k2, conv, b).do(V.tensor_tensor(xc[:], ra[:], ra[:], ALU.mult))
            m = dve.after(m, k1).do(V.scalar_tensor_tensor(th[:], xc[:], 1.0, th[:], ALU.add, ALU.mult))
            k = act.after(m).do(A.activation(th[:], th[:], ACT.Sqrt, scale=-1.0))
            b = dve.after(k, b).do(V.tensor_tensor(ib[:], ib[:], th[:], ALU.mult))
            dve.after(b)
            for t in range(KD):
                h = dve.do(V.tensor_tensor_scan(th[:, t, :], ra[:, t, :], ib[:, t, :], 0.0,
                                                ALU.mult, ALU.add))
            y = dve.after(h, act.done.now()).do(V.tensor_tensor(gate[:], gate[:], th[:], ALU.mult))
            w_out = a["lru_w_out"][0]
            for j in range(2):
                done = self.accumulate_nat(self.rows(w_out, j), gate[:, 4 * j:4 * j + 4, :], j == 0, j == 1,
                                           self.psA, y, r_ready)
            self.add_to_x(done)
            self.join()

    def add_to_x(self, done, ps=None):
        flat = self.x[:].rearrange("p t n -> p (t n)")
        src = (ps or self.psA)[:].rearrange("p a b -> p (a b)")
        return self.dve.after(done).do(self.nc.vector.tensor_tensor(flat, flat, src, ALU.add))


    def mlp(self, layer):
        nc, V, A = self.nc, self.nc.vector, self.nc.scalar
        pe, dve, act, pool = self.compute
        self.rms_to_hT(self.col("mlp", KD, KD * layer))
        w1, w2 = self.a["mlp_w1"][layer], self.a["mlp_w2"][layer]
        with ExitStack() as c:
            relu = self.sb("relu", [P, 2, 4, T], ctx=c)
            aT = self.sb("aT", [P, 8, T], ctx=c)
            shares = {self.freed: 4, act.done: 2, dve.done: 3, **{s: 1 for s in self.arrived[:RING]}}
            with Loop(nc, 4, shares) as i:
                for j in range(2):
                    cols = w1[:, bass.ds(i * 1024 + j * 512, 512)]
                    panel = self.load_panel(cols.rearrange("(k p) n -> p k n", p=P), KD)
                    out, done = self.project_T(panel, self.hT, self.psB[j],
                                               act.done.before_iteration(), dve.done.before_iteration())
                    r = act.after(done, dve.done.before_iteration()).do(
                        A.activation(relu[:, j], out, ACT.Relu))
                    sq = dve.after(r, self.freed.before_iteration()).do(
                        V.tensor_tensor(aT[:, 4 * j:4 * j + 4, :], relu[:, j], relu[:, j], ALU.mult))
                for j in range(2):
                    rows = w2[bass.ds(i * 1024 + j * 512, 512), :]
                    panel = self.load_panel(rows.rearrange("(k p) n -> p k n", p=P), 4)
                    done = self.accumulate_nat(panel, aT[:, 4 * j:4 * j + 4, :], j == 0, j == 1, self.psA,
                                               sq, dve.done.before_iteration())
                self.add_to_x(done)
            self.panels += 3 * 4
            self.join()


    def weighted_values(self, pT, v, heads, ps, *ready):
        M = self.nc.tensor
        self.pe.after(*ready)
        out = ps[:, 0, :].rearrange("p (h t d) -> p h t d", t=TT, d=HD)
        for g, h in enumerate(heads):
            vh = v[:, :, h * HD:(h + 1) * HD]
            M.matmul(out[:, g, 0, :], pT[:, g, 0:P], vh[:, 0, :], start=True, stop=True)
            M.matmul(out[:, g, 1, :], pT[:, g, P:2 * P], vh[:, 0, :], start=True, stop=False)
            last = M.matmul(out[:, g, 1, :], pT[:, g, 2 * P:3 * P], vh[:, 1, :], start=False, stop=True)
        return out, self.pe.do(last)


    def fox(self):
        nc, V, A, G, M = self.nc, self.nc.vector, self.nc.scalar, self.nc.gpsimd, self.nc.tensor
        pe, dve, act, pool = self.compute
        a = self.a
        w_in = a["fox_w_in"][0]
        self.rms_to_hT(self.col("mix", KD, KD))
        with ExitStack() as c:
            sb = lambda n, s: self.sb(n, s, ctx=c)
            nat = [sb(n, [P, TT, D]) for n in ("q_nat", "k_nat", "v_nat")]
            v_nat = nat[2]
            qT = sb("qT", [P, KD, T])
            kTz = sb("kT_padded", [P, NH, T])
            c_sel = sb("minus_head_row", [P, NH, P])
            cT = sb("cum_log_f", [P, T])
            mask = sb("causal", [P, 3 * P])
            score = [sb(f"scores{i}", [P, 4, 3 * P]) for i in range(2)]
            pT = sb("pT", [P, 4, 3 * P])
            wf = sb("w_f", [P, KD, NH])
            bf = sb("b_f", [NH, 1])
            ss = sb("qk_stats", [P, 3, 2, TT * NH])
            nm = sb("minus_max", [P, NH, 3])
            den = sb("softmax_sums", [P, NH, 2])
            sq = sb("squares", [P, TT, 512])
            lf = sb("log_f_work", [NH, 2, T])
            z = pool.do(G.memset(kTz[:], 0.0))
            pool.do(G.memset(c_sel[:], 0.0))
            pool.do(G.memset(mask[:], 0.0))
            pool.do(G.memset(cT[:], 0.0))
            pool.after(pool.done.now())
            pool.do(G.affine_select(out=c_sel[:], in_=c_sel[:], compare_op=ALU.not_equal, fill=-1.0,
                                    base=0, pattern=[[-1, NH], [0, P]], channel_multiplier=1))
            for at in (0, 2 * P):
                pool.do(G.affine_select(out=mask[:, at:at + P], in_=mask[:, at:at + P],
                                        compare_op=ALU.is_ge, fill=NEG, base=0, pattern=[[-1, P]],
                                        channel_multiplier=1))
            act.after(pool.done.now())
            with nc.allow_non_contiguous_dma(reason="one value per partition"):
                self.late.add(A.dma_start(bf[:], a["fox_b_f"][0].rearrange("(n o) -> n o", o=1)))
            self.late.add(A.dma_start(wf[:], w_in[:, 3 * D:].rearrange("(k p) n -> p k n", p=P)))
            qg = self.col("q_gain", 1)
            gain8 = sb("q_gain_eighth", [P, 1])
            g8 = dve.do(V.tensor_scalar(gain8[:], qg, HD ** -0.5, None, ALU.mult))

            free = [None, None]
            for j in range(6):
                ps, n = self.psB[j % 2], nat[j // 2]
                done = self.project_nat(self.columns(w_in, j), self.hT, ps, free[j % 2])
                part = n[:, :, (j % 2) * 512:(j % 2) * 512 + 512]
                copied = act.after(done).do(A.activation(part, ps[:], ACT.Copy))
                free[j % 2] = copied
                if j < 4:
                    m = dve.after(copied, dve.done.now()).do(V.tensor_tensor(sq[:], part, part, ALU.mult))
                    dst = ss[:, 0, j // 2, :].rearrange("p (t h) -> p t h", t=TT)[:, :, 8 * (j % 2):8 * (j % 2) + 8]
                    m = dve.after(m).do(V.tensor_reduce(
                        dst, sq[:].rearrange("p t (h d) -> p t h d", d=HD), axis=AX.X, op=ALU.add))
            pe.after(self.late.now(), free[0])
            for k in range(KD):
                last = M.matmul(self.psB[0][0:NH, 0, 0:T], wf[:, k, :], self.hT[:, k, :],
                                start=(k == 0), stop=(k == KD - 1))
            fdone = pe.do(last)
            fps = self.psB[0][0:NH, 0, 0:T]
            k = act.after(fdone, self.late.now()).do(A.activation(lf[:, 0, :], fps, ACT.Abs, bias=bf[:]))
            bank_free = k
            k = act.after(k).do(A.activation(lf[:, 0, :], lf[:, 0, :], ACT.Exp, scale=-1.0))
            k = act.after(k).do(A.activation(lf[:, 0, :], lf[:, 0, :], ACT.Ln, bias=1.0))
            m = dve.after(bank_free, self.late.now()).do(V.tensor_scalar(lf[:, 1, :], fps, bf[:], 0.0, ALU.add, ALU.min))
            m = dve.after(m, k).do(V.tensor_tensor(lf[:, 1, :], lf[:, 1, :], lf[:, 0, :], ALU.subtract))
            one = self.ones[0:NH, 0:1].to_broadcast([NH, T])
            cdone = dve.after(m).do(V.tensor_tensor_scan(cT[0:NH, :], one, lf[:, 1, :], 0.0, ALU.mult, ALU.add))

            ms, y, t = (ss[:, i].rearrange("p a b -> p (a b)") for i in range(3))
            m = dve.do(V.tensor_scalar(ms, ms, 1.0 / HD, EPS, ALU.mult, ALU.add))
            r = self.rsqrt(ms, y, t, m)
            for i in range(2):
                v3 = nat[i][:].rearrange("p t (h d) -> p (t h) d", d=HD)
                m = dve.after(r).do(V.tensor_tensor(
                    v3, v3, ss[:, 1, i, :].unsqueeze(2).to_broadcast([P, TT * NH, HD]), ALU.mult))
            free = [cdone, None]
            for g in range(4):
                i = g // 2
                out, done = self.transpose_to(nat[i], 4 * (g % 2), 4, self.psB[g % 2], m, free[g % 2])
                c0 = 4 * (g % 2)
                if i == 0:
                    free[g % 2] = dve.after(done, g8).do(V.tensor_scalar(
                        qT[:, c0:c0 + 4, :], out[:], gain8[:], None, ALU.mult))
                else:
                    for half in range(2):
                        rows = slice(64 * half, 64 * half + 64)
                        to = kTz[rows, 2 * c0 + half:2 * c0 + 8:2, :]
                        free[g % 2] = dve.after(done, z).do(V.tensor_scalar(
                            to, out[rows], self.col("k_gain", 1)[rows], None, ALU.mult))
            qk = dve.done.now()

            o_nat = nat[0]
            s_free, o_read, p_free = None, None, None
            for g in range(4):
                heads = range(4 * g, 4 * g + 4)
                S, sc = self.psA, score[g % 2]
                pe.after(qk, cdone, pool.done.now(), s_free)
                for i, h in enumerate(heads):
                    for t0, s1, at in ((0, P, 0), (P, T, P)):
                        out = S[:, i, at:at + s1]
                        M.matmul(out, qT[:, h // 2, t0:t0 + P], kTz[:, h, 0:s1], start=True, stop=False)
                        last = M.matmul(out, c_sel[:, h, :], cT[:, 0:s1], start=False, stop=True)
                s_done = pe.do(last)
                mb = mask[:].unsqueeze(1).to_broadcast([P, 4, 3 * P])
                m = dve.after(s_done, pool.done.now(), o_read).do(V.tensor_tensor(sc[:], S[:, :, 0:3 * P], mb, ALU.add))
                s_free = m
                hs = slice(4 * g, 4 * g + 4)
                dve.after(m).do(V.tensor_reduce(nm[:, hs, 0], sc[:, :, 0:P], axis=AX.X, op=ALU.max, negate=True))
                m = dve.do(V.tensor_reduce(nm[:, hs, 1], sc[:, :, P:], axis=AX.X, op=ALU.max, negate=True))
                act.after(m)
                for i, h in enumerate(heads):
                    for j, cols in enumerate((slice(0, P), slice(P, 3 * P))):
                        k = act.do(A.activation(sc[:, i, cols], sc[:, i, cols], ACT.Exp,
                                                bias=nm[:, h, j:j + 1], accum_out=den[:, h, j:j + 1]))
                pe.after(k, o_read, p_free)
                for i in range(4):
                    bank = self.psB[i // 2][:, i % 2, :]
                    for b in range(3):
                        last = M.transpose(bank[:, b * P:(b + 1) * P], sc[:, i, b * P:(b + 1) * P], self.ident[:])
                t_done = pe.do(last)
                r = dve.after(k).do(V.reciprocal(den[:, hs, :], den[:, hs, :]))
                act.after(t_done, pe.done.now()).do(A.activation(pT[:, 0:2, :], self.psB[0][:, :, 0:3 * P], ACT.Copy))
                p_free = dve.after(t_done).do(V.tensor_copy(pT[:, 2:4, :], self.psB[1][:, :, 0:3 * P]))
                out, done = self.weighted_values(pT, v_nat, heads, self.psB[0], act.done.now(), p_free)
                to = o_nat[:, :, 4 * g * HD:(4 * g + 4) * HD].rearrange("p t (h d) -> p h t d", d=HD)
                o_read = dve.after(done, r).do(V.tensor_tensor(
                    to, out, den[:, hs, :].unsqueeze(3).to_broadcast([P, 4, 2, HD]), ALU.mult))
            o = self.to_T(o_nat, self.hT, o_read)
            w_out = a["fox_w_out"][0]
            for j in range(2):
                done = self.accumulate_nat(self.rows(w_out, j), self.hT[:, 4 * j:4 * j + 4, :], j == 0, j == 1,
                                           self.psA, o, s_free)
            self.add_to_x(done)
            self.join()


    def hybrid(self):
        nc, V, A, G, M = self.nc, self.nc.vector, self.nc.scalar, self.nc.gpsimd, self.nc.tensor
        pe, dve, act, pool = self.compute
        a = self.a
        w_in = a["w_in_2"][0]
        self.join()
        flat = lambda t: t.rearrange("p a b -> p (a b)")
        with ExitStack() as c:
            sb = lambda n, s, dt=F32: self.sb(n, s, dt, ctx=c)
            o_sb = sb("o_sb", [P, TT, SBW])
            o_hg = sb("o_hg", [P, TT, HGW])
            gates = sb("gates", [P, 2, TT, D])
            sig_g = sb("sigmoid_hg", [P, TT, HGW])
            with ExitStack() as c2:
                sb2 = lambda n, s, dt=F32: self.sb(n, s, dt, ctx=c2)
                qT = sb2("sb_qT", [P, 4, T])
                kTz = sb2("sb_kT_padded", [P, SBH, T])
                v_sb = sb2("sb_v", [P, TT, SBW])
                hq = sb2("hg_q", [P, HGH, T])
                hk = sb2("hg_k", [P, HGH, T])
                hb = sb2("hg_cum_log_f", [P, HGH, T])
                hv = sb2("hg_v", [P, TT, HGW])
                mask = sb2("sb_mask", [P, 3 * P])
                lvl = sb2("level_masks", [P, 7, P])
                keep = sb2("scan_keep", [P, HGH * T])
                lb = sb2("lb_work", [P, 4, 4])
                z = pool.do(G.memset(kTz[:], 0.0))
                pool.do(G.memset(mask[:], 1.0))
                pool.do(G.memset(lvl[:], 1.0))
                k0 = pool.do(G.memset(keep[:], 1.0))
                pool.after(k0)
                pool.do(G.memset(keep[:].rearrange("p (n t) -> p n t", t=P)[:, :, 0:1], 0.0))
                pool.do(G.affine_select(out=mask[:, 0:T], in_=mask[:, 0:T], compare_op=ALU.is_gt, fill=0.0,
                                        base=0, pattern=[[1, T]], channel_multiplier=-1))
                pool.do(G.affine_select(out=mask[:, T:], in_=mask[:, T:], compare_op=ALU.is_gt, fill=0.0,
                                        base=0, pattern=[[1, P]], channel_multiplier=-1))
                for l in range(7):
                    h = 2 ** l
                    n = P // (2 * h)
                    for base, pattern, cm in ((0, [[-2 * h, n], [0, 2 * h]], 1),
                                              (h - 1, [[2 * h, n], [0, 2 * h]], -1),
                                              (-h, [[0, n], [1, 2 * h]], 0)):
                        pool.after(pool.done.now())
                        pool.do(G.affine_select(out=lvl[:, l, :], in_=lvl[:, l, :], compare_op=ALU.is_ge,
                                                fill=0.0, base=base, pattern=pattern, channel_multiplier=cm))

                l0, l1 = self.col("lb", 4), self.col("lb", 4, 4)
                m = dve.do(V.tensor_tensor(lb[:, 0], l0, l1, ALU.max))
                m0 = dve.after(m).do(V.tensor_tensor(lb[:, 1], l0, lb[:, 0], ALU.subtract))
                m1 = dve.after(m).do(V.tensor_tensor(lb[:, 2], l1, lb[:, 0], ALU.subtract))
                k = act.after(m1, m0).do(A.activation(lb[:, 1:3], lb[:, 1:3], ACT.Exp))
                m = dve.after(k).do(V.tensor_tensor(lb[:, 2], lb[:, 1], lb[:, 2], ALU.add))
                m = dve.after(m).do(V.reciprocal(lb[:, 2], lb[:, 2]))
                m = dve.after(m).do(V.tensor_tensor(lb[:, 0], lb[:, 1], lb[:, 2], ALU.mult))
                lb_done = dve.after(m).do(V.tensor_scalar(lb[:, 3], lb[:, 0], -1.0, 1.0, ALU.mult, ALU.add))

                x_T = self.to_T(self.x, self.hT)
                free = [x_T, x_T]
                proj = lambda j, ready: (self.project_T if j in (0, 1, 3, 4) else self.project_nat)(
                    self.columns(w_in, j), self.hT, self.psB[j % 2], *ready)
                out, done = proj(0, free)
                free[0] = act.after(done).do(A.activation(qT[:], out, ACT.Copy, scale=HD ** -0.5))
                out, done = proj(1, [free[1]])
                for half in range(2):
                    rows = slice(64 * half, 64 * half + 64)
                    free[1] = dve.after(done, z).do(V.tensor_copy(kTz[rows, half::2, :], out[rows]))
                done = proj(2, [free[0]])
                free[0] = act.after(done).do(A.activation(v_sb[:], self.psB[0][:], ACT.Copy))
                out, done = proj(3, [free[1]])
                k = act.after(done).do(A.activation(hq[:], out, ACT.Sigmoid))
                free[1] = dve.after(k).do(V.tensor_tensor(hq[:], hq[:], out, ALU.mult))
                out, done = proj(4, [free[0]])
                free[0] = k = act.after(done).do(A.activation(hk[:], out, ACT.Sigmoid))
                bc = lambda i: lb[:, i, :].unsqueeze(2).to_broadcast([P, 4, T])
                m = dve.after(k, lb_done).do(V.tensor_tensor(hk[:], hk[:], bc(3), ALU.mult))
                f_done = dve.after(m).do(V.tensor_tensor(hb[:], hk[:], bc(0), ALU.add))
                m = dve.after(f_done).do(V.tensor_scalar(hk[:], hb[:], -1.0, 1.0, ALU.mult, ALU.add))
                done = proj(5, [free[1]])
                free[1] = act.after(done).do(A.activation(hv[:], self.psB[1][:], ACT.Copy))
                done = proj(6, [free[0]])
                free[0] = act.after(done).do(A.activation(sig_g[:], self.psB[0][:], ACT.Sigmoid))
                for j in range(7, 11):
                    done = proj(j, [free[j % 2]])
                    to = gates[:, (j - 7) // 2, :, ((j - 7) % 2) * 512:((j - 7) % 2) * 512 + 512]
                    free[j % 2] = act.after(done).do(A.activation(to, self.psB[j % 2][:], ACT.Sigmoid))

                with ExitStack() as c3:
                    sp, lw, w = (self.sb(n, [P, 4, 3 * P], ctx=c3) for n in ("softplus", "log_w", "sb_w"))
                    zs, o_mark, r_mark = None, None, None
                    for g in range(2):
                        Z = self.psA
                        pe.after(dve.done.now(), act.done.now())
                        for i in range(4):
                            h = 4 * g + i
                            M.matmul(Z[:, i, 0:T], kTz[:, h, 0:P], qT[:, h // 2, :], start=True, stop=True)
                            last = M.matmul(Z[:, i, T:3 * P], kTz[:, h, P:T], qT[:, h // 2, P:T],
                                            start=True, stop=True)
                        z_done = pe.do(last)
                        Zc = Z[:, :, 0:3 * P]
                        k = act.after(z_done, dve.done.now()).do(A.activation(sp[:], Zc, ACT.Abs))
                        z_read = k
                        k = act.after(k).do(A.activation(sp[:], sp[:], ACT.Exp, scale=-1.0))
                        k = act.after(k).do(A.activation(sp[:], sp[:], ACT.Ln, bias=1.0))
                        m = dve.after(k, z_read).do(V.scalar_tensor_tensor(sp[:], Zc, 0.0, sp[:], ALU.max, ALU.add))
                        m = dve.after(m, act.done.now(), pe.done.now()).do(V.tensor_tensor(lw[:], Zc, sp[:], ALU.subtract))
                        mb = mask[:].unsqueeze(1).to_broadcast([P, 4, 3 * P])
                        m = dve.after(m, pool.done.now()).do(V.tensor_tensor(sp[:], sp[:], mb, ALU.mult))
                        pe.after(m, *free)
                        for i in range(4):
                            bank = self.psB[i // 2][:, i % 2, :]
                            M.matmul(bank[:, 0:T], self.after_[:], sp[:, i, 0:T], start=True, stop=False)
                            M.matmul(bank[:, P:T], self.ones[:], sp[:, i, T:], start=False, stop=True)
                            last = M.matmul(bank[:, T:3 * P], self.after_[:], sp[:, i, T:], start=True, stop=True)
                        a_done = pe.do(last)
                        for j in range(2):
                            m = dve.after(a_done).do(V.tensor_tensor(
                                lw[:, 2 * j:2 * j + 2], lw[:, 2 * j:2 * j + 2], self.psB[j][:, :, 0:3 * P], ALU.subtract))
                        k = act.after(m).do(A.activation(w[:], lw[:], ACT.Exp))
                        m = dve.after(k).do(V.tensor_tensor(w[:], w[:], mb, ALU.mult))
                        out, done = self.weighted_values(w, v_sb, range(4 * g, 4 * g + 4), self.psB[0], m)
                        to = o_sb[:, :, 256 * g:256 * g + 256].rearrange("p t (h d) -> p h t d", d=HD)
                        dve.after(done).do(V.tensor_copy(to, out))
                    self.join()

                with ExitStack() as c3:
                    e = self.sb("decay", [P, HGH, T], ctx=c3)
                    qs = self.sb("q_decayed", [P, HGH, T], ctx=c3)
                    ks = self.sb("k_decayed", [P, HGH, T], ctx=c3)
                    S = self.sb("hg_scores", [P, HGH * TT, P], ctx=c3)
                    X = self.sb("hg_cross", [P, HGH, P], ctx=c3)
                    st = self.sb("hg_stats", [P, 3, TT * HGH], ctx=c3)
                    gn = self.sb("hgrn_gain", [P, HGW], ctx=c3)
                    self.late.add(nc.scalar.dma_start(gn[:], a["hgrn_norm_g_2"][0].partition_broadcast(P)))
                    k = act.do(A.activation(hb[:], hb[:], ACT.Ln))
                    b_done = dve.after(k).do(V.tensor_tensor_scan(flat(hb[:]), keep[:], flat(hb[:]), 0.0,
                                                                  ALU.mult, ALU.add))
                    blocks = lambda t, n: flat(t[:]).rearrange("p (n s) -> p n s", s=n)

                    def scores(ps, q, k_):
                        out = ps[:].rearrange("p a b -> p (a b)").rearrange("p (n t) -> p n t", t=P)
                        qv, kv = blocks(q, P), blocks(k_, P)
                        for n in range(HGH * TT):
                            last = M.matmul(out[:, n, :], kv[:, n, :], qv[:, n, :], start=True, stop=True)
                        return out, pe.do(last)

                    out, done = scores(self.psB[0], hq, hk)
                    s_done = dve.after(done).do(V.tensor_tensor(
                        S[:], out, self.ident[:].unsqueeze(1).to_broadcast([P, HGH * TT, P]), ALU.mult))
                    read = [s_done, None]
                    for l in range(7):
                        h = 2 ** l
                        b2, e2 = blocks(hb, 2 * h), blocks(e, 2 * h)
                        mid = b2[:, :, h - 1:h].to_broadcast([P, HGH * T // (2 * h), 2 * h])
                        m = dve.after(b_done, pe.done.now(), pool.done.now()).do(V.tensor_tensor(e2, b2, mid, ALU.subtract))
                        k = act.after(m).do(A.activation(e[:], e[:], ACT.Abs))
                        k = act.after(k).do(A.activation(e[:], e[:], ACT.Exp, scale=-1.0))
                        p = pool.after(k, pe.done.now()).do(G.tensor_tensor(qs[:], hq[:], e[:], ALU.mult))
                        m = dve.after(k).do(V.tensor_tensor(ks[:], hk[:], e[:], ALU.mult))
                        pe.after(m, p, read[(l + 1) % 2])
                        out, done = scores(self.psB[(l + 1) % 2], qs, ks)
                        mk = lvl[:, l, :].bitcast(U32).unsqueeze(1).to_broadcast([P, HGH * TT, P])
                        read[(l + 1) % 2] = s_done = dve.after(done, s_done).do(V.copy_predicated(S[:], mk, out))
                    end = hb[:, :, P - 1:P].to_broadcast([P, HGH, P])
                    m = dve.after(pe.done.now(), pool.done.now()).do(V.tensor_tensor(e[:, :, 0:P], end, hb[:, :, 0:P], ALU.subtract))
                    m = dve.do(V.tensor_copy(e[:, :, P:], hb[:, :, P:]))
                    k = act.after(m).do(A.activation(e[:], e[:], ACT.Exp))
                    m = dve.after(k).do(V.tensor_tensor(qs[:, :, P:], hq[:, :, P:], e[:, :, P:], ALU.mult))
                    m = dve.do(V.tensor_tensor(ks[:, :, 0:P], hk[:, :, 0:P], e[:, :, 0:P], ALU.mult))
                    pe.after(m, *read)
                    for h in range(HGH):
                        last = M.matmul(self.psB[0][:, 0, h * P:(h + 1) * P], ks[:, h, 0:P], qs[:, h, P:],
                                        start=True, stop=True)
                    done = pe.do(last)
                    x_done = dve.after(done).do(V.tensor_copy(
                        X[:], self.psB[0][:, 0, :].rearrange("p (h t) -> p h t", t=P)))
                    pe.after(x_done, s_done)
                    for h in range(HGH):
                        cols = slice(h * P, (h + 1) * P)
                        M.matmul(self.psB[1][:, 0, cols], S[:, 2 * h, :], hv[:, 0, cols], start=True, stop=True)
                        M.matmul(self.psB[1][:, 1, cols], X[:, h, :], hv[:, 0, cols], start=True, stop=False)
                        last = M.matmul(self.psB[1][:, 1, cols], S[:, 2 * h + 1, :], hv[:, 1, cols],
                                        start=False, stop=True)
                    done = pe.do(last)
                    k = act.after(done).do(A.activation(o_hg[:], self.psB[1][:], ACT.Copy))
                    sq = e[:].rearrange("p h t -> p (h t)").rearrange("p (t n) -> p t n", t=TT)
                    m = dve.after(k).do(V.tensor_tensor(sq, o_hg[:], o_hg[:], ALU.mult))
                    m = dve.after(m).do(V.tensor_reduce(st[:, 0], sq.rearrange("p t (h d) -> p (t h) d", d=HGD),
                                                        axis=AX.X, op=ALU.add))
                    m = dve.after(m).do(V.tensor_scalar(st[:, 0], st[:, 0], 1.0 / HGD, EPS, ALU.mult, ALU.add))
                    r = self.rsqrt(st[:, 0], st[:, 1], st[:, 2], m)
                    oh = o_hg[:].rearrange("p t (h d) -> p (t h) d", d=HGD)
                    m = dve.after(r).do(V.tensor_tensor(
                        oh, oh, st[:, 1].unsqueeze(2).to_broadcast([P, TT * HGH, HGD]), ALU.mult))
                    m = dve.after(m, self.late.now()).do(V.tensor_tensor(
                        o_hg[:], o_hg[:], gn[:].unsqueeze(1).to_broadcast([P, TT, HGW]), ALU.mult))
                    m = dve.after(m).do(V.tensor_tensor(o_hg[:], o_hg[:], sig_g[:], ALU.mult))
                    self.join()
            oT = self.sb("branch_T", [P, 2, 4, T], ctx=c)
            ready = self.to_T(o_sb, oT[:, 0])
            ready = self.to_T(o_hg, oT[:, 1], ready)
            done = self.accumulate_nat(self.rows(a["w_branch_sb_2"][0], 0), oT[:, 0], True, True, self.psA, ready)
            g2 = lambda i: gates[:, i].rearrange("p t n -> p (t n)")
            psf = flat(self.psA[:])
            m = dve.after(done).do(V.tensor_tensor(g2(0), g2(0), psf, ALU.mult))
            done = self.accumulate_nat(self.rows(a["w_branch_hgrn_2"][0], 0), oT[:, 1], True, True, self.psA, m)
            m1 = dve.after(done).do(V.tensor_tensor(g2(1), g2(1), psf, ALU.mult))
            m = dve.after(m, m1).do(V.tensor_tensor(g2(0), g2(0), g2(1), ALU.add))
            m = self.to_T(gates[:, 0], self.hT, m)
            for j in range(2):
                done = self.accumulate_nat(self.rows(a["w_out_2"][0], j), self.hT[:, 4 * j:4 * j + 4, :],
                                           j == 0, j == 1, self.psA, m, m1)
            xf = flat(self.x[:])
            dve.after(done).do(V.scalar_tensor_tensor(xf, xf, ALPHA, psf, ALU.mult, ALU.add))
            self.join()

    def layer_norm(self, x, gain, bias, ctx, *ready):
        V, dve = self.nc.vector, self.dve
        bn = self.sb("bn_stats", [P, TT, 2, 6], ctx=ctx)
        mv = self.sb("mean_var", [P, TT, 2], ctx=ctx)
        w = self.sb("ln_work", [P, 3, TT], ctx=ctx)
        dve.after(*ready)
        for tt in range(TT):
            for h in range(2):
                dve.do(V.bn_stats(bn[:, tt, h, :], x[:, tt, h * 512:(h + 1) * 512]))
        dve.after(dve.done.now())
        for tt in range(TT):
            dve.do(V.bn_aggr(mv[:, tt, :], bn[:, tt]))
        m = dve.after(dve.done.now()).do(V.tensor_scalar(w[:, 0], mv[:, :, 1], LN_EPS, None, ALU.add))
        r = self.rsqrt(w[:, 0], w[:, 1], w[:, 2], m)
        dve.after(r)
        out = []
        for tt in range(TT):
            m = dve.do(V.tensor_scalar(x[:, tt, :], x[:, tt, :], mv[:, tt, 0:1], w[:, 1, tt:tt + 1],
                                       ALU.subtract, ALU.mult))
            m = dve.after(m).do(V.tensor_tensor(x[:, tt, :], x[:, tt, :], gain, ALU.mult))
            out.append(dve.after(m).do(V.tensor_tensor(x[:, tt, :], x[:, tt, :], bias, ALU.add)))
        return out


    def moe(self):
        nc, V, A, G, M = self.nc, self.nc.vector, self.nc.scalar, self.nc.gpsimd, self.nc.tensor
        pe, dve, act, pool = self.compute
        a, c = self.a, self.ctx
        sb = self.sb
        flat = lambda t: t.rearrange("p a b -> p (a b)")
        ln = sb("ln_params", [P, 4, D])
        acc = sb("moe_sum", [P, TT, D])
        cnt = sb("expert_counts", [1, NE], I32)
        slot = sb("slot_of_token", [P, TT, NE + 1])
        gate = sb("gate_of_token", [P, TT, NE + 1])
        bT = sb("b_up_T", [P, NE, 16])
        iota = sb("iota", [P, T])
        one_hot = sb("one_hot", [P, TT, SLOTS])
        weighted = sb("gated_one_hot", [P, TT, SLOTS])
        scatter = sb("scatter_matrix", [P, T])
        xg = sb("gathered_T", [P, KD, SLOTS])
        hid = sb("hidden", [P, 16, SLOTS])
        sig = sb("swish_gate", [P, KD, SLOTS])
        actT = sb("activated_T", [P, KD, SLOTS])
        y = sb("expert_out", [P, D])
        U, X, Y = self.psA, self.psB[0], self.psB[1]
        Uw = U[:].rearrange("p a b -> p (a b)").rearrange("p (n s) -> p n s", s=SLOTS)
        Xg = X[:].rearrange("p a b -> p (a b)").rearrange("p (n s) -> p n s", s=SLOTS)

        for i, name in enumerate(("ln1_g_2", "ln1_b_2", "ln2_g_2", "ln2_b_2")):
            self.late.add(A.dma_start(ln[:, i, :], a[name][0].partition_broadcast(P)))
        with ExitStack() as c2:
            rw = sb("router_w", [P, KD, NE], ctx=c2)
            rb = sb("router_b", [P, NE], ctx=c2)
            brow = sb("b_up_rows", [P, 512], ctx=c2)
            bdown = sb("b_down", [P, D], ctx=c2)
            gT = sb("gate_T", [P, T], ctx=c2)
            logit = sb("logits", [P, TT, NE], ctx=c2)
            top = sb("top8", [P, TT, 8], ctx=c2)
            idx = sb("top8_index", [P, TT, 8], U32, ctx=c2)
            idxf = sb("top8_index_f", [P, TT, 8], ctx=c2)
            gts = sb("top4_gates", [P, TT, 2 * TOPK], ctx=c2)
            st = sb("router_stats", [P, TT, 2], ctx=c2)
            sel = sb("chosen", [P, TT, NE], ctx=c2)
            tmp = sb("one_choice", [P, TT, 2, NE], ctx=c2)
            z = [pool.do(G.memset(t, v)) for t, v in (
                (slot[:], -1.0), (gate[:], 0.0), (bdown[:], 0.0), (gT[:], 0.0), (scatter[:], 0.0), (y[:], 0.0))]
            pool.do(G.iota(iota[:], pattern=[[1, T]], base=0, channel_multiplier=0,
                           allow_small_or_imprecise_dtypes=True))
            act.after(pool.done.now())
            self.late.add(A.dma_start(rw[:], a["router_w_2"][0].rearrange("(k p) n -> p k n", p=P)))
            self.late.add(A.dma_start(rb[:], a["router_b_2"][0].partition_broadcast(P)))
            self.late.add(A.dma_start(brow[:], a["expert_b_up_2"][0].rearrange("e (q n) -> (e q) n", q=4)))
            self.late.add(A.dma_start(bdown[0:NE, :], a["expert_b_down_2"][0]))
            loaded = self.late.now()
            ln1 = self.layer_norm(self.x, ln[:, 0, :], ln[:, 1, :], c2, loaded, dve.done.now())
            hT = self.to_T(self.x, self.hT, *ln1)
            pe.after(hT, loaded)
            for tt in range(TT):
                for k in range(KD):
                    last = M.matmul(U[:, tt, 0:NE], self.hT[:, k, tt * P:(tt + 1) * P], rw[:, k, :],
                                    start=(k == 0), stop=(k == KD - 1))
            done = pe.do(last)
            m = dve.after(done, loaded).do(V.tensor_tensor(
                logit[:], U[:, 0:TT, 0:NE], rb[:].unsqueeze(1).to_broadcast([P, TT, NE]), ALU.add))
            dve.after(m)
            for tt in range(TT):
                m = dve.do(V.max(top[:, tt, :], logit[:, tt, :]))
                dve.after(m).do(V.max_index(idx[:, tt, :], top[:, tt, :], logit[:, tt, :]))
            dve.after(dve.done.now()).do(V.tensor_copy(idxf[:], idx[:]))
            m = dve.do(V.tensor_scalar(st[:, :, 0:1], top[:, :, 0:1], -1.0, None, ALU.mult))
            act.after(m)
            for tt in range(TT):
                k = act.do(A.activation(gts[:, tt, 0:TOPK], top[:, tt, 0:TOPK], ACT.Exp,
                                        bias=st[:, tt, 0:1], accum_out=st[:, tt, 1:2]))
            m = dve.after(k).do(V.reciprocal(st[:, :, 1:2], st[:, :, 1:2]))
            m = dve.after(m).do(V.tensor_tensor(gts[:, :, TOPK:], gts[:, :, 0:TOPK],
                                                st[:, :, 1:2].to_broadcast([P, TT, TOPK]), ALU.mult))
            dve.after(m, *z)
            for tt in range(TT):
                for j in range(TOPK):
                    one, gated = (sel[:, tt], gate[:, tt, 0:NE]) if j == 0 else (tmp[:, tt, 0], tmp[:, tt, 1])
                    pick = idxf[:, tt, j:j + 1]
                    dve.after(dve.done.now()).do(V.tensor_scalar(one, iota[:, 0:NE], pick, None, ALU.is_equal))
                    m = dve.do(V.tensor_scalar(gated, iota[:, 0:NE], pick, gts[:, tt, TOPK + j:TOPK + j + 1],
                                               ALU.is_equal, ALU.mult))
                    if j:
                        dve.after(m).do(V.tensor_tensor(sel[:, tt], sel[:, tt], one, ALU.add))
                        m = dve.do(V.tensor_tensor(gate[:, tt, 0:NE], gate[:, tt, 0:NE], gated, ALU.add))
            pe.after(m)
            M.matmul(U[:, 2, 0:NE], self.before[:], sel[:, 0], start=True, stop=True)
            M.matmul(U[:, 3, 0:NE], self.ones[:], sel[:, 0], start=True, stop=False)
            M.matmul(U[:, 3, 0:NE], self.before[:], sel[:, 1], start=False, stop=True)
            M.matmul(U[:, 0, 0:NE], self.ones[:], sel[:, 0], start=True, stop=False)
            last = M.matmul(U[:, 0, 0:NE], self.ones[:], sel[:, 1], start=False, stop=True)
            done = pe.do(last)
            m = dve.after(done).do(V.scalar_tensor_tensor(slot[:, :, 0:NE], U[:, 2:4, 0:NE], 1.0, sel[:],
                                                          ALU.add, ALU.mult))
            dve.after(m).do(V.tensor_scalar(slot[:, :, 0:NE], slot[:, :, 0:NE], -1.0, None, ALU.add))
            counted = dve.do(V.tensor_copy(cnt[:], U[0:1, 0, 0:NE]))
            pe.after(hT)
            for par in range(2):
                for m2 in range(2):
                    last = M.transpose(Y[:, 0, (2 * par + m2) * P:(2 * par + m2 + 1) * P],
                                       brow[:, 256 * m2 + par:256 * (m2 + 1):2], self.ident[:])
            done = pe.do(last)
            for par in range(2):
                for m2 in range(2):
                    src = Y[:, 0, (2 * par + m2) * P:(2 * par + m2 + 1) * P].rearrange("p (e q) -> p e q", q=4)
                    dve.after(done).do(V.tensor_copy(bT[:, :, 8 * par + m2:8 * par + 8:2], src))
            pe.after(m, *ln1)
            for tt in range(TT):
                last = M.transpose(Y[0:NE, 1, tt * P:(tt + 1) * P], gate[:, tt, 0:NE], self.ident[:])
            done = pe.do(last)
            m = dve.after(done, *z).do(V.tensor_copy(gT[0:NE, :], Y[0:NE, 1, 0:T]))
            pe.after(m, dve.done.now(), loaded)
            for tt in range(TT):
                for half in range(2):
                    last = M.matmul(U[:, 2 * tt + half, :], gT[:, tt * P:(tt + 1) * P],
                                    bdown[:, half * 512:(half + 1) * 512], start=True, stop=True)
            done = pe.do(last)
            m = dve.after(done).do(V.scalar_tensor_tensor(flat(acc[:]), flat(self.x[:]), ALPHA, flat(U[:]),
                                                          ALU.mult, ALU.add))
            dve.after(m).do(V.memset(U[:], 0.0))
            self.join()

        sem = lambda name: Count(self.sem(name))
        gathered, gather_copied = sem("x_gathered"), sem("gathered_copied")
        up_done, hidden_read = sem("up_products_done"), sem("up_products_read")
        activated, down_done, y_copied = sem("activated_tiles"), sem("down_products_done"), sem("out_copied")
        weighted_T, scatter_copied = sem("gated_transposed"), sem("scatter_matrix_copied")
        scattered, summed = sem("scattered_tiles"), sem("summed_tiles")
        built, gated = sem("one_hot_built"), sem("gated_one_hot_built")

        px, dx, ax = (Engine(e.engine, self.sem(n)) for e, n in (
            (pe, "extra_pe"), (dve, "extra_dve"), (act, "extra_act")))
        arrived_x = Count(self.sem("extra_panels_arrived"), 16)
        xg_x = sb("extra_gathered_T", [P, KD, SLOTS])
        scatter_x = sb("extra_scatter_matrix", [P, T])
        y_x = sb("extra_out", [P, D])

        w_up, w_down = a["expert_w_up_2"][0], a["expert_w_down_2"][0]
        order = [4, 5] + [(self.panels + r) % RING for r in range(RING)]
        panel = [self.ring[:, s, :].rearrange("p (k n) -> p k n", k=2 if j < 4 else 4)
                 for j, s in enumerate(order)]

        def sources(e):
            for j in range(4):
                yield w_up[bass.ds(e, 1), j * 256:(j + 1) * 256, :].rearrange("o (k p) n -> p (o k) n", p=P)
            for j in range(2):
                yield w_down[bass.ds(e, 1), j * 512:(j + 1) * 512, :].rearrange("o (k p) n -> p (o k) n", p=P)

        def choose(e, base, out, factor, count):
            for tt in range(TT):
                last = V.tensor_scalar(out[:, tt, :], iota[:, base:base + SLOTS], slot[:, tt, bass.ds(e, 1)],
                                       gate[:, tt, bass.ds(e, 1)] if factor else None, ALU.is_equal,
                                       **({"op1": ALU.mult} if factor else {}))
                mark = count.add(last)
            return mark

        def gather():
            for k in range(KD):
                for tt in range(TT):
                    last = M.matmul(Xg[:, k, :], self.x[:, tt, k * P:(k + 1) * P], one_hot[:, tt, :],
                                    start=(tt == 0), stop=(tt == TT - 1))
            return last

        def up(inp, width, arrived, free):
            for j in range(4):
                pe.after(arrived(j))
                for r in range(2):
                    k = 2 * j + r
                    for n in range(16):
                        par, m = n // 8, n % 8
                        last = M.matmul(Uw[:, n, 0:width], panel[j][:, r, 256 * m + par:256 * (m + 1):2],
                                        inp[:, k, 0:width], start=(k == 0 and n % 4 == 0),
                                        stop=(k == KD - 1 and n % 4 == 3))
                if free and j < 3:
                    free.add(last)
            return last

        def activate(half, e, d, s, ready, read, tiles):
            g, l = slice(4 * half, 4 * half + 4), slice(8 + 4 * half, 12 + 4 * half)
            bias = lambda part: bT[:, bass.ds(e, 1), part].rearrange("p o n -> p (o n)").unsqueeze(2) \
                .to_broadcast([P, 4, SLOTS])
            d.after(ready)
            mg = d.do(V.tensor_tensor(hid[:, g, :], Uw[:, g, :], bias(g), ALU.add))
            ml = read.add(V.tensor_tensor(hid[:, l, :], Uw[:, l, :], bias(l), ALU.add))
            m1 = d.after(mg).do(V.tensor_scalar(hid[:, g, :], hid[:, g, :], SWIGLU_LIMIT, None, ALU.min))
            k = s.after(m1).do(A.activation(sig[:, g, :], hid[:, g, :], ACT.Sigmoid, scale=SWIGLU_ALPHA))
            m2 = d.after(ml).do(V.tensor_scalar(hid[:, l, :], hid[:, l, :], -SWIGLU_LIMIT, SWIGLU_LIMIT,
                                                ALU.max, ALU.min))
            m3 = d.after(m2, m1).do(V.scalar_tensor_tensor(hid[:, l, :], hid[:, l, :], 1.0, hid[:, g, :],
                                                           ALU.add, ALU.mult))
            d.after(m3, k)
            return tiles.add(V.tensor_tensor(actT[:, g, :], hid[:, l, :], sig[:, g, :], ALU.mult))

        def down(j):
            for r in range(4):
                k = 4 * j + r
                for half in range(2):
                    last = M.matmul(Y[:, half, :], actT[:, k, :], panel[4 + j][:, r, half * 512:half * 512 + 512],
                                    start=(k == 0), stop=(k == KD - 1))
            return last

        def transpose_weighted(src, after_first=None):
            for tt in range(TT):
                last = M.transpose(X[:, 0, tt * P:(tt + 1) * P], src[:, tt, :], self.ident[:])
                if tt == 0 and after_first:
                    after_first.add(last)
            return last

        def scatter_tile(tt, matrix, rows, after_first=None):
            for half in range(2):
                last = M.matmul((X, Y)[tt][:, half, :], matrix[:, tt * P:(tt + 1) * P],
                                rows[:, half * 512:(half + 1) * 512], start=True, stop=True)
                if half == 0 and after_first:
                    after_first.add(last)
            return last

        def add_tile(tt):
            return V.tensor_tensor(acc[:, tt, :], acc[:, tt, :],
                                   (X, Y)[tt][:].rearrange("p a b -> p (a b)"), ALU.add)

        for eng, counts in ((pe, (gathered, up_done, down_done, weighted_T, scattered)),
                            (act, (gather_copied, y_copied, scatter_copied)),
                            (dve, (hidden_read, activated, summed, built, gated))):
            for n in counts:
                eng.engine.sem_inc(n.sem, 1)
                n.n += 1
        m = choose(0, 0, one_hot, False, built)
        pe.after(m)
        m = gathered.add(gather())
        act.after(m)
        m = gather_copied.add(A.activation(xg[:], Xg[:], ACT.Copy))

        shares = {self.freed: 6, dve.done: 8, act.done: 2, gathered: 1, gather_copied: 1, up_done: 1,
                  hidden_read: 2, activated: 2, down_done: 1, y_copied: 1, weighted_T: 1,
                  scatter_copied: 1, scattered: 2, summed: 2, built: 2, gated: 2,
                  px.done: 6, dx.done: 18, ax.done: 5, arrived_x: 6,
                  **{self.arrived[s]: 1 for s in order}}
        named = [n for n in shares if n not in (px.done, dx.done, ax.done, arrived_x)]
        with Loop(nc, NE, shares) as e:
            marks = []
            for j, src in enumerate(sources(e)):
                self.sp.after((self.freed, self.freed.n - 5 + j, self.freed.loop))
                self.sp.settle(self.settled)
                marks.append(self.arrived[order[j]].add(nc.sync.dma_start(panel[j], src)))
            self.sp.after(counted)
            self.sp.settle(self.settled)
            tokens = nc.values_load(cnt[0:1, bass.ds(e, 1)], min_val=0, max_val=T)
            dve.after(*(n.before_iteration() for n in (dve.done, built, gated, hidden_read, activated, summed)))
            dve.after(gathered.before_iteration())
            m_built = choose(e + 1, 0, one_hot, False, built)
            dve.after(weighted_T.before_iteration())
            m_gated = choose(e, 0, weighted, True, gated)
            pe.after(gather_copied.before_iteration(), hidden_read.before_iteration())
            state = (self.freed.n, up_done.n, dict(pe.waited))
            with nc.tensor.If(tokens < NARROW + 1):
                m_up = up_done.add(up(xg, NARROW, lambda j: marks[j], self.freed))
            self.freed.n, up_done.n, pe.waited = state
            with nc.tensor.Else():
                m_up = up_done.add(up(xg, SLOTS, lambda j: marks[j], self.freed))
            pe.after(y_copied.before_iteration(), scatter_copied.before_iteration())
            s0 = scattered.add(scatter_tile(0, scatter, y, self.freed))
            s1 = scattered.add(scatter_tile(1, scatter, y))
            dve.after(down_done.before_iteration())
            m_act = [activate(0, e, dve, act, m_up, hidden_read, activated)]
            dve.after(s0)
            a0 = summed.add(add_tile(0))
            m_act.append(activate(1, e, dve, act, m_up, hidden_read, activated))
            dve.after(s1)
            a1 = summed.add(add_tile(1))
            pe.after(m_built, a0)
            m_g = gathered.add(gather())
            act.after(m_g, m_up)
            m_gc = gather_copied.add(A.activation(xg[:], Xg[:], ACT.Copy))
            pe.after(a1, m_act[0], marks[4])
            self.freed.add(down(0))
            pe.after(m_act[1], marks[5])
            m_down = down_done.add(down(1))
            act.after(m_down, s1)
            m_y = y_copied.add(A.activation(y[:], Y[:].rearrange("p a b -> p (a b)"), ACT.Copy))
            pe.after(m_gated, m_gc)
            m_t = weighted_T.add(transpose_weighted(weighted, self.freed))
            act.after(m_t, s1)
            m_sc = scatter_copied.add(A.activation(scatter[:], X[:, 0, 0:T], ACT.Copy))

            ends = [n.now() for n in named]
            over = (self.sp, pe, dve, act)
            kept = [dict(eng.waited) for eng in over]
            branch = nc.If(tokens > SLOTS)
            branch.__enter__()
            for eng in over:
                eng.after(*(ends if eng is not self.sp else [self.freed.now()]))
                eng.settle(self.settled)
            for j, src in enumerate(sources(e)):
                arrived_x.add(nc.sync.dma_start(panel[j], src))
            panels_in = arrived_x.now()
            m = choose(e, SLOTS, one_hot, False, dx.done)
            m = px.after(m).do(gather())
            m = ax.after(m).do(A.activation(xg_x[:], Xg[:], ACT.Copy))
            px.after(m, panels_in)
            m = px.do(up(xg_x, SLOTS, lambda j: None, None))
            t0 = activate(0, e, dx, ax, m, dx.done, dx.done)
            t1 = activate(1, e, dx, ax, m, dx.done, dx.done)
            px.after(t0, t1)
            down(0)
            m = px.do(down(1))
            m = ax.after(m).do(A.activation(y_x[:], Y[:].rearrange("p a b -> p (a b)"), ACT.Copy))
            dx.after(px.done.now())
            d = choose(e, SLOTS, one_hot, True, dx.done)
            t = px.after(d).do(transpose_weighted(one_hot))
            m = ax.after(t).do(A.activation(scatter_x[:], X[:, 0, 0:T], ACT.Copy))
            px.after(m)
            s0 = px.do(scatter_tile(0, scatter_x, y_x))
            s1 = px.do(scatter_tile(1, scatter_x, y_x))
            dx.after(s0, s1).do(add_tile(0))
            dx.do(add_tile(1))
            for eng in over:
                eng.after(px.done.now())
                if eng is not self.sp:
                    eng.after(dx.done.now(), ax.done.now(), arrived_x.now())
                eng.settle(self.settled)
            branch.__exit__(None, None, None)
            with nc.Else():
                for eng, count in ((self.sp, arrived_x), (pe, px.done), (dve, dx.done), (act, ax.done)):
                    eng.engine.sem_inc(count.sem, count.step * (count.n - count.loop[2]))
            for eng, waited in zip(over, kept):
                eng.waited = waited

        pe.after(y_copied.now(), scatter_copied.now())
        s0 = scattered.add(scatter_tile(0, scatter, y))
        s1 = scattered.add(scatter_tile(1, scatter, y))
        dve.after(s0, summed.now())
        summed.add(add_tile(0))
        dve.after(s1)
        m = summed.add(add_tile(1))
        out = self.layer_norm(acc, ln[:, 2, :], ln[:, 3, :], c, m)
        for tt in range(TT):
            self.sp.after(out[tt])
            self.stored.add(nc.sync.dma_start(self.out[0, tt * P:(tt + 1) * P, :], acc[:, tt, :]))
        self.sp.after(self.stored.now())


def build(nc, ctx, arrays, out):
    k = Kernel(nc, ctx, arrays, out)
    k.setup()
    k.griffin()
    k.mlp(0)
    k.fox()
    k.mlp(1)
    k.hybrid()
    k.moe()


_INS = [
    "x", "mix_norm", "mlp_norm", "mlp_w1", "mlp_w2", "lru_w_in", "lru_conv_w", "lru_conv_b", "lru_w_r",
    "lru_b_r", "lru_w_i", "lru_b_i", "lru_lambda", "lru_w_out", "fox_w_in", "fox_b_f", "fox_q_gain",
    "fox_k_gain", "fox_w_out", "w_in_2", "hgrn_lb_logits_2", "hgrn_norm_g_2", "w_branch_sb_2",
    "w_branch_hgrn_2", "w_out_2", "ln1_g_2", "ln1_b_2", "router_w_2", "router_b_2", "expert_w_up_2",
    "expert_b_up_2", "expert_w_down_2", "expert_b_down_2", "ln2_g_2", "ln2_b_2",
]


def kernel(**inputs):
    import concourse.bacc as _bacc
    import numpy as _np
    from concourse.bass_utils import run_bass_kernel_spmd as _run

    nc = _bacc.Bacc("TRN2", target_bir_lowering=False, num_devices=1)
    arrays, aps = {}, {}
    for name in _INS:
        a = _np.ascontiguousarray(inputs[name])
        arrays[f"in_{name}"] = a
        aps[name] = nc.dram_tensor(f"in_{name}", a.shape, mybir.dt.from_np(a.dtype), kind="ExternalInput").ap()
    out = nc.dram_tensor("out_x", (1, T, D), F32, kind="ExternalOutput").ap()
    with ExitStack() as ctx:
        build(nc, ctx, aps, out)
    r = _run(nc, [arrays], core_ids=[0])
    return r.results[0]["out_x"]
```

```python
from contextlib import ExitStack

import concourse.bass as bass
import concourse.mybir as mybir

F32 = mybir.dt.float32
I32 = mybir.dt.int32
U32 = mybir.dt.uint32
ALU = mybir.AluOpType
ACT = mybir.ActivationFunctionType
AX = mybir.AxisListType

P = 128
T = 256
TT = T // P
D = 1024
KD = D // P
DFF = 4 * D
NH, HD = 16, 64
SBH, SBW = 8, 512
HGH, HGD, HGW = 4, 128, 512
NE, TOPK = 32, 4
SLOTS = 64
RING = 4
XRING = 6
PANEL = 4096
EPS = 1e-6
LN_EPS = 1e-5
NEG = -1e30
ALPHA = 2.0 ** 0.25
SWIGLU_ALPHA, SWIGLU_LIMIT = 1.702, 7.0


class Count:

    def __init__(self, sem, step=1):
        self.sem, self.step, self.n, self.loop = sem, step, 0, None

    def add(self, instruction):
        instruction.then_inc(self.sem, self.step)
        self.n += 1
        return self.now()

    def now(self):
        return (self, self.n, self.loop)

    def before_iteration(self):
        return (self, self.loop[2], self.loop)


class Engine:

    def __init__(self, engine, sem):
        self.engine, self.done = engine, Count(sem) if sem is not None else None
        self.waited = {}

    def after(self, *marks):
        for mark in marks:
            if mark is None:
                continue
            count, n, loop = mark
            if n <= self.waited.get((count, loop), 0 if loop is None else -RING * 16):
                continue
            assert loop is None or loop is count.loop, "a mark of a loop is used outside of it"
            self.waited[count, loop] = n
            value = n * count.step
            if loop is not None:
                value = value + loop[0] * (loop[1] * count.step)
            self.engine.wait_ge(count.sem, value)
        return self

    def do(self, instruction):
        return self.done.add(instruction)

    def settle(self, sem):
        self.engine.sem_inc(sem, 1)


class Share(tuple):

    __hash__ = object.__hash__

    def __eq__(self, other):
        return self is other


class Loop:

    def __init__(self, nc, trips, shares):
        self.nc, self.trips, self.shares = nc, trips, shares

    def __enter__(self):
        self.fori = self.nc.Fori(0, self.trips)
        i = self.fori.__enter__()
        for count, share in self.shares.items():
            count.loop = Share((i, share, count.n))
        return i

    def __exit__(self, *exc):
        if exc[0] is None:
            for count, share in self.shares.items():
                grown = count.n - count.loop[2]
                assert grown == share, f"{count.sem}: {grown} in an iteration, {share} stated"
                count.n = count.loop[2] + self.trips * share
                count.loop = None
        return self.fori.__exit__(*exc)


class Kernel:
    def __init__(self, nc, ctx, a, out):
        self.nc, self.ctx, self.a, self.out = nc, ctx, a, out
        sem = lambda name: ctx.enter_context(nc.semaphore(name))
        self.sem, self.made = sem, 0
        self.pe = Engine(nc.tensor, sem("pe_done"))
        self.dve = Engine(nc.vector, sem("dve_done"))
        self.act = Engine(nc.scalar, sem("act_done"))
        self.pool = Engine(nc.gpsimd, sem("pool_done"))
        self.sp = Engine(nc.sync, None)
        self.compute = (self.pe, self.dve, self.act, self.pool)
        self.arrived = [Count(sem(f"panel_in_slot{s}"), 16) for s in range(XRING)]
        self.freed = Count(sem("panels_consumed"))
        self.small = Count(sem("small_loads"), 16)
        self.late = Count(sem("late_loads"), 16)
        self.stored = Count(sem("stored"), 16)
        self.settled = sem("waits_settled")
        self.panels = 0
        self.ring = self.sb("panel_ring", [P, XRING, PANEL])
        self.psA = self.ps("psA", [P, 4, 512])
        self.psB = [self.ps(f"psB{j}", [P, 2, 512]) for j in range(2)]
        self.x = self.sb("x", [P, TT, D])
        self.hT = self.sb("hT", [P, KD, T])

    def sb(self, name, shape, dt=F32, ctx=None):
        self.made = self.made + 1
        return (ctx or self.ctx).enter_context(self.nc.sbuf_tensor(f"{name}_{self.made}", shape, dt))

    def ps(self, name, shape, dt=F32):
        return self.ctx.enter_context(self.nc.psum_tensor(name, shape, dt))

    def join(self):
        for e in self.compute:
            for other in self.compute:
                e.after(other.done.now())
            e.after(self.freed.now())


    def load_panel(self, source, parts):
        slot = self.panels % RING
        self.panels += 1
        view = self.ring[:, slot, :].rearrange("p (k n) -> p k n", k=parts)
        count, n, loop = self.freed, self.panels - RING, self.freed.loop
        self.sp.after((count, n, loop))
        if loop is not None:
            self.sp.settle(self.settled)
        mark = self.arrived[slot].add(self.nc.sync.dma_start(view, source))
        return view, mark

    def columns(self, w, j):
        return self.load_panel(w[:, j * 512:(j + 1) * 512].rearrange("(k p) n -> p k n", p=P), KD)

    def rows(self, w, j):
        return self.load_panel(w[j * 512:(j + 1) * 512, :].rearrange("(k p) n -> p k n", p=P), 4)

    def project_T(self, panel, hT, ps, *ready):
        w, arrived = panel
        self.pe.after(arrived, *ready)
        out = ps[:].rearrange("p a b -> p (a b)").rearrange("p (m t) -> p m t", t=T)
        for m in range(4):
            for k in range(KD):
                last = self.nc.tensor.matmul(out[:, m, :], w[:, k, m * P:(m + 1) * P], hT[:, k, :],
                                             start=(k == 0), stop=(k == KD - 1))
        return out, self.freed.add(last)

    def project_nat(self, panel, hT, ps, *ready):
        w, arrived = panel
        self.pe.after(arrived, *ready)
        for tt in range(TT):
            for k in range(KD):
                last = self.nc.tensor.matmul(ps[:, tt, :], hT[:, k, tt * P:(tt + 1) * P], w[:, k, :],
                                             start=(k == 0), stop=(k == KD - 1))
        return self.freed.add(last)

    def accumulate_nat(self, panel, aT, first, last, ps, *ready):
        w, arrived = panel
        self.pe.after(arrived, *ready)
        for k in range(4):
            for tt in range(TT):
                for half in range(2):
                    mm = self.nc.tensor.matmul(ps[:, 2 * tt + half, :], aT[:, k, tt * P:(tt + 1) * P],
                                               w[:, k, half * 512:(half + 1) * 512],
                                               start=first and k == 0, stop=last and k == 3)
        return self.freed.add(mm)


    def transpose_to(self, src, j0, n, ps, *ready):
        self.pe.after(*ready)
        out = ps[:].rearrange("p a b -> p (a b)").rearrange("p (m t) -> p m t", t=T)
        for m in range(n):
            for tt in range(TT):
                last = self.nc.tensor.transpose(out[:, m, tt * P:(tt + 1) * P],
                                                src[:, tt, (j0 + m) * P:(j0 + m + 1) * P], self.ident[:])
        return out, self.pe.do(last)

    def to_T(self, src, dst, *ready, scale=None):
        n, V = src.shape[2] // P, self.nc.vector
        marks = [None, None]
        for g in range((n + 3) // 4):
            m = min(4, n - 4 * g)
            out, done = self.transpose_to(src, 4 * g, m, self.psB[g % 2], *ready, marks[g % 2])
            to = dst[:, 4 * g:4 * g + m, :]
            self.dve.after(done)
            if scale is None:
                marks[g % 2] = self.dve.do(V.tensor_copy(to, out[:, 0:m, :]))
            else:
                s = scale[:, 4 * g:4 * g + m].unsqueeze(2).to_broadcast([P, m, T])
                marks[g % 2] = self.dve.do(V.tensor_tensor(to, out[:, 0:m, :], s, ALU.mult))
        return self.dve.done.now()

    def rsqrt(self, ms, y, t, *ready):
        V, dve, act = self.nc.vector, self.dve, self.act
        a = act.after(*ready).do(self.nc.scalar.activation(y, ms, ACT.Ln))
        a = act.after(a).do(self.nc.scalar.activation(y, y, ACT.Exp, scale=-0.5))
        m = dve.after(a).do(V.tensor_tensor(t, y, y, ALU.mult))
        m = dve.after(m).do(V.tensor_tensor(t, t, ms, ALU.mult))
        m = dve.after(m).do(V.tensor_scalar(t, t, -0.5, 1.5, ALU.mult, ALU.add))
        return dve.after(m).do(V.tensor_tensor(y, y, t, ALU.mult))

    def rms_to_hT(self, gain):
        V, dve, act = self.nc.vector, self.dve, self.act
        self.join()
        with ExitStack() as c:
            xn = self.sb("x_normed", [P, TT, D], ctx=c)
            st = self.sb("rms_stats", [P, 4, TT], ctx=c)
            for tt in range(TT):
                act.do(self.nc.scalar.activation(xn[:, tt, :], self.x[:, tt, :], ACT.Square,
                                                 accum_out=st[:, 0, tt:tt + 1]))
            m = dve.after(act.done.now()).do(
                V.tensor_scalar(st[:, 1, :], st[:, 0, :], 1.0 / D, EPS, ALU.mult, ALU.add))
            r = self.rsqrt(st[:, 1, :], st[:, 2, :], st[:, 3, :], m)
            for tt in range(TT):
                m = dve.after(r).do(V.tensor_scalar(xn[:, tt, :], self.x[:, tt, :], st[:, 2, tt:tt + 1],
                                                    None, ALU.mult))
            self.to_T(xn, self.hT, m, scale=gain)
            self.join()


    def setup(self):
        nc, G, pool = self.nc, self.nc.gpsimd, self.pool
        a = self.a
        for tt in range(TT):
            self.small.add(nc.scalar.dma_start(self.x[:, tt, :], a["x"][0, tt * P:(tt + 1) * P, :]))
        rows = self.sb("param_rows", [P, P])
        z = pool.do(G.memset(rows[:], 0.0))
        at, self.col_of = 0, {}
        nc.scalar.wait_ge(self.pool.done.sem, 1)

        def put(name, src, n):
            nonlocal at
            self.small.add(nc.scalar.dma_start(rows[at:at + n, :], src))
            self.col_of[name] = at
            at += n

        put("mix", a["mix_norm"].rearrange("l (c p) -> (l c) p", p=P), 16)
        put("mlp", a["mlp_norm"].rearrange("l (c p) -> (l c) p", p=P), 16)
        put("conv_w", a["lru_conv_w"][0].rearrange("l (c p) -> (l c) p", p=P), 32)
        put("conv_b", a["lru_conv_b"][0].rearrange("(c p) -> c p", p=P), 8)
        put("b_r", a["lru_b_r"][0].rearrange("(c n) p -> c (n p)", n=2), 8)
        put("b_i", a["lru_b_i"][0].rearrange("(c n) p -> c (n p)", n=2), 8)
        put("lam", a["lru_lambda"][0].rearrange("(c p) -> c p", p=P), 8)
        put("lb", a["hgrn_lb_logits_2"].rearrange("l (c p) -> (l c) p", p=P), 8)
        for name in ("q_gain", "k_gain"):
            for half in range(2):
                self.small.add(nc.scalar.dma_start(rows[at:at + 1, half * HD:(half + 1) * HD],
                                                   a["fox_" + name]))
            self.col_of[name] = at
            at += 1
        self.ident = self.sb("ident", [P, P])
        self.ones = self.sb("ones", [P, P])
        self.before = self.sb("before", [P, P])
        self.after_ = self.sb("after_", [P, P])
        m0 = pool.do(G.memset(self.ident[:], 0.0))
        m1 = pool.do(G.memset(self.ones[:], 1.0))
        pool.after(m0).do(G.affine_select(out=self.ident[:], in_=self.ident[:], compare_op=ALU.not_equal,
                                          fill=1.0, base=0, pattern=[[-1, P]], channel_multiplier=1))
        pool.after(m1).do(G.affine_select(out=self.before[:], in_=self.ones[:], compare_op=ALU.is_gt,
                                          fill=0.0, base=0, pattern=[[1, P]], channel_multiplier=-1))
        pool.do(G.affine_select(out=self.after_[:], in_=self.ones[:], compare_op=ALU.is_gt,
                                fill=0.0, base=0, pattern=[[-1, P]], channel_multiplier=1))
        self.cols = self.sb("param_cols", [P, P])
        self.pe.after(pool.done.now(), self.small.now())
        t = self.pe.do(nc.tensor.transpose(self.psB[0][:, 0, 0:P], rows[:], self.ident[:]))
        self.dve.after(t).do(nc.vector.tensor_copy(self.cols[:], self.psB[0][:, 0, 0:P]))
        for e in self.compute:
            e.after(self.small.now())
        self.join()

    def col(self, name, n, skip=0):
        at = self.col_of[name] + skip
        return self.cols[:, at:at + n]


    def griffin(self):
        nc, V, A, G = self.nc, self.nc.vector, self.nc.scalar, self.nc.gpsimd
        pe, dve, act, pool = self.compute
        a = self.a
        self.rms_to_hT(self.col("mix", KD))
        with ExitStack() as c:
            sb = lambda n, s: self.sb(n, s, ctx=c)
            gate = sb("gate", [P, KD, T])
            xpad = sb("x_branch", [P, KD, T + 3])
            xc = sb("x_conv", [P, KD, T])
            wri = sb("w_ri", [P, 2, KD, P])
            ra = sb("r_then_a", [P, KD, T])
            ib = sb("i_then_b", [P, KD, T])
            th = sb("tanh_then_h", [P, KD, T])
            lam = sb("lam_work", [P, 5, KD])
            z0 = pool.do(G.memset(wri[:], 0.0))
            z1 = pool.do(G.memset(xpad[:, :, 0:3], 0.0))
            act.after(z0)
            for n, name in enumerate(("lru_w_r", "lru_w_i")):
                w = a[name][0].rearrange("(c n) d e -> d n c e", n=2)
                for half in range(2):
                    self.late.add(A.dma_start(wri[half * 64:half * 64 + 64, n, :, half * 64:half * 64 + 64],
                                              w[:, half, :, :]))
            u, s, s2, acc, ls = (lam[:, i, :] for i in range(5))
            L = self.col("lam", KD)
            k = act.do(A.activation(u, L, ACT.Abs))
            k = act.after(k).do(A.activation(u, u, ACT.Exp, scale=-1.0))
            m = dve.after(k).do(V.tensor_scalar(s2, u, 2.0, None, ALU.add))
            m = dve.after(m).do(V.reciprocal(s, s2))
            m = dve.after(m).do(V.tensor_tensor(s, s, u, ALU.mult))
            m = dve.after(m).do(V.tensor_tensor(s2, s, s, ALU.mult))
            m = dve.after(m).do(V.tensor_scalar(acc, s2, 2.0 / 17, 2.0 / 15, ALU.mult, ALU.add))
            for odd in (13, 11, 9, 7, 5, 3, 1):
                m = dve.after(m).do(V.tensor_tensor(acc, acc, s2, ALU.mult))
                m = dve.after(m).do(V.tensor_scalar(acc, acc, 2.0 / odd, None, ALU.add))
            m = dve.after(m).do(V.tensor_tensor(acc, acc, s, ALU.mult))
            m = dve.after(m).do(V.tensor_scalar(ls, L, 0.0, None, ALU.min))
            m = dve.after(m).do(V.tensor_tensor(ls, ls, acc, ALU.subtract))
            c8 = dve.after(m).do(V.tensor_scalar(ls, ls, 8.0, None, ALU.mult))

            w_in = a["lru_w_in"][0]
            free = [None, None]
            for j in range(4):
                out, done = self.project_T(self.columns(w_in, j), self.hT, self.psB[j % 2], free[j % 2])
                if j < 2:
                    free[j % 2] = act.after(done).do(
                        A.activation(gate[:, 4 * j:4 * j + 4, :], out, ACT.Gelu_apprx_tanh))
                    continue
                t0 = 4 * (j - 2)
                copied = dve.after(done, z1).do(V.tensor_copy(xpad[:, t0:t0 + 4, 3:3 + T], out))
                free[j % 2] = copied
                w = lambda k, t: self.col("conv_w", 1, 8 * k + t)
                tiles = range(t0, t0 + 4)
                m = {}
                for t in tiles:
                    m[t] = dve.after(copied).do(V.tensor_scalar(
                        xc[:, t, :], xpad[:, t, 0:T], w(0, t), self.col("conv_b", 1, t), ALU.mult, ALU.add))
                for k in range(1, 4):
                    for t in tiles:
                        m[t] = dve.after(m[t]).do(V.scalar_tensor_tensor(
                            xc[:, t, :], xpad[:, t, k:k + T], w(k, t), xc[:, t, :], ALU.mult, ALU.add))
            conv = dve.done.now()
            pe.after(conv, self.late.now(), *free)
            rps = self.psA[:].rearrange("p a (b t) -> p (a b) t", t=T)
            for t in range(KD):
                r_done = nc.tensor.matmul(rps[:, t, :], wri[:, 0, t, :], xc[:, t, :], start=True, stop=True)
            r_done = pe.do(r_done)
            ips = [self.psB[j][:].rearrange("p a (b t) -> p (a b) t", t=T) for j in range(2)]
            for t in range(KD):
                i_done = nc.tensor.matmul(ips[t // 4][:, t % 4, :], wri[:, 1, t, :], xc[:, t, :],
                                          start=True, stop=True)
            i_done = pe.do(i_done)
            act.after(r_done)
            for t in range(KD):
                act.do(A.activation(ra[:, t, :], rps[:, t, :], ACT.Sigmoid, bias=self.col("b_r", 1, t)))
            r_ready = act.done.now()
            act.after(i_done)
            for t in range(KD):
                act.do(A.activation(ib[:, t, :], ips[t // 4][:, t % 4, :], ACT.Sigmoid,
                                    bias=self.col("b_i", 1, t)))
            i_ready = act.done.now()
            c8b = ls.unsqueeze(2).to_broadcast([P, KD, T])
            m = dve.after(r_ready, c8).do(V.tensor_tensor(ra[:], ra[:], c8b, ALU.mult))
            k1 = act.after(m).do(A.activation(th[:], ra[:], ACT.Tanh))
            k2 = act.after(k1).do(A.activation(ra[:], ra[:], ACT.Exp))
            b = dve.after(i_ready).do(V.tensor_tensor(ib[:], ib[:], xc[:], ALU.mult))
            m = dve.after(k2, conv, b).do(V.tensor_tensor(xc[:], ra[:], ra[:], ALU.mult))
            m = dve.after(m, k1).do(V.scalar_tensor_tensor(th[:], xc[:], 1.0, th[:], ALU.add, ALU.mult))
            k = act.after(m).do(A.activation(th[:], th[:], ACT.Sqrt, scale=-1.0))
            b = dve.after(k, b).do(V.tensor_tensor(ib[:], ib[:], th[:], ALU.mult))
            dve.after(b)
            for t in range(KD):
                h = dve.do(V.tensor_tensor_scan(th[:, t, :], ra[:, t, :], ib[:, t, :], 0.0,
                                                ALU.mult, ALU.add))
            y = dve.after(h, act.done.now()).do(V.tensor_tensor(gate[:], gate[:], th[:], ALU.mult))
            w_out = a["lru_w_out"][0]
            for j in range(2):
                done = self.accumulate_nat(self.rows(w_out, j), gate[:, 4 * j:4 * j + 4, :], j == 0, j == 1,
                                           self.psA, y, r_ready)
            self.add_to_x(done)
            self.join()

    def add_to_x(self, done, ps=None):
        flat = self.x[:].rearrange("p t n -> p (t n)")
        src = (ps or self.psA)[:].rearrange("p a b -> p (a b)")
        return self.dve.after(done).do(self.nc.vector.tensor_tensor(flat, flat, src, ALU.add))


    def mlp(self, layer):
        nc, V, A = self.nc, self.nc.vector, self.nc.scalar
        pe, dve, act, pool = self.compute
        self.rms_to_hT(self.col("mlp", KD, KD * layer))
        w1, w2 = self.a["mlp_w1"][layer], self.a["mlp_w2"][layer]
        with ExitStack() as c:
            relu = self.sb("relu", [P, 2, 4, T], ctx=c)
            aT = self.sb("aT", [P, 8, T], ctx=c)
            shares = {self.freed: 4, act.done: 2, dve.done: 3, **{s: 1 for s in self.arrived[:RING]}}
            with Loop(nc, 4, shares) as i:
                for j in range(2):
                    cols = w1[:, bass.ds(i * 1024 + j * 512, 512)]
                    panel = self.load_panel(cols.rearrange("(k p) n -> p k n", p=P), KD)
                    out, done = self.project_T(panel, self.hT, self.psB[j],
                                               act.done.before_iteration(), dve.done.before_iteration())
                    r = act.after(done, dve.done.before_iteration()).do(
                        A.activation(relu[:, j], out, ACT.Relu))
                    sq = dve.after(r, self.freed.before_iteration()).do(
                        V.tensor_tensor(aT[:, 4 * j:4 * j + 4, :], relu[:, j], relu[:, j], ALU.mult))
                for j in range(2):
                    rows = w2[bass.ds(i * 1024 + j * 512, 512), :]
                    panel = self.load_panel(rows.rearrange("(k p) n -> p k n", p=P), 4)
                    done = self.accumulate_nat(panel, aT[:, 4 * j:4 * j + 4, :], j == 0, j == 1, self.psA,
                                               sq, dve.done.before_iteration())
                self.add_to_x(done)
            self.panels += 3 * 4
            self.join()


    def weighted_values(self, pT, v, heads, ps, *ready):
        M = self.nc.tensor
        self.pe.after(*ready)
        out = ps[:, 0, :].rearrange("p (h t d) -> p h t d", t=TT, d=HD)
        for g, h in enumerate(heads):
            vh = v[:, :, h * HD:(h + 1) * HD]
            M.matmul(out[:, g, 0, :], pT[:, g, 0:P], vh[:, 0, :], start=True, stop=True)
            M.matmul(out[:, g, 1, :], pT[:, g, P:2 * P], vh[:, 0, :], start=True, stop=False)
            last = M.matmul(out[:, g, 1, :], pT[:, g, 2 * P:3 * P], vh[:, 1, :], start=False, stop=True)
        return out, self.pe.do(last)


    def fox(self):
        nc, V, A, G, M = self.nc, self.nc.vector, self.nc.scalar, self.nc.gpsimd, self.nc.tensor
        pe, dve, act, pool = self.compute
        a = self.a
        w_in = a["fox_w_in"][0]
        self.rms_to_hT(self.col("mix", KD, KD))
        with ExitStack() as c:
            sb = lambda n, s: self.sb(n, s, ctx=c)
            nat = [sb(n, [P, TT, D]) for n in ("q_nat", "k_nat", "v_nat")]
            v_nat = nat[2]
            qT = sb("qT", [P, KD, T])
            kTz = sb("kT_padded", [P, NH, T])
            c_sel = sb("minus_head_row", [P, NH, P])
            cT = sb("cum_log_f", [P, T])
            mask = sb("causal", [P, 3 * P])
            score = [sb(f"scores{i}", [P, 4, 3 * P]) for i in range(2)]
            pT = sb("pT", [P, 4, 3 * P])
            wf = sb("w_f", [P, KD, NH])
            bf = sb("b_f", [NH, 1])
            ss = sb("qk_stats", [P, 3, 2, TT * NH])
            nm = sb("minus_max", [P, NH, 3])
            den = sb("softmax_sums", [P, NH, 2])
            sq = sb("squares", [P, TT, 512])
            lf = sb("log_f_work", [NH, 2, T])
            z = pool.do(G.memset(kTz[:], 0.0))
            pool.do(G.memset(c_sel[:], 0.0))
            pool.do(G.memset(mask[:], 0.0))
            pool.do(G.memset(cT[:], 0.0))
            pool.after(pool.done.now())
            pool.do(G.affine_select(out=c_sel[:], in_=c_sel[:], compare_op=ALU.not_equal, fill=-1.0,
                                    base=0, pattern=[[-1, NH], [0, P]], channel_multiplier=1))
            for at in (0, 2 * P):
                pool.do(G.affine_select(out=mask[:, at:at + P], in_=mask[:, at:at + P],
                                        compare_op=ALU.is_ge, fill=NEG, base=0, pattern=[[-1, P]],
                                        channel_multiplier=1))
            act.after(pool.done.now())
            with nc.allow_non_contiguous_dma(reason="one value per partition"):
                self.late.add(A.dma_start(bf[:], a["fox_b_f"][0].rearrange("(n o) -> n o", o=1)))
            self.late.add(A.dma_start(wf[:], w_in[:, 3 * D:].rearrange("(k p) n -> p k n", p=P)))
            qg = self.col("q_gain", 1)
            gain8 = sb("q_gain_eighth", [P, 1])
            g8 = dve.do(V.tensor_scalar(gain8[:], qg, HD ** -0.5, None, ALU.mult))

            free = [None, None]
            for j in range(6):
                ps, n = self.psB[j % 2], nat[j // 2]
                done = self.project_nat(self.columns(w_in, j), self.hT, ps, free[j % 2])
                part = n[:, :, (j % 2) * 512:(j % 2) * 512 + 512]
                copied = act.after(done).do(A.activation(part, ps[:], ACT.Copy))
                free[j % 2] = copied
                if j < 4:
                    m = dve.after(copied, dve.done.now()).do(V.tensor_tensor(sq[:], part, part, ALU.mult))
                    dst = ss[:, 0, j // 2, :].rearrange("p (t h) -> p t h", t=TT)[:, :, 8 * (j % 2):8 * (j % 2) + 8]
                    m = dve.after(m).do(V.tensor_reduce(
                        dst, sq[:].rearrange("p t (h d) -> p t h d", d=HD), axis=AX.X, op=ALU.add))
            pe.after(self.late.now(), free[0])
            for k in range(KD):
                last = M.matmul(self.psB[0][0:NH, 0, 0:T], wf[:, k, :], self.hT[:, k, :],
                                start=(k == 0), stop=(k == KD - 1))
            fdone = pe.do(last)
            fps = self.psB[0][0:NH, 0, 0:T]
            k = act.after(fdone, self.late.now()).do(A.activation(lf[:, 0, :], fps, ACT.Abs, bias=bf[:]))
            bank_free = k
            k = act.after(k).do(A.activation(lf[:, 0, :], lf[:, 0, :], ACT.Exp, scale=-1.0))
            k = act.after(k).do(A.activation(lf[:, 0, :], lf[:, 0, :], ACT.Ln, bias=1.0))
            m = dve.after(bank_free, self.late.now()).do(V.tensor_scalar(lf[:, 1, :], fps, bf[:], 0.0, ALU.add, ALU.min))
            m = dve.after(m, k).do(V.tensor_tensor(lf[:, 1, :], lf[:, 1, :], lf[:, 0, :], ALU.subtract))
            one = self.ones[0:NH, 0:1].to_broadcast([NH, T])
            cdone = dve.after(m).do(V.tensor_tensor_scan(cT[0:NH, :], one, lf[:, 1, :], 0.0, ALU.mult, ALU.add))

            ms, y, t = (ss[:, i].rearrange("p a b -> p (a b)") for i in range(3))
            m = dve.do(V.tensor_scalar(ms, ms, 1.0 / HD, EPS, ALU.mult, ALU.add))
            r = self.rsqrt(ms, y, t, m)
            for i in range(2):
                v3 = nat[i][:].rearrange("p t (h d) -> p (t h) d", d=HD)
                m = dve.after(r).do(V.tensor_tensor(
                    v3, v3, ss[:, 1, i, :].unsqueeze(2).to_broadcast([P, TT * NH, HD]), ALU.mult))
            free = [cdone, None]
            for g in range(4):
                i = g // 2
                out, done = self.transpose_to(nat[i], 4 * (g % 2), 4, self.psB[g % 2], m, free[g % 2])
                c0 = 4 * (g % 2)
                if i == 0:
                    free[g % 2] = dve.after(done, g8).do(V.tensor_scalar(
                        qT[:, c0:c0 + 4, :], out[:], gain8[:], None, ALU.mult))
                else:
                    for half in range(2):
                        rows = slice(64 * half, 64 * half + 64)
                        to = kTz[rows, 2 * c0 + half:2 * c0 + 8:2, :]
                        free[g % 2] = dve.after(done, z).do(V.tensor_scalar(
                            to, out[rows], self.col("k_gain", 1)[rows], None, ALU.mult))
            qk = dve.done.now()

            o_nat = nat[0]
            s_free, o_read, p_free = None, None, None
            for g in range(4):
                heads = range(4 * g, 4 * g + 4)
                S, sc = self.psA, score[g % 2]
                pe.after(qk, cdone, pool.done.now(), s_free)
                for i, h in enumerate(heads):
                    for t0, s1, at in ((0, P, 0), (P, T, P)):
                        out = S[:, i, at:at + s1]
                        M.matmul(out, qT[:, h // 2, t0:t0 + P], kTz[:, h, 0:s1], start=True, stop=False)
                        last = M.matmul(out, c_sel[:, h, :], cT[:, 0:s1], start=False, stop=True)
                s_done = pe.do(last)
                mb = mask[:].unsqueeze(1).to_broadcast([P, 4, 3 * P])
                m = dve.after(s_done, pool.done.now(), o_read).do(V.tensor_tensor(sc[:], S[:, :, 0:3 * P], mb, ALU.add))
                s_free = m
                hs = slice(4 * g, 4 * g + 4)
                dve.after(m).do(V.tensor_reduce(nm[:, hs, 0], sc[:, :, 0:P], axis=AX.X, op=ALU.max, negate=True))
                m = dve.do(V.tensor_reduce(nm[:, hs, 1], sc[:, :, P:], axis=AX.X, op=ALU.max, negate=True))
                act.after(m)
                for i, h in enumerate(heads):
                    for j, cols in enumerate((slice(0, P), slice(P, 3 * P))):
                        k = act.do(A.activation(sc[:, i, cols], sc[:, i, cols], ACT.Exp,
                                                bias=nm[:, h, j:j + 1], accum_out=den[:, h, j:j + 1]))
                pe.after(k, o_read, p_free)
                for i in range(4):
                    bank = self.psB[i // 2][:, i % 2, :]
                    for b in range(3):
                        last = M.transpose(bank[:, b * P:(b + 1) * P], sc[:, i, b * P:(b + 1) * P], self.ident[:])
                t_done = pe.do(last)
                r = dve.after(k).do(V.reciprocal(den[:, hs, :], den[:, hs, :]))
                act.after(t_done, pe.done.now()).do(A.activation(pT[:, 0:2, :], self.psB[0][:, :, 0:3 * P], ACT.Copy))
                p_free = dve.after(t_done).do(V.tensor_copy(pT[:, 2:4, :], self.psB[1][:, :, 0:3 * P]))
                out, done = self.weighted_values(pT, v_nat, heads, self.psB[0], act.done.now(), p_free)
                to = o_nat[:, :, 4 * g * HD:(4 * g + 4) * HD].rearrange("p t (h d) -> p h t d", d=HD)
                o_read = dve.after(done, r).do(V.tensor_tensor(
                    to, out, den[:, hs, :].unsqueeze(3).to_broadcast([P, 4, 2, HD]), ALU.mult))
            o = self.to_T(o_nat, self.hT, o_read)
            w_out = a["fox_w_out"][0]
            for j in range(2):
                done = self.accumulate_nat(self.rows(w_out, j), self.hT[:, 4 * j:4 * j + 4, :], j == 0, j == 1,
                                           self.psA, o, s_free)
            self.add_to_x(done)
            self.join()


    def hybrid(self):
        nc, V, A, G, M = self.nc, self.nc.vector, self.nc.scalar, self.nc.gpsimd, self.nc.tensor
        pe, dve, act, pool = self.compute
        a = self.a
        w_in = a["w_in_2"][0]
        self.join()
        flat = lambda t: t.rearrange("p a b -> p (a b)")
        with ExitStack() as c:
            sb = lambda n, s, dt=F32: self.sb(n, s, dt, ctx=c)
            o_sb = sb("o_sb", [P, TT, SBW])
            o_hg = sb("o_hg", [P, TT, HGW])
            gates = sb("gates", [P, 2, TT, D])
            sig_g = sb("sigmoid_hg", [P, TT, HGW])
            with ExitStack() as c2:
                sb2 = lambda n, s, dt=F32: self.sb(n, s, dt, ctx=c2)
                qT = sb2("sb_qT", [P, 4, T])
                kTz = sb2("sb_kT_padded", [P, SBH, T])
                v_sb = sb2("sb_v", [P, TT, SBW])
                hq = sb2("hg_q", [P, HGH, T])
                hk = sb2("hg_k", [P, HGH, T])
                hb = sb2("hg_cum_log_f", [P, HGH, T])
                hv = sb2("hg_v", [P, TT, HGW])
                mask = sb2("sb_mask", [P, 3 * P])
                lvl = sb2("level_masks", [P, 7, P])
                keep = sb2("scan_keep", [P, T])
                gn = sb2("hgrn_gain", [P, HGW])
                self.late.add(A.dma_start(gn[:], a["hgrn_norm_g_2"][0].partition_broadcast(P)))
                lb = sb2("lb_work", [P, 4, 4])
                z = pool.do(G.memset(kTz[:], 0.0))
                pool.do(G.memset(mask[:], 1.0))
                pool.do(G.memset(lvl[:], 1.0))
                k0 = pool.do(G.memset(keep[:], 1.0))
                pool.after(k0)
                pool.do(G.memset(keep[:].rearrange("p (n t) -> p n t", t=P)[:, :, 0:1], 0.0))
                pool.do(G.affine_select(out=mask[:, 0:T], in_=mask[:, 0:T], compare_op=ALU.is_gt, fill=0.0,
                                        base=0, pattern=[[1, T]], channel_multiplier=-1))
                pool.do(G.affine_select(out=mask[:, T:], in_=mask[:, T:], compare_op=ALU.is_gt, fill=0.0,
                                        base=0, pattern=[[1, P]], channel_multiplier=-1))
                for l in range(7):
                    h = 2 ** l
                    n = P // (2 * h)
                    for base, pattern, cm in ((0, [[-2 * h, n], [0, 2 * h]], 1),
                                              (h - 1, [[2 * h, n], [0, 2 * h]], -1),
                                              (-h, [[0, n], [1, 2 * h]], 0)):
                        pool.after(pool.done.now())
                        pool.do(G.affine_select(out=lvl[:, l, :], in_=lvl[:, l, :], compare_op=ALU.is_ge,
                                                fill=0.0, base=base, pattern=pattern, channel_multiplier=cm))

                l0, l1 = self.col("lb", 4), self.col("lb", 4, 4)
                m = dve.do(V.tensor_tensor(lb[:, 0], l0, l1, ALU.max))
                m0 = dve.after(m).do(V.tensor_tensor(lb[:, 1], l0, lb[:, 0], ALU.subtract))
                m1 = dve.after(m).do(V.tensor_tensor(lb[:, 2], l1, lb[:, 0], ALU.subtract))
                k = act.after(m1, m0).do(A.activation(lb[:, 1:3], lb[:, 1:3], ACT.Exp))
                m = dve.after(k).do(V.tensor_tensor(lb[:, 2], lb[:, 1], lb[:, 2], ALU.add))
                m = dve.after(m).do(V.reciprocal(lb[:, 2], lb[:, 2]))
                m = dve.after(m).do(V.tensor_tensor(lb[:, 0], lb[:, 1], lb[:, 2], ALU.mult))
                lb_done = dve.after(m).do(V.tensor_scalar(lb[:, 3], lb[:, 0], -1.0, 1.0, ALU.mult, ALU.add))

                x_T = self.to_T(self.x, self.hT)
                free = [x_T, x_T]
                proj = lambda j: (self.project_T if j in (0, 1, 3, 4) else self.project_nat)(
                    self.columns(w_in, j), self.hT, self.psB[j % 2], free[j % 2])
                out, done = proj(0)
                q_done = free[0] = act.after(done).do(A.activation(qT[:], out, ACT.Copy, scale=HD ** -0.5))
                out, done = proj(1)
                for half in range(2):
                    rows = slice(64 * half, 64 * half + 64)
                    k_done = free[1] = dve.after(done, z).do(V.tensor_copy(kTz[rows, half::2, :], out[rows]))
                done = proj(2)
                v_done = free[0] = act.after(done).do(A.activation(v_sb[:], self.psB[0][:], ACT.Copy))

                Z = self.psA
                Zc = Z[:, :, 0:3 * P]
                mb = mask[:].unsqueeze(1).to_broadcast([P, 4, 3 * P])

                def stick_scores(g, *ready):
                    pe.after(q_done, k_done, *ready)
                    for i in range(4):
                        h = 4 * g + i
                        M.matmul(Z[:, i, 0:T], kTz[:, h, 0:P], qT[:, h // 2, :], start=True, stop=True)
                        last = M.matmul(Z[:, i, T:3 * P], kTz[:, h, P:T], qT[:, h // 2, P:T],
                                        start=True, stop=True)
                    z_done = pe.do(last)
                    k = z_read = act.after(z_done, *ready).do(A.activation(sp[:], Zc, ACT.Abs))
                    k = act.after(k).do(A.activation(sp[:], sp[:], ACT.Exp, scale=-1.0))
                    k = act.after(k).do(A.activation(sp[:], sp[:], ACT.Ln, bias=1.0))
                    m = dve.after(k, z_read).do(V.scalar_tensor_tensor(sp[:], Zc, 0.0, sp[:], ALU.max, ALU.add))
                    lw_done = dve.after(m).do(V.tensor_tensor(lw[:], Zc, sp[:], ALU.subtract))
                    return dve.after(lw_done, masks).do(V.tensor_tensor(sp[:], sp[:], mb, ALU.mult))

                def stick_sums(ready):
                    pe.after(ready)
                    for i in range(4):
                        bank = Z[:, i, :]
                        M.matmul(bank[:, 0:T], self.after_[:], sp[:, i, 0:T], start=True, stop=False)
                        M.matmul(bank[:, P:T], self.ones[:], sp[:, i, T:], start=False, stop=True)
                        last = M.matmul(bank[:, T:3 * P], self.after_[:], sp[:, i, T:], start=True, stop=True)
                    return pe.do(last)

                def stick_weights(done):
                    m = dve.after(done).do(V.tensor_tensor(lw[:], lw[:], Zc, ALU.subtract))
                    k = act.after(m).do(A.activation(w[:], lw[:], ACT.Exp))
                    return dve.after(k).do(V.tensor_tensor(w[:], w[:], mb, ALU.mult))

                def stick_values(g, ready):
                    out, done = self.weighted_values(w, v_sb, range(4 * g, 4 * g + 4), Z, v_done, ready)
                    to = o_sb[:, :, 256 * g:256 * g + 256].rearrange("p t (h d) -> p h t d", d=HD)
                    return dve.after(done).do(V.tensor_copy(to, out))

                masks = pool.done.now()
                with ExitStack() as c3:
                    sp, lw, w = (self.sb(n, [P, 4, 3 * P], ctx=c3) for n in ("softplus", "log_w", "sb_w"))
                    m = stick_scores(0)
                    out, done = proj(3)
                    summed = stick_sums(m)
                    k = act.after(done).do(A.activation(hq[:], out, ACT.Sigmoid))
                    free[1] = dve.after(k).do(V.tensor_tensor(hq[:], hq[:], out, ALU.mult))
                    m = stick_weights(summed)
                    out, done = proj(4)
                    free[0] = k = act.after(done).do(A.activation(hk[:], out, ACT.Sigmoid))
                    values = stick_values(0, m)
                    z_ready = stick_scores(1, values)
                    bc = lambda i: lb[:, i, :].unsqueeze(2).to_broadcast([P, 4, T])
                    m = dve.after(k, lb_done).do(V.tensor_tensor(hk[:], hk[:], bc(3), ALU.mult))
                    f_done = dve.after(m).do(V.tensor_tensor(hb[:], hk[:], bc(0), ALU.add))
                    hk_done = dve.after(f_done).do(V.tensor_scalar(hk[:], hb[:], -1.0, 1.0, ALU.mult, ALU.add))
                    k = act.after(hk_done).do(A.activation(hb[:], hb[:], ACT.Ln))
                    done = proj(5)
                    summed = stick_sums(z_ready)
                    free[1] = hv_done = act.after(done).do(A.activation(hv[:], self.psB[1][:], ACT.Copy))
                    m = stick_weights(summed)
                    dve.after(k)
                    for h in range(HGH):
                        b_done = dve.do(V.tensor_tensor_scan(hb[:, h], keep[:], hb[:, h], 0.0, ALU.mult, ALU.add))
                    done = proj(6)
                    free[0] = act.after(done).do(A.activation(sig_g[:], self.psB[0][:], ACT.Sigmoid))
                    o_sb_done = stick_values(1, m)

                gate_free = [o_sb_done, o_sb_done]

                def gate_tiles():
                    for j in range(4):
                        (wj, arrived), ps = self.columns(w_in, 7 + j), self.psA[:, 2 * (j % 2):2 * (j % 2) + 2, :]
                        for tt in range(TT):
                            pe.after(arrived, gate_free[j % 2])
                            for k in range(KD):
                                last = M.matmul(ps[:, tt, :], self.hT[:, k, tt * P:(tt + 1) * P], wj[:, k, :],
                                                start=(k == 0), stop=(k == KD - 1))
                            if tt:
                                done = self.freed.add(last)
                                to = gates[:, j // 2, :, (j % 2) * 512:(j % 2) * 512 + 512]
                                gate_free[j % 2] = act.after(done).do(A.activation(to, ps, ACT.Copy))
                            yield

                gate_tile = gate_tiles()
                with ExitStack() as c3:
                    E = [self.sb("decay", [P, HGH, T], ctx=c3), kTz[:, 0:4, :]]
                    Q = [self.sb("q_decayed", [P, HGH, T], ctx=c3), qT]
                    K = [self.sb("k_decayed", [P, HGH, T], ctx=c3), kTz[:, 4:8, :]]
                    S = self.sb("hg_scores", [P, HGH * TT, P], ctx=c3)
                    X = self.sb("hg_cross", [P, HGH, P], ctx=c3)
                    st = self.sb("hg_stats", [P, 3, TT * HGH], ctx=c3)
                    blocks = lambda t, n: flat(t[:]).rearrange("p (n s) -> p n s", s=n)
                    LEVELS = 7
                    decayed, exps = {}, {}
                    scored = {-2: o_sb_done, -1: o_sb_done}
                    read = {-2: free[0], -1: free[1]}

                    def scores(ps, q, k_):
                        out = ps[:].rearrange("p a b -> p (a b)").rearrange("p (n t) -> p n t", t=P)
                        qv, kv = blocks(q, P), blocks(k_, P)
                        for n in range(HGH * TT):
                            last = M.matmul(out[:, n, :], kv[:, n, :], qv[:, n, :], start=True, stop=True)
                        return out, pe.do(last)

                    def decay(l):
                        e = E[l % 2]
                        dve.after(b_done, o_sb_done, *decayed.get(l - 2, ()))
                        if l < LEVELS:
                            h = 2 ** l
                            b2, e2 = blocks(hb, 2 * h), blocks(e, 2 * h)
                            mid = b2[:, :, h - 1:h].to_broadcast([P, HGH * T // (2 * h), 2 * h])
                            m = dve.do(V.tensor_tensor(e2, b2, mid, ALU.subtract))
                            k = act.after(m).do(A.activation(e[:], e[:], ACT.Abs))
                            exps[l] = act.after(k).do(A.activation(e[:], e[:], ACT.Exp, scale=-1.0))
                        else:
                            end = hb[:, :, P - 1:P].to_broadcast([P, HGH, P])
                            m0 = dve.do(V.tensor_tensor(e[:, :, 0:P], end, hb[:, :, 0:P], ALU.subtract))
                            m1 = dve.do(V.tensor_copy(e[:, :, P:], hb[:, :, P:]))
                            exps[l] = act.after(m0, m1).do(A.activation(e[:], e[:], ACT.Exp))

                    def decay_qk(l):
                        e, q, k_ = E[l % 2], Q[l % 2], K[l % 2]
                        qc, kc = (slice(P, T), slice(0, P)) if l == LEVELS else (slice(0, T), slice(0, T))
                        p = pool.after(exps[l], scored[l - 2]).do(
                            G.tensor_tensor(q[:, :, qc], hq[:, :, qc], e[:, :, qc], ALU.mult))
                        m = dve.after(exps[l], scored[l - 2]).do(
                            V.tensor_tensor(k_[:, :, kc], hk[:, :, kc], e[:, :, kc], ALU.mult))
                        decayed[l] = (p, m)

                    decay(0)
                    pe.after(read[-1], hk_done)
                    out, done = scores(self.psB[1], hq, hk)
                    next(gate_tile)
                    decay_qk(0)
                    decay(1)
                    s_done = read[-1] = dve.after(done).do(V.tensor_tensor(
                        S[:], out, self.ident[:].unsqueeze(1).to_broadcast([P, HGH * TT, P]), ALU.mult))
                    for l in range(LEVELS):
                        pe.after(*decayed[l], read[l - 2])
                        out, scored[l] = scores(self.psB[l % 2], Q[l % 2], K[l % 2])
                        next(gate_tile)
                        decay_qk(l + 1)
                        if l + 2 <= LEVELS:
                            decay(l + 2)
                        mk = lvl[:, l, :].bitcast(U32).unsqueeze(1).to_broadcast([P, HGH * TT, P])
                        s_done = read[l] = dve.after(scored[l], s_done).do(V.copy_predicated(S[:], mk, out))
                    next(gate_tile, None)
                    pe.after(*decayed[LEVELS], read[LEVELS - 2])
                    for h in range(HGH):
                        last = M.matmul(self.psB[1][:, 0, h * P:(h + 1) * P], K[1][:, h, 0:P], Q[1][:, h, P:],
                                        start=True, stop=True)
                    done = pe.do(last)
                    x_done = dve.after(done).do(V.tensor_copy(
                        X[:], self.psB[1][:, 0, :].rearrange("p (h t) -> p h t", t=P)))
                    oT = [t[:].rearrange("p a b -> p (a b)").rearrange("p (m t) -> p m t", t=T) for t in (v_sb, hv)]
                    out, done = self.transpose_to(o_sb, 0, 4, self.psB[0], s_done, o_sb_done)
                    sb_T = act.after(done).do(A.activation(oT[0], out, ACT.Copy))
                    pe.after(x_done, s_done, hv_done)
                    for h in range(HGH):
                        cols = slice(h * P, (h + 1) * P)
                        M.matmul(self.psB[1][:, 0, cols], S[:, 2 * h, :], hv[:, 0, cols], start=True, stop=True)
                        M.matmul(self.psB[1][:, 1, cols], X[:, h, :], hv[:, 0, cols], start=True, stop=False)
                        last = M.matmul(self.psB[1][:, 1, cols], S[:, 2 * h + 1, :], hv[:, 1, cols],
                                        start=False, stop=True)
                    done = pe.do(last)
                    branch_sb = self.accumulate_nat(self.rows(a["w_branch_sb_2"][0], 0), oT[0], True, True,
                                                    self.psA, sb_T, *gate_free)
                    k = act.after(done).do(A.activation(o_hg[:], self.psB[1][:], ACT.Copy))
                    sq = E[0][:].rearrange("p h t -> p (h t)").rearrange("p (t n) -> p t n", t=TT)
                    m = dve.after(k, *decayed[LEVELS - 1]).do(V.tensor_tensor(sq, o_hg[:], o_hg[:], ALU.mult))
                    m = dve.after(m).do(V.tensor_reduce(st[:, 0], sq.rearrange("p t (h d) -> p (t h) d", d=HGD),
                                                        axis=AX.X, op=ALU.add))
                    m = dve.after(m).do(V.tensor_scalar(st[:, 0], st[:, 0], 1.0 / HGD, EPS, ALU.mult, ALU.add))
                    r = self.rsqrt(st[:, 0], st[:, 1], st[:, 2], m)
                    g2 = lambda i: gates[:, i].rearrange("p t n -> p (t n)")
                    act.after(*gate_free)
                    sigmoids = [act.do(A.activation(g2(i), g2(i), ACT.Sigmoid)) for i in range(2)]
                    oh = o_hg[:].rearrange("p t (h d) -> p (t h) d", d=HGD)
                    m = dve.after(r).do(V.tensor_tensor(
                        oh, oh, st[:, 1].unsqueeze(2).to_broadcast([P, TT * HGH, HGD]), ALU.mult))
                    m = dve.after(m, self.late.now()).do(V.tensor_tensor(
                        o_hg[:], o_hg[:], gn[:].unsqueeze(1).to_broadcast([P, TT, HGW]), ALU.mult))
                    m = dve.after(m).do(V.tensor_tensor(o_hg[:], o_hg[:], sig_g[:], ALU.mult))
                    out, done = self.transpose_to(o_hg, 0, 4, self.psB[0], m, sb_T)
                    hg_T = act.after(done).do(A.activation(oT[1], out, ACT.Copy))
                    psf = flat(self.psA[:])
                    m = dve.after(branch_sb, *sigmoids).do(V.tensor_tensor(g2(0), g2(0), psf, ALU.mult))
                    done = self.accumulate_nat(self.rows(a["w_branch_hgrn_2"][0], 0), oT[1], True, True,
                                               self.psA, hg_T, m)
                    m1 = dve.after(done).do(V.tensor_tensor(g2(1), g2(1), psf, ALU.mult))
                    m = dve.after(m, m1).do(V.tensor_tensor(g2(0), g2(0), g2(1), ALU.add))
                    m = self.to_T(gates[:, 0], self.hT, m, hg_T)
                    for j in range(2):
                        done = self.accumulate_nat(self.rows(a["w_out_2"][0], j), self.hT[:, 4 * j:4 * j + 4, :],
                                                   j == 0, j == 1, self.psA, m, m1)
                    xf = flat(self.x[:])
                    dve.after(done).do(V.scalar_tensor_tensor(xf, xf, ALPHA, psf, ALU.mult, ALU.add))
                    self.join()

    def layer_norm(self, x, gain, bias, ctx, *ready):
        V, dve = self.nc.vector, self.dve
        bn = self.sb("bn_stats", [P, TT, 2, 6], ctx=ctx)
        mv = self.sb("mean_var", [P, TT, 2], ctx=ctx)
        w = self.sb("ln_work", [P, 3, TT], ctx=ctx)
        dve.after(*ready)
        for tt in range(TT):
            for h in range(2):
                dve.do(V.bn_stats(bn[:, tt, h, :], x[:, tt, h * 512:(h + 1) * 512]))
        dve.after(dve.done.now())
        for tt in range(TT):
            dve.do(V.bn_aggr(mv[:, tt, :], bn[:, tt]))
        m = dve.after(dve.done.now()).do(V.tensor_scalar(w[:, 0], mv[:, :, 1], LN_EPS, None, ALU.add))
        r = self.rsqrt(w[:, 0], w[:, 1], w[:, 2], m)
        dve.after(r)
        out = []
        for tt in range(TT):
            m = dve.do(V.tensor_scalar(x[:, tt, :], x[:, tt, :], mv[:, tt, 0:1], w[:, 1, tt:tt + 1],
                                       ALU.subtract, ALU.mult))
            m = dve.after(m).do(V.tensor_tensor(x[:, tt, :], x[:, tt, :], gain, ALU.mult))
            out.append(dve.after(m).do(V.tensor_tensor(x[:, tt, :], x[:, tt, :], bias, ALU.add)))
        return out


    def moe(self):
        nc, V, A, G, M = self.nc, self.nc.vector, self.nc.scalar, self.nc.gpsimd, self.nc.tensor
        pe, dve, act, pool = self.compute
        a, c = self.a, self.ctx
        sb = self.sb
        flat = lambda t: t.rearrange("p a b -> p (a b)")
        ln = sb("ln_params", [P, 4, D])
        acc = sb("moe_sum", [P, TT, D])
        cnt = sb("expert_counts", [1, NE], I32)
        slot = sb("slot_of_token", [P, TT, NE + 1])
        gate = sb("gate_of_token", [P, TT, NE + 1])
        brow = sb("b_up", [P, 2 * D])
        brow_of = sb("b_up_selector", [P, SLOTS])
        iota = sb("iota", [P, T])
        iota_ab = sb("iota_ab", [P, 2, P])
        ids = sb("slot_ids_ab", [P, 2, P])
        one_hot = sb("one_hot", [P, TT, P])
        weighted = sb("gated_one_hot", [P, 2, TT, P])
        scatter = sb("scatter_matrix", [P, 2, T])
        xg = sb("gathered_T", [P, KD, P])
        glu = sb("glu", [P, 512])
        lin = sb("linear", [P, 512])
        sig = sb("swish_gate", [P, 512])
        actT = sb("activated_T", [P, 4, P])
        y = sb("expert_out", [P, 512])
        U, AT, DN = self.psA[:, 0:2, :], self.psA[:, 2, :], self.psA[:, 3, :]
        X, S = self.psB[0], self.psB[1]
        Xg = X[:].rearrange("p a b -> p (a b)").rearrange("p (n s) -> p n s", s=P)

        for i, name in enumerate(("ln1_g_2", "ln1_b_2", "ln2_g_2", "ln2_b_2")):
            self.late.add(A.dma_start(ln[:, i, :], a[name][0].partition_broadcast(P)))
        with ExitStack() as c2:
            rw = sb("router_w", [P, KD, NE], ctx=c2)
            rb = sb("router_b", [P, NE], ctx=c2)
            bdown = sb("b_down", [P, D], ctx=c2)
            gT = sb("gate_T", [P, T], ctx=c2)
            logit = sb("logits", [P, TT, NE], ctx=c2)
            top = sb("top8", [P, TT, 8], ctx=c2)
            idx = sb("top8_index", [P, TT, 8], U32, ctx=c2)
            idxf = sb("top8_index_f", [P, TT, 8], ctx=c2)
            gts = sb("top4_gates", [P, TT, 2 * TOPK], ctx=c2)
            st = sb("router_stats", [P, TT, 2], ctx=c2)
            sel = sb("chosen", [P, TT, NE], ctx=c2)
            tmp = sb("one_choice", [P, TT, 2, NE], ctx=c2)
            z = [pool.do(G.memset(t, v)) for t, v in (
                (slot[:], -1.0), (gate[:], 0.0), (bdown[:], 0.0), (gT[:], 0.0), (scatter[:], 0.0), (y[:], 0.0), (brow[:], 0.0),
                (iota_ab[:], -1000.0))]
            pool.do(G.iota(iota[:], pattern=[[1, T]], base=0, channel_multiplier=0,
                           allow_small_or_imprecise_dtypes=True))
            pool.after(pool.done.now())
            for ab in range(2):
                pool.do(G.iota(iota_ab[:, ab, ab * SLOTS:(ab + 1) * SLOTS], pattern=[[1, SLOTS]], base=0,
                               channel_multiplier=0, allow_small_or_imprecise_dtypes=True))
            act.after(pool.done.now())
            self.late.add(A.dma_start(rw[:], a["router_w_2"][0].rearrange("(k p) n -> p k n", p=P)))
            self.late.add(A.dma_start(rb[:], a["router_b_2"][0].partition_broadcast(P)))
            self.late.add(A.dma_start(brow[0:NE, :], a["expert_b_up_2"][0]))
            self.late.add(A.dma_start(bdown[0:NE, :], a["expert_b_down_2"][0]))
            loaded = self.late.now()
            ln1 = self.layer_norm(self.x, ln[:, 0, :], ln[:, 1, :], c2, loaded, dve.done.now())
            hT = self.to_T(self.x, self.hT, *ln1)
            W = self.psA
            pe.after(hT, loaded)
            for tt in range(TT):
                for k in range(KD):
                    last = M.matmul(W[:, tt, 0:NE], self.hT[:, k, tt * P:(tt + 1) * P], rw[:, k, :],
                                    start=(k == 0), stop=(k == KD - 1))
            done = pe.do(last)
            m = dve.after(done, loaded).do(V.tensor_tensor(
                logit[:], W[:, 0:TT, 0:NE], rb[:].unsqueeze(1).to_broadcast([P, TT, NE]), ALU.add))
            dve.after(m)
            for tt in range(TT):
                m = dve.do(V.max(top[:, tt, :], logit[:, tt, :]))
                dve.after(m).do(V.max_index(idx[:, tt, :], top[:, tt, :], logit[:, tt, :]))
            dve.after(dve.done.now()).do(V.tensor_copy(idxf[:], idx[:]))
            m = dve.do(V.tensor_scalar(st[:, :, 0:1], top[:, :, 0:1], -1.0, None, ALU.mult))
            act.after(m)
            for tt in range(TT):
                k = act.do(A.activation(gts[:, tt, 0:TOPK], top[:, tt, 0:TOPK], ACT.Exp,
                                        bias=st[:, tt, 0:1], accum_out=st[:, tt, 1:2]))
            m = dve.after(k).do(V.reciprocal(st[:, :, 1:2], st[:, :, 1:2]))
            m = dve.after(m).do(V.tensor_tensor(gts[:, :, TOPK:], gts[:, :, 0:TOPK],
                                                st[:, :, 1:2].to_broadcast([P, TT, TOPK]), ALU.mult))
            dve.after(m, *z)
            for tt in range(TT):
                for j in range(TOPK):
                    one, gated = (sel[:, tt], gate[:, tt, 0:NE]) if j == 0 else (tmp[:, tt, 0], tmp[:, tt, 1])
                    pick = idxf[:, tt, j:j + 1]
                    dve.after(dve.done.now()).do(V.tensor_scalar(one, iota[:, 0:NE], pick, None, ALU.is_equal))
                    m = dve.do(V.tensor_scalar(gated, iota[:, 0:NE], pick, gts[:, tt, TOPK + j:TOPK + j + 1],
                                               ALU.is_equal, ALU.mult))
                    if j:
                        dve.after(m).do(V.tensor_tensor(sel[:, tt], sel[:, tt], one, ALU.add))
                        m = dve.do(V.tensor_tensor(gate[:, tt, 0:NE], gate[:, tt, 0:NE], gated, ALU.add))
            pe.after(m)
            M.matmul(W[:, 2, 0:NE], self.before[:], sel[:, 0], start=True, stop=True)
            M.matmul(W[:, 3, 0:NE], self.ones[:], sel[:, 0], start=True, stop=False)
            M.matmul(W[:, 3, 0:NE], self.before[:], sel[:, 1], start=False, stop=True)
            M.matmul(W[:, 0, 0:NE], self.ones[:], sel[:, 0], start=True, stop=False)
            last = M.matmul(W[:, 0, 0:NE], self.ones[:], sel[:, 1], start=False, stop=True)
            done = pe.do(last)
            m = dve.after(done).do(V.scalar_tensor_tensor(slot[:, :, 0:NE], W[:, 2:4, 0:NE], 1.0, sel[:],
                                                          ALU.add, ALU.mult))
            dve.after(m).do(V.tensor_scalar(slot[:, :, 0:NE], slot[:, :, 0:NE], -1.0, None, ALU.add))
            counted = dve.do(V.tensor_copy(cnt[:], W[0:1, 0, 0:NE]))
            pe.after(m, *ln1)
            for tt in range(TT):
                last = M.transpose(S[0:NE, 0, tt * P:(tt + 1) * P], gate[:, tt, 0:NE], self.ident[:])
            done = pe.do(last)
            m = dve.after(done, *z).do(V.tensor_copy(gT[0:NE, :], S[0:NE, 0, 0:T]))
            pe.after(m, dve.done.now(), loaded)
            for tt in range(TT):
                for half in range(2):
                    last = M.matmul(W[:, 2 * tt + half, :], gT[:, tt * P:(tt + 1) * P],
                                    bdown[:, half * 512:(half + 1) * 512], start=True, stop=True)
            done = pe.do(last)
            m = dve.after(done).do(V.scalar_tensor_tensor(flat(acc[:]), flat(self.x[:]), ALPHA, flat(W[:]),
                                                          ALU.mult, ALU.add))
            self.join()

        sem = lambda name: Count(self.sem(name))
        selected, built, gated = sem("bias_row_selected"), sem("one_hot_built"), sem("gated_one_hot_built")
        gathered, gather_copied = sem("x_gathered"), sem("gathered_copied")
        up_done, hidden_read, activated = sem("up_products_done"), sem("up_products_read"), sem("activated")
        act_T, act_copied = sem("activated_transposed"), sem("activated_copied")
        down_done, y_copied = sem("down_products_done"), sem("out_copied")
        weighted_T, scatter_copied = sem("gated_transposed"), sem("scatter_matrix_copied")
        scattered, summed = sem("scattered_tiles"), sem("summed_tiles")
        px, dx, ax = (Engine(e.engine, self.sem(n)) for e, n in (
            (pe, "extra_pe"), (dve, "extra_dve"), (act, "extra_act")))
        xg_x = sb("extra_gathered_T", [P, KD, P])
        scatter_x = sb("extra_scatter_matrix", [P, 2, T])
        y_x = sb("extra_out", [P, 512])

        w_up, w_down = a["expert_w_up_2"][0], a["expert_w_down_2"][0]
        order = [4, 5] + [(self.panels + r) % RING for r in range(RING)]
        panel = [self.ring[:, s, :].rearrange("p (k n) -> p k n", k=2 if j < 4 else 4)
                 for j, s in enumerate(order)]

        def sources(e):
            for j in range(4):
                yield w_up[bass.ds(e, 1), j * 256:(j + 1) * 256, :].rearrange("o (k p) n -> p (o k) n", p=P)
            for j in range(2):
                yield w_down[bass.ds(e, 1), j * 512:(j + 1) * 512, :].rearrange("o (k p) n -> p (o k) n", p=P)

        def choose(e, numbers, out, factor, count):
            for tt in range(TT):
                last = V.tensor_scalar(out[:, tt, :], numbers, slot[:, tt, bass.ds(e, 1)],
                                       gate[:, tt, bass.ds(e, 1)] if factor else None, ALU.is_equal,
                                       **({"op1": ALU.mult} if factor else {}))
                mark = count.add(last)
            return mark

        def select_bias(e):
            return V.tensor_scalar(brow_of[:], self.ones[:, 0:SLOTS], self.ident[:, bass.ds(e, 1)], None, ALU.mult)

        def gather():
            for k in range(KD):
                for tt in range(TT):
                    last = M.matmul(Xg[:, k, :], self.x[:, tt, k * P:(k + 1) * P], one_hot[:, tt, :],
                                    start=(tt == 0), stop=(tt == TT - 1))
            return last

        def halves(ps, lhsT, rhs, **flags):
            M.matmul(ps[0:SLOTS], lhsT, rhs[0], **flags)
            return M.matmul(ps[SLOTS:P], lhsT, rhs[1], **flags)

        def up(inp, arrived, free):
            for q in range(2):
                halves(U[:, q, :], brow_of[:], [brow[:, c:c + 512] for c in (512 * q, D + 512 * q)],
                       start=True, stop=False)
            for j in range(4):
                pe.after(arrived(j))
                for r in range(2):
                    for q in range(2):
                        last = halves(U[:, q, :], inp[:, 2 * j + r, 0:SLOTS],
                                      [panel[j][:, r, c:c + 512] for c in (512 * q, D + 512 * q)],
                                      start=False, stop=(j == 3 and r == 1))
                if free and j < 3:
                    free.add(last)
            return last

        def activate(d, s, ready, read, tiles):
            even, odd = (U.rearrange("p a b -> p (a b)")[:, i::2] for i in range(2))
            d.after(ready)
            m1 = d.do(V.tensor_scalar(glu[:], even, SWIGLU_LIMIT, None, ALU.min))
            k = s.after(m1).do(A.activation(sig[:], glu[:], ACT.Sigmoid, scale=SWIGLU_ALPHA))
            m2 = read.add(V.tensor_scalar(lin[:], odd, -SWIGLU_LIMIT, SWIGLU_LIMIT, ALU.max, ALU.min))
            m3 = d.after(m2).do(V.scalar_tensor_tensor(lin[:], lin[:], 1.0, glu[:], ALU.add, ALU.mult))
            d.after(m3, k)
            return tiles.add(V.tensor_tensor(glu[:], lin[:], sig[:], ALU.mult))

        def transpose_activated(after_first=None):
            for n in range(4):
                last = M.transpose(AT[:, n * P:(n + 1) * P], glu[:, n * P:(n + 1) * P], self.ident[:])
                if n == 0 and after_first:
                    after_first.add(last)
            return last

        def down(arrived, free):
            for j in range(2):
                pe.after(arrived(j))
                for r in range(4):
                    k = 4 * j + r
                    last = halves(DN, actT[:, r, j * SLOTS:(j + 1) * SLOTS],
                                  [panel[4 + j][:, r, c:c + 512] for c in (0, 512)],
                                  start=(k == 0), stop=(k == KD - 1))
                if free and j == 0:
                    free.add(last)
            return last

        def transpose_weighted(after_first=None):
            for ab in range(2):
                for tt in range(TT):
                    c = (2 * ab + tt) * P
                    last = M.transpose(AT[:, c:c + P], weighted[:, ab, tt, :], self.ident[:])
                    if ab == tt == 0 and after_first:
                        after_first.add(last)
            return last

        def scatter_tile(tt, matrix, rows):
            for ab in range(2):
                last = M.matmul((S, X)[tt][:, ab, :], matrix[:, ab, tt * P:(tt + 1) * P], rows[:],
                                start=True, stop=True)
            return last

        def add_tile(tt):
            return V.tensor_tensor(acc[:, tt, :], acc[:, tt, :],
                                   (S, X)[tt][:].rearrange("p a b -> p (a b)"), ALU.add)

        at4 = AT.rearrange("p (n s) -> p n s", s=P)
        at2 = AT.rearrange("p (a t) -> p a t", t=T)

        for eng, counts in ((pe, (gathered, up_done, act_T, down_done, weighted_T, scattered)),
                            (act, (gather_copied, act_copied, y_copied, scatter_copied)),
                            (dve, (selected, hidden_read, activated, summed, built, gated))):
            for n in counts:
                eng.engine.sem_inc(n.sem, 1)
                n.n += 1
        selected.add(select_bias(0))
        m = choose(0, iota[:, 0:P], one_hot, False, built)
        pe.after(m)
        m = gathered.add(gather())
        act.after(m)
        m = gather_copied.add(A.activation(xg[:], Xg[:], ACT.Copy))

        shares = {self.freed: 6, dve.done: 2, act.done: 1, gathered: 1, gather_copied: 1, up_done: 1,
                  selected: 1, hidden_read: 1, activated: 1, act_T: 1, act_copied: 1, down_done: 1,
                  y_copied: 1, weighted_T: 1, scatter_copied: 1, scattered: 2, summed: 2, built: 2, gated: 4,
                  px.done: 21, dx.done: 45, ax.done: 15, **{self.arrived[s]: 1 for s in order}}
        named = [n for n in shares if n not in (px.done, dx.done, ax.done, self.freed)]
        with Loop(nc, NE, shares) as e:
            marks = []
            for j, src in enumerate(sources(e)):
                self.sp.after((self.freed, self.freed.n - 5 + j, self.freed.loop))
                self.sp.settle(self.settled)
                marks.append(self.arrived[order[j]].add(nc.sync.dma_start(panel[j], src)))
            tokens = nc.values_load(cnt[0:1, bass.ds(e, 1)], min_val=0, max_val=T,
                                    engines=[x.engine.engine for x in (pe, dve, act)])
            dve.after(*(n.before_iteration() for n in (dve.done, selected, built, gated, hidden_read,
                                                       activated, summed, gathered)))
            m_built = choose(e + 1, iota[:, 0:P], one_hot, False, built)
            dve.after(weighted_T.before_iteration())
            for ab in range(2):
                m_gated = choose(e, iota_ab[:, ab, :], weighted[:, ab], True, gated)

            def dense_part(free):
                pe.after(gather_copied.before_iteration(), hidden_read.before_iteration(),
                         selected.before_iteration())
                m = {"up": up_done.add(up(xg, lambda j: marks[j], free))}
                pe.after(m_built, summed.before_iteration())
                m["gather"] = gathered.add(gather())
                pe.after(y_copied.before_iteration(), scatter_copied.before_iteration())
                m["s0"] = scattered.add(scatter_tile(0, scatter, y))
                pe.after((activated, activated.n + 1, activated.loop))
                m["act"] = act_T.add(transpose_activated(free))
                pe.after((gather_copied, gather_copied.n + 1, gather_copied.loop))
                m["s1"] = scattered.add(scatter_tile(1, scatter, y))
                pe.after((act_copied, act_copied.n + 1, act_copied.loop))
                m["down"] = down_done.add(down(lambda j: marks[4 + j], free))
                pe.after(m_gated)
                m["weighted"] = weighted_T.add(transpose_weighted(free))
                return m

            counts = (self.freed, up_done, gathered, scattered, act_T, down_done, weighted_T)
            state, waited = [n.n for n in counts], dict(pe.waited)
            with nc.tensor.If(tokens < SLOTS + 1):
                m = dense_part(self.freed)
            for n, v in zip(counts, state):
                n.n = v
            pe.waited = waited
            with nc.tensor.Else():
                m = dense_part(None)
            self.freed.n = state[0] + 6
            dve.after(act_T.before_iteration())
            activate(dve, act, m["up"], hidden_read, activated)
            selected.add(select_bias(e + 1))
            act.after(m["gather"], m["up"])
            gather_copied.add(A.activation(xg[:], Xg[:], ACT.Copy))
            act.after(m["act"], down_done.before_iteration())
            act_copied.add(A.activation(actT[:], at4, ACT.Copy))
            for tt in range(TT):
                dve.after(m[f"s{tt}"])
                summed.add(add_tile(tt))
            act.after(m["down"], m["s1"])
            y_copied.add(A.activation(y[:], DN, ACT.Copy))
            act.after(m["weighted"])
            scatter_copied.add(A.activation(scatter[:], at2, ACT.Copy))

            def extra_pass(base):
                m = dx.do(V.tensor_scalar(ids[:], iota_ab[:], float(base), None, ALU.add))
                m = choose(e, iota[:, base:base + SLOTS], one_hot[:, :, 0:SLOTS], False, dx.done)
                m = px.after(m).do(gather())
                m = ax.after(m).do(A.activation(xg_x[:], Xg[:], ACT.Copy))
                px.after(dx.after(px.done.now()).do(select_bias(e)), m)
                m = px.do(up(xg_x, lambda j: None, None))
                m = activate(dx, ax, m, dx.done, dx.done)
                m = px.after(m).do(transpose_activated())
                m = ax.after(m).do(A.activation(actT[:], at4, ACT.Copy))
                px.after(m)
                m = px.do(down(lambda j: None, None))
                ax.after(m).do(A.activation(y_x[:], DN, ACT.Copy))
                dx.after(px.done.now(), dx.done.now())
                dx.do(select_bias(e + 1))
                for ab in range(2):
                    m = choose(e, ids[:, ab, :], weighted[:, ab], True, dx.done)
                m = px.after(m, ax.done.now()).do(transpose_weighted())
                m = ax.after(m).do(A.activation(scatter_x[:], at2, ACT.Copy))
                px.after(m, ax.done.now())
                for tt in range(TT):
                    m = px.do(scatter_tile(tt, scatter_x, y_x))
                    dx.after(m).do(add_tile(tt))

            over = (pe, dve, act)
            lines = (px, dx, ax)

            def passes(bases, condition, entry, last):
                kept = [dict(eng.waited) for eng in over + lines]
                start = [x.done.n for x in lines]
                branch = nc.If(condition)
                branch.__enter__()
                for eng in over:
                    eng.after(*entry)
                for eng, x in zip(over, lines):
                    x.waited = eng.waited
                for base in bases:
                    extra_pass(base)
                for eng in over:
                    eng.after(*(x.done.now() for x in lines))
                    eng.settle(self.settled)
                branch.__exit__(None, None, None)
                with nc.Else():
                    for eng, x, n in zip(over, lines, start):
                        eng.engine.sem_inc(x.done.sem, x.done.n - n)
                for eng, waited in zip(over + lines, kept):
                    eng.waited = waited

            entry = [n.now() for n in named]
            passes((SLOTS,), tokens > SLOTS, entry, False)
            passes((2 * SLOTS, 3 * SLOTS), tokens > 2 * SLOTS, [x.done.now() for x in lines] + entry, True)
            with nc.tensor.If(tokens > SLOTS):
                nc.tensor.sem_inc(self.freed.sem, 6)

        pe.after(y_copied.now(), scatter_copied.now(), gather_copied.now(), summed.now())
        s0 = scattered.add(scatter_tile(0, scatter, y))
        s1 = scattered.add(scatter_tile(1, scatter, y))
        dve.after(s0, summed.now())
        summed.add(add_tile(0))
        dve.after(s1)
        m = summed.add(add_tile(1))
        out = self.layer_norm(acc, ln[:, 2, :], ln[:, 3, :], c, m)
        for tt in range(TT):
            self.sp.after(out[tt])
            self.stored.add(nc.sync.dma_start(self.out[0, tt * P:(tt + 1) * P, :], acc[:, tt, :]))
        self.sp.after(self.stored.now())


def build(nc, ctx, arrays, out):
    k = Kernel(nc, ctx, arrays, out)
    k.setup()
    k.griffin()
    k.mlp(0)
    k.fox()
    k.mlp(1)
    k.hybrid()
    k.moe()


_INS = [
    "x", "mix_norm", "mlp_norm", "mlp_w1", "mlp_w2", "lru_w_in", "lru_conv_w", "lru_conv_b", "lru_w_r",
    "lru_b_r", "lru_w_i", "lru_b_i", "lru_lambda", "lru_w_out", "fox_w_in", "fox_b_f", "fox_q_gain",
    "fox_k_gain", "fox_w_out", "w_in_2", "hgrn_lb_logits_2", "hgrn_norm_g_2", "w_branch_sb_2",
    "w_branch_hgrn_2", "w_out_2", "ln1_g_2", "ln1_b_2", "router_w_2", "router_b_2", "expert_w_up_2",
    "expert_b_up_2", "expert_w_down_2", "expert_b_down_2", "ln2_g_2", "ln2_b_2",
]


def kernel(**inputs):
    import concourse.bacc as _bacc
    import numpy as _np
    from concourse.bass_utils import run_bass_kernel_spmd as _run

    nc = _bacc.Bacc("TRN2", target_bir_lowering=False, num_devices=1)
    arrays, aps = {}, {}
    for name in _INS:
        a = _np.ascontiguousarray(inputs[name])
        arrays[f"in_{name}"] = a
        aps[name] = nc.dram_tensor(f"in_{name}", a.shape, mybir.dt.from_np(a.dtype), kind="ExternalInput").ap()
    out = nc.dram_tensor("out_x", (1, T, D), F32, kind="ExternalOutput").ap()
    with ExitStack() as ctx:
        build(nc, ctx, aps, out)
    r = _run(nc, [arrays], core_ids=[0])
    return r.results[0]["out_x"]
```

```python
from contextlib import ExitStack

import concourse.bass as bass
import concourse.mybir as mybir

F32 = mybir.dt.float32
F32R = mybir.dt.float32r
I32 = mybir.dt.int32
U32 = mybir.dt.uint32
ALU = mybir.AluOpType
ACT = mybir.ActivationFunctionType
AX = mybir.AxisListType

P = 128
T = 256
TT = T // P
D = 1024
KD = D // P
NH, HD = 16, 64
SBH, SBW = 8, 512
HGH, HGD, HGW = 4, 128, 512
NE, TOPK = 32, 4
SLOTS = 64
RING = 4
XRING = 6
PANEL = 4096
EPS = 1e-6
LN_EPS = 1e-5
NEG = -1e30
KEEP12 = -4096
ALPHA = 2.0 ** 0.25
SWIGLU_ALPHA, SWIGLU_LIMIT = 1.702, 7.0


class Count:

    def __init__(self, sem, step=1):
        self.sem, self.step, self.n, self.loop = sem, step, 0, None

    def add(self, instruction):
        instruction.then_inc(self.sem, self.step)
        self.n += 1
        return self.now()

    def now(self):
        return (self, self.n, self.loop)

    def before_iteration(self, but=0):
        return (self, self.loop[2] - but, self.loop)


class Engine:

    def __init__(self, engine, sem):
        self.engine, self.done = engine, Count(sem) if sem is not None else None
        self.waited = {}

    def after(self, *marks):
        for mark in marks:
            if mark is None:
                continue
            count, n, loop = mark
            if n <= self.waited.get((count, loop), 0 if loop is None else -RING * 16):
                continue
            assert loop is None or loop is count.loop, "a mark of a loop is used outside of it"
            self.waited[count, loop] = n
            value = n * count.step
            if loop is not None:
                value = value + loop[0] * (loop[1] * count.step)
            self.engine.wait_ge(count.sem, value)
        return self

    def do(self, instruction):
        return self.done.add(instruction)

    def settle(self, sem):
        self.engine.sem_inc(sem, 1)


class Share(tuple):

    __hash__ = object.__hash__

    def __eq__(self, other):
        return self is other


class Loop:

    def __init__(self, nc, trips, shares):
        self.nc, self.trips, self.shares = nc, trips, shares

    def __enter__(self):
        self.fori = self.nc.Fori(0, self.trips)
        i = self.fori.__enter__()
        for count, share in self.shares.items():
            count.loop = Share((i, share, count.n))
        return i

    def __exit__(self, *exc):
        if exc[0] is None:
            for count, share in self.shares.items():
                grown = count.n - count.loop[2]
                assert grown == share, f"{count.sem}: {grown} in an iteration, {share} stated"
                count.n = count.loop[2] + self.trips * share
                count.loop = None
        return self.fori.__exit__(*exc)


class Kernel:
    def __init__(self, nc, ctx, a, out):
        self.nc, self.ctx, self.a, self.out = nc, ctx, a, out
        sem = lambda name: ctx.enter_context(nc.semaphore(name))
        self.sem, self.made = sem, 0
        self.pe = Engine(nc.tensor, sem("pe_done"))
        self.dve = Engine(nc.vector, sem("dve_done"))
        self.act = Engine(nc.scalar, sem("act_done"))
        self.pool = Engine(nc.gpsimd, sem("pool_done"))
        self.sp = Engine(nc.sync, None)
        self.compute = (self.pe, self.dve, self.act, self.pool)
        self.arrived = [Count(sem(f"panel_in_slot{s}"), 16) for s in range(XRING)]
        self.freed = Count(sem("panels_consumed"))
        self.low_parts = Count(sem("low_parts_split"))
        self.small = Count(sem("small_loads"), 16)
        self.late = Count(sem("late_loads"), 16)
        self.stored = Count(sem("stored"), 16)
        self.settled = sem("waits_settled")
        self.panels = 0
        self.ring = self.sb("panel_ring", [P, XRING, PANEL])
        self.psA = self.ps("psA", [P, 4, 512])
        self.psB = [self.ps(f"psB{j}", [P, 2, 512]) for j in range(2)]
        self.x = self.sb("x", [P, TT, D])
        self.hT = self.sb("hT", [P, KD, T])
        self.rms_stats = self.sb("rms_stats", [P, 4, TT])
        self.x_ready, self.tiles_apart = [None, None], False

    def sb(self, name, shape, dt=F32, ctx=None):
        self.made = self.made + 1
        return (ctx or self.ctx).enter_context(self.nc.sbuf_tensor(f"{name}_{self.made}", shape, dt))

    def ps(self, name, shape, dt=F32):
        return self.ctx.enter_context(self.nc.psum_tensor(name, shape, dt))

    def join(self):
        for e in self.compute:
            for other in self.compute:
                e.after(other.done.now())
            e.after(self.freed.now())


    def load_panel(self, source, parts):
        slot = self.panels % RING
        self.panels += 1
        view = self.ring[:, slot, :].rearrange("p (k n) -> p k n", k=parts)
        count, n, loop = self.freed, self.panels - RING, self.freed.loop
        self.sp.after((count, n, loop))
        if loop is not None:
            self.sp.settle(self.settled)
        mark = self.arrived[slot].add(self.nc.sync.dma_start(view, source))
        return view, mark

    def columns(self, w, j, dynamic=False):
        at = bass.ds(j * 512, 512) if dynamic else slice(j * 512, (j + 1) * 512)
        return self.load_panel(w[:, at].rearrange("(k p) n -> p k n", p=P), KD)

    def rows(self, w, j, dynamic=False):
        at = bass.ds(j * 512, 512) if dynamic else slice(j * 512, (j + 1) * 512)
        return self.load_panel(w[at, :].rearrange("(k p) n -> p k n", p=P), 4)

    def project_T(self, panel, hT, ps, *ready):
        w, arrived = panel
        self.pe.after(arrived, *ready)
        out = ps[:].rearrange("p a b -> p (a b)").rearrange("p (m t) -> p m t", t=T)
        for m in range(4):
            for k in range(KD):
                last = self.nc.tensor.matmul(out[:, m, :], w[:, k, m * P:(m + 1) * P], hT[:, k, :],
                                             start=(k == 0), stop=(k == KD - 1))
        return out, self.freed.add(last)

    def project_nat(self, panel, hT, ps, *ready):
        w, arrived = panel
        self.pe.after(arrived, *ready)
        for tt in range(TT):
            for k in range(KD):
                last = self.nc.tensor.matmul(ps[:, tt, :], hT[:, k, tt * P:(tt + 1) * P], w[:, k, :],
                                             start=(k == 0), stop=(k == KD - 1))
        return self.freed.add(last)

    def accumulate_nat(self, panel, aT, first, last, ps, *ready):
        w, arrived = panel
        self.pe.after(arrived, *ready)
        steps = [(k, tt) for k in range(4) for tt in range(TT)]
        if last:
            steps.sort(key=lambda step: step[1])
        for k, tt in steps:
            for half in range(2):
                mm = self.nc.tensor.matmul(ps[:, 2 * tt + half, :], aT[:, k, tt * P:(tt + 1) * P],
                                           w[:, k, half * 512:(half + 1) * 512],
                                           start=first and k == 0, stop=last and k == 3)
            if last and (k, tt) == (3, 0):
                first_tile = self.pe.do(mm)
        done = self.freed.add(mm)
        return (first_tile, done) if last else done


    def transpose_to(self, src, j0, n, ps, *ready):
        self.pe.after(*ready)
        out = ps[:].rearrange("p a b -> p (a b)").rearrange("p (m t) -> p m t", t=T)
        for m in range(n):
            for tt in range(TT):
                last = self.nc.tensor.transpose(out[:, m, tt * P:(tt + 1) * P],
                                                src[:, tt, (j0 + m) * P:(j0 + m + 1) * P], self.ident[:])
        return out, self.pe.do(last)

    def to_T(self, src, dst, *ready, scale=None):
        n, V = src.shape[2] // P, self.nc.vector
        marks = [None, None]
        for g in range((n + 3) // 4):
            m = min(4, n - 4 * g)
            out, done = self.transpose_to(src, 4 * g, m, self.psB[g % 2], *ready, marks[g % 2])
            to = dst[:, 4 * g:4 * g + m, :]
            self.dve.after(done)
            if scale is None:
                marks[g % 2] = self.dve.do(V.tensor_copy(to, out[:, 0:m, :]))
            else:
                s = scale[:, 4 * g:4 * g + m].unsqueeze(2).to_broadcast([P, m, T])
                marks[g % 2] = self.dve.do(V.tensor_tensor(to, out[:, 0:m, :], s, ALU.mult))
        return self.dve.done.now()

    def rsqrt(self, ms, y, t, *ready):
        a = self.act.after(*ready).do(self.nc.scalar.activation(y, ms, ACT.Sqrt))
        a = self.dve.after(a).do(self.nc.vector.reciprocal(y, y))
        return self.newton_rsqrt(ms, y, t, a)

    def newton_rsqrt(self, ms, y, t, ready):
        V, dve = self.nc.vector, self.dve
        m = dve.after(ready).do(V.tensor_tensor(t, y, y, ALU.mult))
        m = dve.after(m).do(V.tensor_tensor(t, t, ms, ALU.mult))
        m = dve.after(m).do(V.tensor_scalar(t, t, -0.5, 1.5, ALU.mult, ALU.add))
        return dve.after(m).do(V.tensor_tensor(y, y, t, ALU.mult))

    def rms_to_hT(self, gain):
        V, dve, act = self.nc.vector, self.dve, self.act
        xn = self.ring[:, RING, 0:TT * D].rearrange("p (t n) -> p t n", t=TT)
        st = self.rms_stats
        written = []
        both = slice(0, TT)
        for tiles in ([slice(0, 1), slice(1, 2)] if self.tiles_apart else [both]):
            for tt in range(TT)[tiles]:
                m = act.after(self.x_ready[tt]).do(self.nc.scalar.activation(
                    xn[:, tt, :], self.x[:, tt, :], ACT.Square, accum_out=st[:, 0, tt:tt + 1]))
            m = dve.after(act.done.now()).do(
                V.tensor_scalar(st[:, 1, tiles], st[:, 0, tiles], 1.0 / D, EPS, ALU.mult, ALU.add))
            r = self.rsqrt(st[:, 1, tiles], st[:, 2, tiles], st[:, 3, tiles], m)
            normed = [dve.after(r, self.x_ready[tt]).do(V.tensor_scalar(
                xn[:, tt, :], self.x[:, tt, :], st[:, 2, tt:tt + 1], None, ALU.mult)) for tt in range(TT)[tiles]]
            for tt, m in zip(range(TT)[tiles], normed):
                ps = self.psB[tt][:].rearrange("p a b -> p (a b)").rearrange("p (k t) -> p k t", t=P)
                self.pe.after(m)
                for k in range(KD):
                    last = self.nc.tensor.transpose(ps[:, k, :], xn[:, tt, k * P:(k + 1) * P], self.ident[:])
                written.append(dve.after(self.pe.do(last), self.freed.now()).do(V.tensor_tensor(
                    self.hT[:, :, tt * P:(tt + 1) * P], ps, gain.unsqueeze(2).to_broadcast([P, KD, P]), ALU.mult)))
        self.join()


    def setup(self):
        nc, G, pool = self.nc, self.nc.gpsimd, self.pool
        a = self.a
        for tt in range(TT):
            self.small.add(nc.scalar.dma_start(self.x[:, tt, :], a["x"][0, tt * P:(tt + 1) * P, :]))
        rows = self.sb("param_rows", [P, P])
        pool.do(G.memset(rows[:], 0.0))
        at, self.col_of = 0, {}
        nc.scalar.wait_ge(self.pool.done.sem, 1)

        def put(name, src, n):
            nonlocal at
            self.small.add(nc.scalar.dma_start(rows[at:at + n, :], src))
            self.col_of[name] = at
            at += n

        put("mix", a["mix_norm"].rearrange("l (c p) -> (l c) p", p=P), 16)
        put("mlp", a["mlp_norm"].rearrange("l (c p) -> (l c) p", p=P), 16)
        put("conv_w", a["lru_conv_w"][0].rearrange("l (c p) -> (l c) p", p=P), 32)
        put("conv_b", a["lru_conv_b"][0].rearrange("(c p) -> c p", p=P), 8)
        put("b_r", a["lru_b_r"][0].rearrange("(c n) p -> c (n p)", n=2), 8)
        put("b_i", a["lru_b_i"][0].rearrange("(c n) p -> c (n p)", n=2), 8)
        put("lam", a["lru_lambda"][0].rearrange("(c p) -> c p", p=P), 8)
        put("lb", a["hgrn_lb_logits_2"].rearrange("l (c p) -> (l c) p", p=P), 8)
        for name in ("q_gain", "k_gain"):
            for half in range(2):
                self.small.add(nc.scalar.dma_start(rows[at:at + 1, half * HD:(half + 1) * HD],
                                                   a["fox_" + name]))
            self.col_of[name] = at
            at += 1
        self.sp.after(self.small.now())
        self.ident = self.sb("ident", [P, P])
        self.ones = self.sb("ones", [P, P])
        self.before = self.sb("before", [P, P])
        self.after_ = self.sb("after_", [P, P])
        m0 = pool.do(G.memset(self.ident[:], 0.0))
        m1 = pool.do(G.memset(self.ones[:], 1.0))
        pool.after(m0).do(G.affine_select(out=self.ident[:], in_=self.ident[:], compare_op=ALU.not_equal,
                                          fill=1.0, base=0, pattern=[[-1, P]], channel_multiplier=1))
        pool.after(m1).do(G.affine_select(out=self.before[:], in_=self.ones[:], compare_op=ALU.is_gt,
                                          fill=0.0, base=0, pattern=[[1, P]], channel_multiplier=-1))
        pool.do(G.affine_select(out=self.after_[:], in_=self.ones[:], compare_op=ALU.is_gt,
                                fill=0.0, base=0, pattern=[[-1, P]], channel_multiplier=1))
        self.cols = self.sb("param_cols", [P, P])
        self.pe.after(pool.done.now(), self.small.now())
        t = self.pe.do(nc.tensor.transpose(self.psB[0][:, 0, 0:P], rows[:], self.ident[:]))
        self.dve.after(t).do(nc.vector.tensor_copy(self.cols[:], self.psB[0][:, 0, 0:P]))
        for e in self.compute:
            e.after(self.small.now())
        self.join()

    def col(self, name, n, skip=0):
        at = self.col_of[name] + skip
        return self.cols[:, at:at + n]


    def griffin(self):
        nc, V, A, G = self.nc, self.nc.vector, self.nc.scalar, self.nc.gpsimd
        pe, dve, act, pool = self.compute
        a = self.a
        self.rms_to_hT(self.col("mix", KD))
        with ExitStack() as c:
            sb = lambda n, s: self.sb(n, s, ctx=c)
            gate = sb("gate", [P, KD, T])
            xpad = sb("x_branch", [P, KD, T + 3])
            xc = sb("x_conv", [P, KD, T])
            wri = sb("w_ri", [P, 2, KD, P])
            ra = sb("r_then_a", [P, KD, T])
            ib = sb("i_then_b", [P, KD, T])
            th = sb("tanh_then_h", [P, KD, T])
            lam = sb("lam_work", [P, 5, KD])
            z0 = pool.do(G.memset(wri[:], 0.0))
            z1 = pool.do(G.memset(xpad[:, :, 0:3], 0.0))
            act.after(z0)
            for n, name in enumerate(("lru_w_r", "lru_w_i")):
                w = a[name][0].rearrange("(c n) d e -> d n c e", n=2)
                for half in range(2):
                    self.late.add(A.dma_start(wri[half * 64:half * 64 + 64, n, :, half * 64:half * 64 + 64],
                                              w[:, half, :, :]))
            u, s, s2, acc, ls = (lam[:, i, :] for i in range(5))
            L = self.col("lam", KD)
            k = act.do(A.activation(u, L, ACT.Abs))
            k = act.after(k).do(A.activation(u, u, ACT.Exp, scale=-1.0))
            m = dve.after(k).do(V.tensor_scalar(s2, u, 2.0, None, ALU.add))
            m = dve.after(m).do(V.reciprocal(s, s2))
            m = dve.after(m).do(V.tensor_tensor(s, s, u, ALU.mult))
            m = dve.after(m).do(V.tensor_tensor(s2, s, s, ALU.mult))
            m = dve.after(m).do(V.tensor_scalar(acc, s2, 2.0 / 17, 2.0 / 15, ALU.mult, ALU.add))
            for odd in (13, 11, 9, 7, 5, 3, 1):
                m = dve.after(m).do(V.tensor_tensor(acc, acc, s2, ALU.mult))
                m = dve.after(m).do(V.tensor_scalar(acc, acc, 2.0 / odd, None, ALU.add))
            m = dve.after(m).do(V.tensor_tensor(acc, acc, s, ALU.mult))
            m = dve.after(m).do(V.tensor_scalar(ls, L, 0.0, None, ALU.min))
            m = dve.after(m).do(V.tensor_tensor(ls, ls, acc, ALU.subtract))
            c8 = dve.after(m).do(V.tensor_scalar(ls, ls, 8.0, None, ALU.mult))

            w_in = a["lru_w_in"][0]
            free = [None, None]
            c8b = ls.unsqueeze(2).to_broadcast([P, KD, T])
            r_ps = self.psA[:, 0:2, :].rearrange("p a (b t) -> p (a b) t", t=T)
            i_ps = self.psA[:, 2:4, :].rearrange("p a (b t) -> p (a b) t", t=T)

            def convolve(j):
                out, done = self.project_T(self.columns(w_in, 2 + j), self.hT, self.psB[j])
                tiles = range(4 * j, 4 * j + 4)
                copied = free[j] = dve.after(done, z1).do(V.tensor_copy(xpad[:, 4 * j:4 * j + 4, 3:3 + T], out))
                w = lambda k, t: self.col("conv_w", 1, 8 * k + t)
                m = {}
                for t in tiles:
                    m[t] = dve.after(copied).do(V.tensor_scalar(
                        xc[:, t, :], xpad[:, t, 0:T], w(0, t), self.col("conv_b", 1, t), ALU.mult, ALU.add))
                for k in range(1, 4):
                    for t in tiles:
                        m[t] = dve.after(m[t]).do(V.scalar_tensor_tensor(
                            xc[:, t, :], xpad[:, t, k:k + T], w(k, t), xc[:, t, :], ALU.mult, ALU.add))
                return m[4 * j + 3]

            def gates(j, conv, read):
                pe.after(conv, self.late.now(), *read)
                for ps, n in ((r_ps, 0), (i_ps, 1)):
                    for t in range(4):
                        done = nc.tensor.matmul(ps[:, t, :], wri[:, n, 4 * j + t, :], xc[:, 4 * j + t, :],
                                                start=True, stop=True)
                    act.after(pe.do(done))
                    to, bias = ((ra, "b_r"), (ib, "b_i"))[n]
                    for t in range(4 * j, 4 * j + 4):
                        k = act.do(A.activation(to[:, t, :], ps[:, t - 4 * j, :], ACT.Sigmoid,
                                                bias=self.col(bias, 1, t)))
                    yield k

            def recurrence(j, conv, r_ready, i_ready):
                h4 = slice(4 * j, 4 * j + 4)
                ra4, th4, ib4, xc4 = ra[:, h4], th[:, h4], ib[:, h4], xc[:, h4]
                m = dve.after(r_ready, c8).do(V.tensor_tensor(ra4, ra4, c8b[:, h4], ALU.mult))
                k1 = act.after(m).do(A.activation(th4, ra4, ACT.Tanh))
                k2 = act.after(k1).do(A.activation(ra4, ra4, ACT.Exp))
                b = dve.after(i_ready, conv).do(V.tensor_tensor(ib4, ib4, xc4, ALU.mult))
                m = dve.after(k2, b).do(V.tensor_tensor(xc4, ra4, ra4, ALU.mult))
                m = dve.after(m, k1).do(V.scalar_tensor_tensor(th4, xc4, 1.0, th4, ALU.add, ALU.mult))
                k = act.after(m).do(A.activation(th4, th4, ACT.Sqrt, scale=-1.0))
                b = dve.after(k).do(V.tensor_tensor(ib4, ib4, th4, ALU.mult))
                dve.after(b)
                for t in range(4 * j, 4 * j + 4):
                    h = dve.do(V.tensor_tensor_scan(th[:, t, :], ra[:, t, :], ib[:, t, :], 0.0,
                                                    ALU.mult, ALU.add))
                return h

            def gate_branch(j):
                out, done = self.project_T(self.columns(w_in, j), self.hT, self.psB[j], free[j])
                return act.after(done).do(A.activation(gate[:, 4 * j:4 * j + 4, :], out, ACT.Gelu_apprx_tanh))

            conv = [convolve(0), convolve(1)]
            r0, i0 = gates(0, conv[0], ())
            h0 = recurrence(0, conv[0], r0, i0)
            gelu = gate_branch(0)
            y0 = dve.after(h0, gelu).do(V.tensor_tensor(gate[:, 0:4], gate[:, 0:4], th[:, 0:4], ALU.mult))
            r1, i1 = gates(1, conv[1], (r0, i0))
            h1 = recurrence(1, conv[1], r1, i1)
            gelu = gate_branch(1)
            y1 = dve.after(h1, gelu).do(V.tensor_tensor(gate[:, 4:8], gate[:, 4:8], th[:, 4:8], ALU.mult))
            w_out = a["lru_w_out"][0]
            for j in range(2):
                done = self.accumulate_nat(self.rows(w_out, j), gate[:, 4 * j:4 * j + 4, :], j == 0, j == 1,
                                           self.psA, (y0, y1)[j], i1)
            self.add_to_x(done)

    def add_to_x(self, done):
        for tt in range(TT):
            self.x_ready[tt] = self.dve.after(done[tt]).do(self.nc.vector.tensor_tensor(
                self.x[:, tt, :], self.x[:, tt, :],
                self.psA[:, 2 * tt:2 * tt + 2, :].rearrange("p a b -> p (a b)"), ALU.add))
        self.tiles_apart = True


    def split_high(self, src, t, high, *ready):
        V, dve, act = self.nc.vector, self.dve, self.act
        m = dve.after(*ready).do(V.tensor_scalar(t.bitcast(I32), src.bitcast(I32), KEEP12, None, ALU.bitwise_and))
        return m, act.after(m).do(self.nc.scalar.activation(high, t, ACT.Copy))

    def mlp(self, layer):
        nc, V, A, M = self.nc, self.nc.vector, self.nc.scalar, self.nc.tensor
        pe, dve, act, pool = self.compute
        self.rms_to_hT(self.col("mlp", KD, KD * layer))
        w1, w2 = self.a["mlp_w1"][layer], self.a["mlp_w2"][layer]
        low = self.low_parts
        with ExitStack() as c:
            HALF = PANEL // 2
            part = lambda name, n: [self.sb(f"{name}_{p}", [P, n], F32R, ctx=c) for p in ("high", "low")]
            h_parts = part("hT", KD * T)
            a_parts = [part(f"aT{j}", 4 * T) for j in range(2)]
            w_parts = [part(f"w{b}", HALF) for b in range(2)]
            cut = self.sb("cut", [P, HALF], ctx=c)
            relu = self.sb("relu", [P, 4 * T], ctx=c)
            sq = self.sb("relu_squared", [P, 4 * T], ctx=c)
            flat_h = self.hT[:].rearrange("p k t -> p (k t)")
            m, k = self.split_high(flat_h, cut[:], h_parts[0][:])
            m = dve.after(m).do(V.tensor_tensor(h_parts[1][:], flat_h, cut[:], ALU.subtract))
            h_ready = (m, k)
            for tt in range(TT):
                for half in range(2):
                    last = M.matmul(self.psA[:, 2 * tt + half, :], self.ident[:],
                                    self.x[:, tt, half * 512:(half + 1) * 512], start=True, stop=False)
            pe.do(last)
            pe.after(*h_ready)
            shares = {self.freed: 4, low: 4, pe.done: 8, act.done: 14, dve.done: 12,
                      **{s: 1 for s in self.arrived[:RING]}}
            with Loop(nc, 4, shares) as i:
                halves_done = {}
                hi_marks = {}

                def split(n, view, arrived):
                    cut_free = hi_marks.get(n - 1, act.done.before_iteration())
                    read = halves_done[n - 2] if n >= 2 else pe.done.before_iteration(but=1 - n)
                    w = w_parts[n % 2]
                    to = lambda t: t.rearrange("p (a b) -> p a b", b=view.shape[2])
                    act.after(read)
                    m, hi_marks[n] = self.split_high(view, to(cut[:]), to(w[0][:]), arrived, cut_free, read,
                                                     dve.done.before_iteration(), low_mark[0])
                    dve.after(m)
                    rest = V.tensor_tensor(to(w[1][:]), view, to(cut[:]), ALU.subtract)
                    low_mark[0] = (self.freed if n % 2 else low).add(rest)
                    return hi_marks[n], low_mark[0]

                low_mark = [self.freed.before_iteration()]

                def activate(j, done):
                    u = self.psB[j][:].rearrange("p a b -> p (a b)")
                    k = act.after(done, *sq_read).do(A.activation(relu[:], u, ACT.Relu))
                    k = act.after(k).do(A.activation(sq[:], relu[:], ACT.Square))
                    m, k = self.split_high(sq[:], cut[:, 0:4 * T], a_parts[j][0][:], k, hi_marks[2 * j + 3],
                                           pe.done.before_iteration(), low_mark[0])
                    hi_marks[2 * j + 3] = k
                    m = dve.after(m).do(V.tensor_tensor(a_parts[j][1][:], sq[:], cut[:, 0:4 * T], ALU.subtract))
                    sq_read.append(m)
                    low_mark[0] = m
                    return k, m

                sq_read = [dve.done.before_iteration()]
                a_ready = {}

                def load(j):
                    if j < 2:
                        view, arrived = self.columns(w1, i * 2 + j, dynamic=True)
                        for h in range(2):
                            yield view[:, :, 256 * h:256 * h + 256], arrived
                    else:
                        view, arrived = self.rows(w2, i * 2 + j - 2, dynamic=True)
                        for h in range(2):
                            yield view[:, 2 * h:2 * h + 2, :], arrived

                PARTS = ((0, 0), (0, 1), (1, 0))

                def multiply(n, marks):
                    j = n // 2
                    pe.after(*marks)
                    if j < 2:
                        ps = self.psB[j][:].rearrange("p a b -> p (a b)").rearrange("p (m t) -> p m t", t=T)
                        pe.after(act.done.before_iteration())
                        w = [t[:].rearrange("p (k n) -> p k n", n=256) for t in w_parts[n % 2]]
                        h = [t[:].rearrange("p (k t) -> p k t", t=T) for t in h_parts]
                        for m in range(2):
                            for k in range(KD):
                                for p, q in PARTS:
                                    last = M.matmul(ps[:, 2 * (n % 2) + m, :], w[p][:, k, m * P:(m + 1) * P],
                                                    h[q][:, k, :], start=(k == 0 and p == q),
                                                    stop=(k == KD - 1 and p == 1))
                    else:
                        pe.after(*a_ready[j - 2])
                        w = [t[:].rearrange("p (k n) -> p k n", n=D) for t in w_parts[n % 2]]
                        at = [t[:].rearrange("p (k t) -> p k t", t=T) for t in a_parts[j - 2]]
                        for k in range(2):
                            for tt in range(TT):
                                for half in range(2):
                                    for p, q in PARTS:
                                        last = M.matmul(self.psA[:, 2 * tt + half, :],
                                                        at[p][:, 2 * (n % 2) + k, tt * P:(tt + 1) * P],
                                                        w[q][:, k, half * 512:(half + 1) * 512],
                                                        start=False, stop=False)
                    halves_done[n] = pe.do(last)

                views = [v for j in range(4) for v in load(j)]
                ready = {n: split(n, *views[n]) for n in range(2)}
                for n in range(8):
                    multiply(n, ready[n])
                    if n + 2 < 8:
                        ready[n + 2] = split(n + 2, *views[n + 2])
                    if n in (1, 3):
                        a_ready[n // 2] = activate(n // 2, halves_done[n])
            self.panels += 3 * 4
            for bank in range(4):
                last = M.matmul(self.psA[:, bank, 0:1], self.ident[:], self.before[:, 0:1], start=False, stop=True)
            done = pe.do(last)
            for tt in range(TT):
                self.x_ready[tt] = dve.after(done).do(V.tensor_copy(
                    self.x[:, tt, :], self.psA[:, 2 * tt:2 * tt + 2, :].rearrange("p a b -> p (a b)")))
            self.tiles_apart = False


    def weighted_values(self, pT, v, heads, ps, *ready):
        M = self.nc.tensor
        self.pe.after(*ready)
        out = ps[:, 0, :].rearrange("p (h t d) -> p h t d", t=TT, d=HD)
        for g, h in enumerate(heads):
            vh = v[:, :, h * HD:(h + 1) * HD]
            M.matmul(out[:, g, 0, :], pT[:, g, 0:P], vh[:, 0, :], start=True, stop=True)
            M.matmul(out[:, g, 1, :], pT[:, g, P:2 * P], vh[:, 0, :], start=True, stop=False)
            last = M.matmul(out[:, g, 1, :], pT[:, g, 2 * P:3 * P], vh[:, 1, :], start=False, stop=True)
        return out, self.pe.do(last)


    def fox(self):
        nc, V, A, G, M = self.nc, self.nc.vector, self.nc.scalar, self.nc.gpsimd, self.nc.tensor
        pe, dve, act, pool = self.compute
        a = self.a
        w_in = a["fox_w_in"][0]
        self.rms_to_hT(self.col("mix", KD, KD))
        with ExitStack() as c:
            sb = lambda n, s: self.sb(n, s, ctx=c)
            nat = [sb(n, [P, TT, D]) for n in ("q_nat", "k_nat", "v_nat")]
            v_nat = nat[2]
            qT = sb("qT", [P, KD, T])
            kTz = sb("kT_padded", [P, NH, T])
            c_sel = sb("minus_head_row", [P, NH, P])
            cT = sb("cum_log_f", [P, T])
            mask = sb("causal", [P, 3 * P])
            score = [sb(f"scores{i}", [P, 2, 3 * P]) for i in range(2)]
            pT = sb("pT", [P, 4, 3 * P])
            wf = sb("w_f", [P, KD, NH])
            bf = sb("b_f", [NH, 1])
            ss = sb("qk_stats", [P, 3, 2, TT * NH])
            nm = sb("minus_max", [P, NH, 3])
            den = sb("softmax_sums", [P, NH, 2])
            sq = sb("squares", [P, TT, 512])
            lf = sb("log_f_work", [NH, 2, T])
            z = pool.do(G.memset(kTz[:], 0.0))
            pool.do(G.memset(c_sel[:], 0.0))
            pool.do(G.memset(mask[:], 0.0))
            pool.do(G.memset(cT[:], 0.0))
            pool.after(pool.done.now())
            pool.do(G.affine_select(out=c_sel[:], in_=c_sel[:], compare_op=ALU.not_equal, fill=-1.0,
                                    base=0, pattern=[[-1, NH], [0, P]], channel_multiplier=1))
            for at in (0, 2 * P):
                pool.do(G.affine_select(out=mask[:, at:at + P], in_=mask[:, at:at + P],
                                        compare_op=ALU.is_ge, fill=NEG, base=0, pattern=[[-1, P]],
                                        channel_multiplier=1))
            act.after(pool.done.now())
            with nc.allow_non_contiguous_dma(reason="one value per partition"):
                self.late.add(A.dma_start(bf[:], a["fox_b_f"][0].rearrange("(n o) -> n o", o=1)))
            self.late.add(A.dma_start(wf[:], w_in[:, 3 * D:].rearrange("(k p) n -> p k n", p=P)))
            qg = self.col("q_gain", 1)
            gain8 = sb("q_gain_eighth", [P, 1])
            g8 = dve.do(V.tensor_scalar(gain8[:], qg, HD ** -0.5, None, ALU.mult))

            free = [None, None]

            def project(j):
                ps, n = self.psB[j % 2], nat[j // 2]
                done = self.project_nat(self.columns(w_in, j), self.hT, ps, free[j % 2])
                part = n[:, :, (j % 2) * 512:(j % 2) * 512 + 512]
                free[j % 2] = act.after(done).do(A.activation(part, ps[:], ACT.Copy))
                return part

            for j in range(4):
                part = project(j)
                m = dve.after(free[j % 2], dve.done.now()).do(V.tensor_tensor(sq[:], part, part, ALU.mult))
                dst = ss[:, 0, j // 2, :].rearrange("p (t h) -> p t h", t=TT)[:, :, 8 * (j % 2):8 * (j % 2) + 8]
                m = dve.after(m).do(V.tensor_reduce(
                    dst, sq[:].rearrange("p t (h d) -> p t h d", d=HD), axis=AX.X, op=ALU.add))
            pe.after(self.late.now())
            for k in range(KD):
                last = M.matmul(self.psA[0:NH, 0, 0:T], wf[:, k, :], self.hT[:, k, :],
                                start=(k == 0), stop=(k == KD - 1))
            fdone = pe.do(last)
            fps = self.psA[0:NH, 0, 0:T]
            k = act.after(fdone, self.late.now()).do(A.activation(lf[:, 0, :], fps, ACT.Abs, bias=bf[:]))
            bank_free = k
            k = act.after(k).do(A.activation(lf[:, 0, :], lf[:, 0, :], ACT.Exp, scale=-1.0))
            k = act.after(k).do(A.activation(lf[:, 0, :], lf[:, 0, :], ACT.Ln, bias=1.0))
            m = dve.after(bank_free, self.late.now()).do(
                V.tensor_scalar(lf[:, 1, :], fps, bf[:], 0.0, ALU.add, ALU.min))
            m = dve.after(m, k).do(V.tensor_tensor(lf[:, 1, :], lf[:, 1, :], lf[:, 0, :], ALU.subtract))
            one = self.ones[0:NH, 0:1].to_broadcast([NH, T])
            cdone = dve.after(m).do(V.tensor_tensor_scan(cT[0:NH, :], one, lf[:, 1, :], 0.0, ALU.mult, ALU.add))

            ms, y, t = (ss[:, i].rearrange("p a b -> p (a b)") for i in range(3))
            m = dve.do(V.tensor_scalar(ms, ms, 1.0 / HD, EPS, ALU.mult, ALU.add))
            r = self.rsqrt(ms, y, t, m)
            for i in range(2):
                v3 = nat[i][:].rearrange("p t (h d) -> p (t h) d", d=HD)
                m = dve.after(r).do(V.tensor_tensor(
                    v3, v3, ss[:, 1, i, :].unsqueeze(2).to_broadcast([P, TT * NH, HD]), ALU.mult))
            for j in (4, 5):
                project(j)
            for g in range(4):
                i = g // 2
                out, done = self.transpose_to(nat[i], 4 * (g % 2), 4, self.psB[g % 2], m, free[g % 2])
                c0 = 4 * (g % 2)
                if i == 0:
                    free[g % 2] = dve.after(done, g8).do(V.tensor_scalar(
                        qT[:, c0:c0 + 4, :], out[:], gain8[:], None, ALU.mult))
                else:
                    for half in range(2):
                        rows = slice(64 * half, 64 * half + 64)
                        to = kTz[rows, 2 * c0 + half:2 * c0 + 8:2, :]
                        free[g % 2] = dve.after(done, z).do(V.tensor_scalar(
                            to, out[rows], self.col("k_gain", 1)[rows], None, ALU.mult))
            qk = dve.done.now()

            o_nat = nat[0]
            PAIRS = NH // 2
            s_free, softmaxed, copied, o_read = {}, {}, {}, {}
            mb = mask[:].unsqueeze(1).to_broadcast([P, 2, 3 * P])

            def pair_scores(g):
                S, sc = self.psA[:, 2 * (g % 2):2 * (g % 2) + 2, :], score[g % 2]
                pe.after(qk, cdone, pool.done.now(), s_free.get(g - 2))
                for i, h in enumerate((2 * g, 2 * g + 1)):
                    for t0, s1, at in ((0, P, 0), (P, T, P)):
                        out = S[:, i, at:at + s1]
                        M.matmul(out, qT[:, h // 2, t0:t0 + P], kTz[:, h, 0:s1], start=True, stop=False)
                        last = M.matmul(out, c_sel[:, h, :], cT[:, 0:s1], start=False, stop=True)
                return S, sc, pe.do(last)

            def pair_softmax(g, S, sc, s_done):
                m = s_free[g] = dve.after(s_done, softmaxed.get(g - 2)).do(
                    V.tensor_tensor(sc[:], S[:, :, 0:3 * P], mb, ALU.add))
                hs = slice(2 * g, 2 * g + 2)
                dve.after(m)
                m0 = dve.do(V.tensor_reduce(nm[:, hs, 0], sc[:, :, 0:P], axis=AX.X, op=ALU.max, negate=True))
                m1 = dve.do(V.tensor_reduce(nm[:, hs, 1], sc[:, :, P:], axis=AX.X, op=ALU.max, negate=True))
                act.after(m0, m1)
                for i, h in enumerate((2 * g, 2 * g + 1)):
                    for j, cols in enumerate((slice(0, P), slice(P, 3 * P))):
                        k = act.do(A.activation(sc[:, i, cols], sc[:, i, cols], ACT.Exp,
                                                bias=nm[:, h, j:j + 1], accum_out=den[:, h, j:j + 1]))
                softmaxed[g] = k

            def pair_transpose(g):
                ps = self.psB[g % 2]
                pe.after(softmaxed[g], qk, o_read.get(g - 2))
                for i in range(2):
                    for b in range(3):
                        last = M.transpose(ps[:, i, b * P:(b + 1) * P], score[g % 2][:, i, b * P:(b + 1) * P],
                                           self.ident[:])
                done = pe.do(last)
                copied[g] = act.after(done).do(A.activation(
                    pT[:, 2 * (g % 2):2 * (g % 2) + 2, :], ps[:, :, 0:3 * P], ACT.Copy))

            def pair_values(g):
                out, done = self.weighted_values(pT[:, 2 * (g % 2):2 * (g % 2) + 2, :], v_nat, (2 * g, 2 * g + 1),
                                                 self.psB[g % 2], copied[g], *free)
                hs = slice(2 * g, 2 * g + 2)
                r = dve.after(softmaxed[g]).do(V.reciprocal(den[:, hs, :], den[:, hs, :]))
                to = o_nat[:, :, 2 * g * HD:(2 * g + 2) * HD].rearrange("p t (h d) -> p h t d", d=HD)
                o_read[g] = dve.after(done, r).do(V.tensor_tensor(
                    to, out[:, 0:2], den[:, hs, :].unsqueeze(3).to_broadcast([P, 2, 2, HD]), ALU.mult))

            v_ready = act.done.now()
            free = [v_ready]
            for g in range(PAIRS + 2):
                if g < PAIRS:
                    parts = pair_scores(g)
                if g >= 2:
                    pair_values(g - 2)
                if 1 <= g <= PAIRS:
                    pair_transpose(g - 1)
                if g < PAIRS:
                    pair_softmax(g, *parts)
            o_read, s_free = o_read[PAIRS - 1], s_free[PAIRS - 1]
            o = self.to_T(o_nat, self.hT, o_read)
            w_out = a["fox_w_out"][0]
            for j in range(2):
                done = self.accumulate_nat(self.rows(w_out, j), self.hT[:, 4 * j:4 * j + 4, :], j == 0, j == 1,
                                           self.psA, o, s_free)
            self.add_to_x(done)


    def hybrid(self):
        nc, V, A, G, M = self.nc, self.nc.vector, self.nc.scalar, self.nc.gpsimd, self.nc.tensor
        pe, dve, act, pool = self.compute
        a = self.a
        w_in = a["w_in_2"][0]
        self.join()
        flat = lambda t: t.rearrange("p a b -> p (a b)")
        with ExitStack() as c:
            sb = lambda n, s, dt=F32: self.sb(n, s, dt, ctx=c)
            o_sb = sb("o_sb", [P, TT, SBW])
            o_hg = sb("o_hg", [P, TT, HGW])
            gates = sb("gates", [P, 2, TT, D])
            sig_g = sb("sigmoid_hg", [P, TT, HGW])
            with ExitStack() as c2:
                sb2 = lambda n, s, dt=F32: self.sb(n, s, dt, ctx=c2)
                qT = sb2("sb_qT", [P, 4, T])
                kTz = sb2("sb_kT_padded", [P, SBH, T])
                v_sb = sb2("sb_v", [P, TT, SBW])
                hq = sb2("hg_q", [P, HGH, T])
                hk = sb2("hg_k", [P, HGH, T])
                hb = sb2("hg_cum_log_f", [P, HGH, T])
                hv = sb2("hg_v", [P, TT, HGW])
                mask = sb2("sb_mask", [P, 3 * P])
                lvl = sb2("level_masks", [P, 7, P])
                keep = sb2("scan_keep", [P, T])
                gn = sb2("hgrn_gain", [P, HGW])
                self.late.add(A.dma_start(gn[:], a["hgrn_norm_g_2"][0].partition_broadcast(P)))
                lb = sb2("lb_work", [P, 4, 4])
                z = pool.do(G.memset(kTz[:], 0.0))
                pool.do(G.memset(mask[:], 1.0))
                pool.do(G.memset(lvl[:], 1.0))
                k0 = pool.do(G.memset(keep[:], 1.0))
                pool.after(k0)
                pool.do(G.memset(keep[:].rearrange("p (n t) -> p n t", t=P)[:, :, 0:1], 0.0))
                pool.do(G.affine_select(out=mask[:, 0:T], in_=mask[:, 0:T], compare_op=ALU.is_gt, fill=0.0,
                                        base=0, pattern=[[1, T]], channel_multiplier=-1))
                pool.do(G.affine_select(out=mask[:, T:], in_=mask[:, T:], compare_op=ALU.is_gt, fill=0.0,
                                        base=0, pattern=[[1, P]], channel_multiplier=-1))
                for l in range(7):
                    h = 2 ** l
                    n = P // (2 * h)
                    for base, pattern, cm in ((0, [[-2 * h, n], [0, 2 * h]], 1),
                                              (h - 1, [[2 * h, n], [0, 2 * h]], -1),
                                              (-h, [[0, n], [1, 2 * h]], 0)):
                        pool.after(pool.done.now())
                        pool.do(G.affine_select(out=lvl[:, l, :], in_=lvl[:, l, :], compare_op=ALU.is_ge,
                                                fill=0.0, base=base, pattern=pattern, channel_multiplier=cm))

                l0, l1 = self.col("lb", 4), self.col("lb", 4, 4)
                m = dve.do(V.tensor_tensor(lb[:, 0], l0, l1, ALU.max))
                m0 = dve.after(m).do(V.tensor_tensor(lb[:, 1], l0, lb[:, 0], ALU.subtract))
                m1 = dve.after(m).do(V.tensor_tensor(lb[:, 2], l1, lb[:, 0], ALU.subtract))
                k = act.after(m1, m0).do(A.activation(lb[:, 1:3], lb[:, 1:3], ACT.Exp))
                m = dve.after(k).do(V.tensor_tensor(lb[:, 2], lb[:, 1], lb[:, 2], ALU.add))
                m = dve.after(m).do(V.reciprocal(lb[:, 2], lb[:, 2]))
                m = dve.after(m).do(V.tensor_tensor(lb[:, 0], lb[:, 1], lb[:, 2], ALU.mult))
                lb_done = dve.after(m).do(V.tensor_scalar(lb[:, 3], lb[:, 0], -1.0, 1.0, ALU.mult, ALU.add))

                x_T = self.to_T(self.x, self.hT)
                free = [x_T, x_T]
                proj = lambda j: (self.project_T if j in (0, 1, 3, 4) else self.project_nat)(
                    self.columns(w_in, j), self.hT, self.psB[j % 2], free[j % 2])
                out, done = proj(0)
                q_done = free[0] = act.after(done).do(A.activation(qT[:], out, ACT.Copy, scale=HD ** -0.5))
                out, done = proj(1)
                for half in range(2):
                    rows = slice(64 * half, 64 * half + 64)
                    k_done = free[1] = dve.after(done, z).do(V.tensor_copy(kTz[rows, half::2, :], out[rows]))
                done = proj(2)
                v_done = free[0] = act.after(done).do(A.activation(v_sb[:], self.psB[0][:], ACT.Copy))

                Z = self.psA
                Zc = Z[:, :, 0:3 * P]
                mb = mask[:].unsqueeze(1).to_broadcast([P, 4, 3 * P])

                def stick_scores(g, *ready):
                    pe.after(q_done, k_done, *ready)
                    for i in range(4):
                        h = 4 * g + i
                        M.matmul(Z[:, i, 0:T], kTz[:, h, 0:P], qT[:, h // 2, :], start=True, stop=True)
                        last = M.matmul(Z[:, i, T:3 * P], kTz[:, h, P:T], qT[:, h // 2, P:T],
                                        start=True, stop=True)
                    z_done = pe.do(last)
                    k = z_read = act.after(z_done, *ready).do(A.activation(sp[:], Zc, ACT.Abs))
                    k = act.after(k).do(A.activation(sp[:], sp[:], ACT.Exp, scale=-1.0))
                    k = act.after(k).do(A.activation(sp[:], sp[:], ACT.Ln, bias=1.0))
                    m = dve.after(k, z_read).do(V.scalar_tensor_tensor(sp[:], Zc, 0.0, sp[:], ALU.max, ALU.add))
                    lw_done = dve.after(m).do(V.tensor_tensor(lw[:], Zc, sp[:], ALU.subtract))
                    return dve.after(lw_done, masks).do(V.tensor_tensor(sp[:], sp[:], mb, ALU.mult))

                def stick_sums(ready):
                    pe.after(ready)
                    for i in range(4):
                        bank = Z[:, i, :]
                        M.matmul(bank[:, 0:T], self.after_[:], sp[:, i, 0:T], start=True, stop=False)
                        M.matmul(bank[:, P:T], self.ones[:], sp[:, i, T:], start=False, stop=True)
                        last = M.matmul(bank[:, T:3 * P], self.after_[:], sp[:, i, T:], start=True, stop=True)
                    return pe.do(last)

                def stick_weights(done):
                    m = dve.after(done).do(V.tensor_tensor(lw[:], lw[:], Zc, ALU.subtract))
                    k = act.after(m).do(A.activation(w[:], lw[:], ACT.Exp))
                    return dve.after(k).do(V.tensor_tensor(w[:], w[:], mb, ALU.mult))

                def stick_values(g, ready):
                    out, done = self.weighted_values(w, v_sb, range(4 * g, 4 * g + 4), Z, v_done, ready)
                    to = o_sb[:, :, 256 * g:256 * g + 256].rearrange("p t (h d) -> p h t d", d=HD)
                    return dve.after(done).do(V.tensor_copy(to, out))

                masks = pool.done.now()
                with ExitStack() as c3:
                    sp, lw, w = (self.sb(n, [P, 4, 3 * P], ctx=c3) for n in ("softplus", "log_w", "sb_w"))
                    m = stick_scores(0)
                    out, done = proj(3)
                    summed = stick_sums(m)
                    k = act.after(done).do(A.activation(hq[:], out, ACT.Sigmoid))
                    free[1] = dve.after(k).do(V.tensor_tensor(hq[:], hq[:], out, ALU.mult))
                    m = stick_weights(summed)
                    out, done = proj(4)
                    free[0] = k = act.after(done).do(A.activation(hk[:], out, ACT.Sigmoid))
                    values = stick_values(0, m)
                    z_ready = stick_scores(1, values)
                    bc = lambda i: lb[:, i, :].unsqueeze(2).to_broadcast([P, 4, T])
                    m = dve.after(k, lb_done).do(V.tensor_tensor(hk[:], hk[:], bc(3), ALU.mult))
                    f_done = dve.after(m).do(V.tensor_tensor(hb[:], hk[:], bc(0), ALU.add))
                    hk_done = dve.after(f_done).do(V.tensor_scalar(hk[:], hb[:], -1.0, 1.0, ALU.mult, ALU.add))
                    k = act.after(hk_done).do(A.activation(hb[:], hb[:], ACT.Ln))
                    done = proj(5)
                    summed = stick_sums(z_ready)
                    free[1] = hv_done = act.after(done).do(A.activation(hv[:], self.psB[1][:], ACT.Copy))
                    m = stick_weights(summed)
                    dve.after(k)
                    for h in range(HGH):
                        b_done = dve.do(V.tensor_tensor_scan(hb[:, h], keep[:], hb[:, h], 0.0, ALU.mult, ALU.add))
                    done = proj(6)
                    free[0] = act.after(done).do(A.activation(sig_g[:], self.psB[0][:], ACT.Sigmoid))
                    o_sb_done = stick_values(1, m)

                gate_free = [o_sb_done, o_sb_done]

                def gate_tiles():
                    for j in range(4):
                        (wj, arrived), ps = self.columns(w_in, 7 + j), self.psA[:, 2 * (j % 2):2 * (j % 2) + 2, :]
                        for tt in range(TT):
                            pe.after(arrived, gate_free[j % 2])
                            for k in range(KD):
                                last = M.matmul(ps[:, tt, :], self.hT[:, k, tt * P:(tt + 1) * P], wj[:, k, :],
                                                start=(k == 0), stop=(k == KD - 1))
                            if tt:
                                done = self.freed.add(last)
                                to = gates[:, j // 2, :, (j % 2) * 512:(j % 2) * 512 + 512]
                                gate_free[j % 2] = act.after(done).do(A.activation(to, ps, ACT.Copy))
                            yield

                gate_tile = gate_tiles()
                with ExitStack() as c3:
                    E = [self.sb("decay", [P, HGH, T], ctx=c3), kTz[:, 0:4, :]]
                    Q = [self.sb("q_decayed", [P, HGH, T], ctx=c3), qT]
                    K = [self.sb("k_decayed", [P, HGH, T], ctx=c3), kTz[:, 4:8, :]]
                    S = self.sb("hg_scores", [P, HGH * TT, P], ctx=c3)
                    X = self.sb("hg_cross", [P, HGH, P], ctx=c3)
                    st = self.sb("hg_stats", [P, 3, TT * HGH], ctx=c3)
                    blocks = lambda t, n: flat(t[:]).rearrange("p (n s) -> p n s", s=n)
                    LEVELS = 7
                    decayed, exps = {}, {}
                    scored = {-2: o_sb_done, -1: o_sb_done}
                    read = {-2: free[0], -1: free[1]}

                    def scores(ps, q, k_):
                        out = ps[:].rearrange("p a b -> p (a b)").rearrange("p (n t) -> p n t", t=P)
                        qv, kv = blocks(q, P), blocks(k_, P)
                        for n in range(HGH * TT):
                            last = M.matmul(out[:, n, :], kv[:, n, :], qv[:, n, :], start=True, stop=True)
                        return out, pe.do(last)

                    def decay(l):
                        e = E[l % 2]
                        dve.after(b_done, o_sb_done, *decayed.get(l - 2, ()))
                        if l < LEVELS:
                            h = 2 ** l
                            b2, e2 = blocks(hb, 2 * h), blocks(e, 2 * h)
                            mid = b2[:, :, h - 1:h].to_broadcast([P, HGH * T // (2 * h), 2 * h])
                            m = dve.do(V.tensor_tensor(e2, b2, mid, ALU.subtract))
                            k = act.after(m).do(A.activation(e[:], e[:], ACT.Abs))
                            exps[l] = act.after(k).do(A.activation(e[:], e[:], ACT.Exp, scale=-1.0))
                        else:
                            end = hb[:, :, P - 1:P].to_broadcast([P, HGH, P])
                            m0 = dve.do(V.tensor_tensor(e[:, :, 0:P], end, hb[:, :, 0:P], ALU.subtract))
                            m1 = dve.do(V.tensor_copy(e[:, :, P:], hb[:, :, P:]))
                            exps[l] = act.after(m0, m1).do(A.activation(e[:], e[:], ACT.Exp))

                    def decay_qk(l):
                        e, q, k_ = E[l % 2], Q[l % 2], K[l % 2]
                        qc, kc = (slice(P, T), slice(0, P)) if l == LEVELS else (slice(0, T), slice(0, T))
                        p = pool.after(exps[l], scored[l - 2]).do(
                            G.tensor_tensor(q[:, :, qc], hq[:, :, qc], e[:, :, qc], ALU.mult))
                        m = dve.after(exps[l], scored[l - 2]).do(
                            V.tensor_tensor(k_[:, :, kc], hk[:, :, kc], e[:, :, kc], ALU.mult))
                        decayed[l] = (p, m)

                    decay(0)
                    pe.after(read[-1], hk_done)
                    out, done = scores(self.psB[1], hq, hk)
                    next(gate_tile)
                    decay_qk(0)
                    decay(1)
                    s_done = read[-1] = dve.after(done).do(V.tensor_tensor(
                        S[:], out, self.ident[:].unsqueeze(1).to_broadcast([P, HGH * TT, P]), ALU.mult))
                    for l in range(LEVELS):
                        pe.after(*decayed[l], read[l - 2])
                        out, scored[l] = scores(self.psB[l % 2], Q[l % 2], K[l % 2])
                        next(gate_tile)
                        decay_qk(l + 1)
                        if l + 2 <= LEVELS:
                            decay(l + 2)
                        mk = lvl[:, l, :].bitcast(U32).unsqueeze(1).to_broadcast([P, HGH * TT, P])
                        s_done = read[l] = dve.after(scored[l], s_done).do(V.copy_predicated(S[:], mk, out))
                    next(gate_tile, None)
                    pe.after(*decayed[LEVELS], read[LEVELS - 2])
                    for h in range(HGH):
                        last = M.matmul(self.psB[1][:, 0, h * P:(h + 1) * P], K[1][:, h, 0:P], Q[1][:, h, P:],
                                        start=True, stop=True)
                    done = pe.do(last)
                    x_done = dve.after(done).do(V.tensor_copy(
                        X[:], self.psB[1][:, 0, :].rearrange("p (h t) -> p h t", t=P)))
                    oT = [t[:].rearrange("p a b -> p (a b)").rearrange("p (m t) -> p m t", t=T) for t in (v_sb, hv)]
                    out, done = self.transpose_to(o_sb, 0, 4, self.psB[0], s_done, o_sb_done)
                    sb_T = act.after(done).do(A.activation(oT[0], out, ACT.Copy))
                    pe.after(x_done, s_done, hv_done)
                    for h in range(HGH):
                        cols = slice(h * P, (h + 1) * P)
                        M.matmul(self.psB[1][:, 0, cols], S[:, 2 * h, :], hv[:, 0, cols], start=True, stop=True)
                        M.matmul(self.psB[1][:, 1, cols], X[:, h, :], hv[:, 0, cols], start=True, stop=False)
                        last = M.matmul(self.psB[1][:, 1, cols], S[:, 2 * h + 1, :], hv[:, 1, cols],
                                        start=False, stop=True)
                    done = pe.do(last)
                    branch_sb = self.accumulate_nat(self.rows(a["w_branch_sb_2"][0], 0), oT[0], True, True,
                                                    self.psA, sb_T, *gate_free)
                    k = act.after(done).do(A.activation(o_hg[:], self.psB[1][:], ACT.Copy))
                    sq = E[0][:].rearrange("p h t -> p (h t)").rearrange("p (t n) -> p t n", t=TT)
                    m = dve.after(k, *decayed[LEVELS - 1]).do(V.tensor_tensor(sq, o_hg[:], o_hg[:], ALU.mult))
                    m = dve.after(m).do(V.tensor_reduce(st[:, 0], sq.rearrange("p t (h d) -> p (t h) d", d=HGD),
                                                        axis=AX.X, op=ALU.add))
                    m = dve.after(m).do(V.tensor_scalar(st[:, 0], st[:, 0], 1.0 / HGD, EPS, ALU.mult, ALU.add))
                    r = self.rsqrt(st[:, 0], st[:, 1], st[:, 2], m)
                    g2 = lambda i: gates[:, i].rearrange("p t n -> p (t n)")
                    act.after(*gate_free)
                    sigmoids = [act.do(A.activation(g2(i), g2(i), ACT.Sigmoid)) for i in range(2)]
                    oh = o_hg[:].rearrange("p t (h d) -> p (t h) d", d=HGD)
                    m = dve.after(r).do(V.tensor_tensor(
                        oh, oh, st[:, 1].unsqueeze(2).to_broadcast([P, TT * HGH, HGD]), ALU.mult))
                    m = dve.after(m, self.late.now()).do(V.tensor_tensor(
                        o_hg[:], o_hg[:], gn[:].unsqueeze(1).to_broadcast([P, TT, HGW]), ALU.mult))
                    m = dve.after(m).do(V.tensor_tensor(o_hg[:], o_hg[:], sig_g[:], ALU.mult))
                    out, done = self.transpose_to(o_hg, 0, 4, self.psB[0], m, sb_T)
                    hg_T = act.after(done).do(A.activation(oT[1], out, ACT.Copy))
                    psf = flat(self.psA[:])
                    m = dve.after(*branch_sb, *sigmoids).do(V.tensor_tensor(g2(0), g2(0), psf, ALU.mult))
                    done = self.accumulate_nat(self.rows(a["w_branch_hgrn_2"][0], 0), oT[1], True, True,
                                               self.psA, hg_T, m)
                    m1 = dve.after(*done).do(V.tensor_tensor(g2(1), g2(1), psf, ALU.mult))
                    m = dve.after(m, m1).do(V.tensor_tensor(g2(0), g2(0), g2(1), ALU.add))
                    m = self.to_T(gates[:, 0], self.hT, m, hg_T)
                    for j in range(2):
                        done = self.accumulate_nat(self.rows(a["w_out_2"][0], j), self.hT[:, 4 * j:4 * j + 4, :],
                                                   j == 0, j == 1, self.psA, m, m1)
                    for tt in range(TT):
                        dve.after(done[tt]).do(V.scalar_tensor_tensor(
                            self.x[:, tt, :], self.x[:, tt, :], ALPHA, flat(self.psA[:, 2 * tt:2 * tt + 2, :]),
                            ALU.mult, ALU.add))
                    self.join()

    def layer_norm(self, x, gain, bias, ctx, *ready):
        V, dve = self.nc.vector, self.dve
        bn = self.sb("bn_stats", [P, TT, 2, 6], ctx=ctx)
        mv = self.sb("mean_var", [P, TT, 2], ctx=ctx)
        w = self.sb("ln_work", [P, 3, TT], ctx=ctx)
        for tt in range(TT):
            for h in range(2):
                dve.do(V.bn_stats(bn[:, tt, h, :], x[:, tt, h * 512:(h + 1) * 512]))
        dve.after(dve.done.now())
        for tt in range(TT):
            dve.do(V.bn_aggr(mv[:, tt, :], bn[:, tt]))
        stats = dve.done.now()
        m = dve.after(stats).do(V.tensor_scalar(w[:, 0], mv[:, :, 1], LN_EPS, None, ALU.add))
        centred = []
        a = self.act.after(m).do(self.nc.scalar.activation(w[:, 1], w[:, 0], ACT.Sqrt))
        dve.after(*ready)
        for tt in range(TT):
            centred.append(dve.do(V.scalar_tensor_tensor(x[:, tt, :], x[:, tt, :], mv[:, tt, 0:1], gain,
                                                         ALU.subtract, ALU.mult)))
        a = dve.after(a).do(V.reciprocal(w[:, 1], w[:, 1]))
        r = self.newton_rsqrt(w[:, 0], w[:, 1], w[:, 2], a)
        dve.after(r, *centred)
        return [dve.do(V.scalar_tensor_tensor(x[:, tt, :], x[:, tt, :], w[:, 1, tt:tt + 1], bias,
                                              ALU.mult, ALU.add)) for tt in range(TT)]


    def moe(self):
        nc, V, A, G, M = self.nc, self.nc.vector, self.nc.scalar, self.nc.gpsimd, self.nc.tensor
        pe, dve, act, pool = self.compute
        a, c = self.a, self.ctx
        sb = self.sb
        flat = lambda t: t.rearrange("p a b -> p (a b)")
        ln = sb("ln_params", [P, 4, D])
        acc = sb("moe_sum", [P, TT, D])
        cnt = sb("expert_counts", [1, NE], I32)
        slot = sb("slot_of_token", [P, TT, NE + 1])
        gate = sb("gate_of_token", [P, TT, NE + 1])
        brow = sb("b_up", [P, 2 * D])
        brow_of = sb("b_up_selector", [P, SLOTS])
        iota = sb("iota", [P, T])
        iota_ab = sb("iota_ab", [P, 2, P])
        ids = sb("slot_ids_ab", [P, 2, P])
        one_hot = sb("one_hot", [P, TT, P])
        weighted = sb("gated_one_hot", [P, 2, TT, P])
        scatter = sb("scatter_matrix", [P, 2, T])
        xg = sb("gathered_T", [P, KD, P])
        glu = sb("glu", [P, 512])
        lin = sb("linear", [P, 512])
        sig = sb("swish_gate", [P, 512])
        actT = sb("activated_T", [P, 4, P])
        y = sb("expert_out", [P, 512])
        U, AT, DN = self.psA[:, 0:2, :], self.psA[:, 2, :], self.psA[:, 3, :]
        X, S = self.psB[0], self.psB[1]
        Xg = X[:].rearrange("p a b -> p (a b)").rearrange("p (n s) -> p n s", s=P)

        rw = sb("router_w", [P, KD, NE])
        rb = sb("router_b", [P, NE])
        bdown = sb("b_down", [P, D])
        gT = sb("gate_T", [P, T])
        logit = sb("logits", [P, TT, NE])
        top = sb("top8", [P, TT, 8])
        idx = sb("top8_index", [P, TT, 8], U32)
        idxf = sb("top8_index_f", [P, TT, 8])
        gts = sb("top4_exps", [P, TT, TOPK])
        gn = sb("top4_gates", [P, TT, TOPK])
        st = sb("router_stats", [P, TT, 2])
        sel = sb("chosen", [P, TT, NE])
        choice = sb("choices", [P, TT, TOPK, NE])
        gated_choice = sb("gated_choices", [P, TT, TOPK, NE])
        for i, name in enumerate(("ln1_g_2", "ln1_b_2")):
            self.late.add(A.dma_start(ln[:, i, :], a[name][0].partition_broadcast(P)))
        self.late.add(A.dma_start(rw[:], a["router_w_2"][0].rearrange("(k p) n -> p k n", p=P)))
        self.late.add(A.dma_start(rb[:], a["router_b_2"][0].partition_broadcast(P)))
        loaded = self.late.now()
        z = [pool.do(G.memset(t, v)) for t, v in ((bdown[:], 0.0), (brow[:], 0.0))]
        pool.do(G.iota(iota[:], pattern=[[1, T]], base=0, channel_multiplier=0,
                       allow_small_or_imprecise_dtypes=True))
        act.after(*z)
        self.small.add(A.dma_start(brow[0:NE, :], a["expert_b_up_2"][0]))
        self.small.add(A.dma_start(bdown[0:NE, :], a["expert_b_down_2"][0]))
        for i, name in enumerate(("ln2_g_2", "ln2_b_2")):
            self.small.add(A.dma_start(ln[:, 2 + i, :], a[name][0].partition_broadcast(P)))
        biases = self.small.now()
        pool.do(G.memset(slot[:], -1.0))
        pool.do(G.memset(gate[:], 0.0))
        pool.do(G.memset(gT[:], 0.0))
        pool.do(G.memset(iota_ab[:], -1000.0))
        pool.after(pool.done.now())
        for ab in range(2):
            pool.do(G.iota(iota_ab[:, ab, ab * SLOTS:(ab + 1) * SLOTS], pattern=[[1, SLOTS]], base=0,
                           channel_multiplier=0, allow_small_or_imprecise_dtypes=True))
        pool.do(G.memset(scatter[:], 0.0))
        z = pool.do(G.memset(y[:], 0.0))
        self.sp.after(loaded)
        ln1 = self.layer_norm(self.x, ln[:, 0, :], ln[:, 1, :], c, loaded)
        hT = self.to_T(self.x, self.hT, *ln1)
        W = self.psA
        pe.after(hT, loaded)
        for tt in range(TT):
            for k in range(KD):
                last = M.matmul(W[:, tt, 0:NE], self.hT[:, k, tt * P:(tt + 1) * P], rw[:, k, :],
                                start=(k == 0), stop=(k == KD - 1))
        done = pe.do(last)
        m = dve.after(done, loaded).do(V.tensor_tensor(
            logit[:], W[:, 0:TT, 0:NE], rb[:].unsqueeze(1).to_broadcast([P, TT, NE]), ALU.add))
        dve.after(m)
        tops = [dve.do(V.max(top[:, tt, :], logit[:, tt, :])) for tt in range(TT)]
        dve.after(*tops)
        for tt in range(TT):
            dve.do(V.max_index(idx[:, tt, :], top[:, tt, :], logit[:, tt, :]))
        negated = dve.do(V.tensor_scalar(st[:, :, 0:1], top[:, :, 0:1], -1.0, None, ALU.mult))
        m = dve.after(dve.done.now()).do(V.tensor_copy(idxf[:], idx[:]))
        dve.after(m, pool.done.now())
        numbers = iota[:, 0:NE].unsqueeze(1).to_broadcast([P, TOPK, NE])
        picks = [dve.do(V.tensor_tensor(choice[:, tt], numbers,
                                        idxf[:, tt, 0:TOPK].unsqueeze(2).to_broadcast([P, TOPK, NE]), ALU.is_equal))
                 for tt in range(TT)]
        m = dve.after(*picks).do(V.tensor_reduce(sel[:], choice[:].rearrange("p t j e -> p t e j"), axis=AX.X,
                                                 op=ALU.add))
        pe.after(m)
        M.matmul(W[:, 2, 0:NE], self.before[:], sel[:, 0], start=True, stop=True)
        M.matmul(W[:, 3, 0:NE], self.ones[:], sel[:, 0], start=True, stop=False)
        M.matmul(W[:, 3, 0:NE], self.before[:], sel[:, 1], start=False, stop=True)
        M.matmul(W[:, 0, 0:NE], self.ones[:], sel[:, 0], start=True, stop=False)
        last = M.matmul(W[:, 0, 0:NE], self.ones[:], sel[:, 1], start=False, stop=True)
        placed = pe.do(last)
        act.after(negated)
        for tt in range(TT):
            k = act.do(A.activation(gts[:, tt, :], top[:, tt, 0:TOPK], ACT.Exp,
                                    bias=st[:, tt, 0:1], accum_out=st[:, tt, 1:2]))
        m = dve.after(placed).do(V.scalar_tensor_tensor(slot[:, :, 0:NE], W[:, 2:4, 0:NE], 1.0, sel[:],
                                                        ALU.add, ALU.mult))
        slots = dve.after(m).do(V.tensor_scalar(slot[:, :, 0:NE], slot[:, :, 0:NE], -1.0, None, ALU.add))
        counted = dve.do(V.tensor_copy(cnt[:], W[0:1, 0, 0:NE]))

        sem = lambda name: Count(self.sem(name))
        selected, built, gated = sem("bias_row_selected"), sem("one_hot_built"), sem("gated_one_hot_built")
        gathered, gather_copied = sem("x_gathered"), sem("gathered_copied")
        up_done, hidden_read, activated = sem("up_products_done"), sem("up_products_read"), sem("activated")
        act_T, act_copied = sem("activated_transposed"), sem("activated_copied")
        down_done, y_copied = sem("down_products_done"), sem("out_copied")
        weighted_T, scatter_copied = sem("gated_transposed"), sem("scatter_matrix_copied")
        scattered, summed = sem("scattered_tiles"), sem("summed_tiles")
        px, dx, ax = (Engine(e.engine, self.sem(n)) for e, n in (
            (pe, "extra_pe"), (dve, "extra_dve"), (act, "extra_act")))
        xg_x = sb("extra_gathered_T", [P, KD, P])
        scatter_x = sb("extra_scatter_matrix", [P, 2, T])
        y_x = sb("extra_out", [P, 512])

        w_up, w_down = a["expert_w_up_2"][0], a["expert_w_down_2"][0]
        order = [4, 5] + [(self.panels + r) % RING for r in range(RING)]
        panel = [self.ring[:, s, :].rearrange("p (k n) -> p k n", k=2 if j < 4 else 4)
                 for j, s in enumerate(order)]

        def sources(e):
            for j in range(4):
                yield w_up[bass.ds(e, 1), j * 256:(j + 1) * 256, :].rearrange("o (k p) n -> p (o k) n", p=P)
            for j in range(2):
                yield w_down[bass.ds(e, 1), j * 512:(j + 1) * 512, :].rearrange("o (k p) n -> p (o k) n", p=P)

        def choose(e, numbers, out, factor, count):
            for tt in range(TT):
                last = V.tensor_scalar(out[:, tt, :], numbers, slot[:, tt, bass.ds(e, 1)],
                                       gate[:, tt, bass.ds(e, 1)] if factor else None, ALU.is_equal,
                                       **({"op1": ALU.mult} if factor else {}))
                mark = count.add(last)
            return mark

        def select_bias(e):
            return V.tensor_scalar(brow_of[:], self.ones[:, 0:SLOTS], self.ident[:, bass.ds(e, 1)], None, ALU.mult)

        def gather():
            for k in range(KD):
                for tt in range(TT):
                    last = M.matmul(Xg[:, k, :], self.x[:, tt, k * P:(k + 1) * P], one_hot[:, tt, :],
                                    start=(tt == 0), stop=(tt == TT - 1))
            return last

        def halves(ps, lhsT, rhs, **flags):
            M.matmul(ps[0:SLOTS], lhsT, rhs[0], **flags)
            return M.matmul(ps[SLOTS:P], lhsT, rhs[1], **flags)

        def up(inp, arrived, free):
            for q in range(2):
                halves(U[:, q, :], brow_of[:], [brow[:, c:c + 512] for c in (512 * q, D + 512 * q)],
                       start=True, stop=False)
            for j in range(4):
                pe.after(arrived(j))
                for r in range(2):
                    for q in range(2):
                        last = halves(U[:, q, :], inp[:, 2 * j + r, 0:SLOTS],
                                      [panel[j][:, r, c:c + 512] for c in (512 * q, D + 512 * q)],
                                      start=False, stop=(j == 3 and r == 1))
                if free and j < 3:
                    free.add(last)
            return last

        def activate(d, s, ready, read, tiles):
            even, odd = (U.rearrange("p a b -> p (a b)")[:, i::2] for i in range(2))
            d.after(ready)
            m1 = d.do(V.tensor_scalar(glu[:], even, SWIGLU_LIMIT, None, ALU.min))
            k = s.after(m1).do(A.activation(sig[:], glu[:], ACT.Sigmoid, scale=SWIGLU_ALPHA))
            m2 = read.add(V.tensor_scalar(lin[:], odd, -SWIGLU_LIMIT, SWIGLU_LIMIT, ALU.max, ALU.min))
            m3 = d.after(m2).do(V.scalar_tensor_tensor(lin[:], lin[:], 1.0, glu[:], ALU.add, ALU.mult))
            d.after(m3, k)
            return tiles.add(V.tensor_tensor(glu[:], lin[:], sig[:], ALU.mult))

        def transpose_activated(after_first=None):
            for n in range(4):
                last = M.transpose(AT[:, n * P:(n + 1) * P], glu[:, n * P:(n + 1) * P], self.ident[:])
                if n == 0 and after_first:
                    after_first.add(last)
            return last

        def down(arrived, free):
            for j in range(2):
                pe.after(arrived(j))
                for r in range(4):
                    k = 4 * j + r
                    last = halves(DN, actT[:, r, j * SLOTS:(j + 1) * SLOTS],
                                  [panel[4 + j][:, r, c:c + 512] for c in (0, 512)],
                                  start=(k == 0), stop=(k == KD - 1))
                if free and j == 0:
                    free.add(last)
            return last

        def transpose_weighted(after_first=None):
            for ab in range(2):
                for tt in range(TT):
                    c = (2 * ab + tt) * P
                    last = M.transpose(AT[:, c:c + P], weighted[:, ab, tt, :], self.ident[:])
                    if ab == tt == 0 and after_first:
                        after_first.add(last)
            return last

        def scatter_tile(tt, matrix, rows):
            for ab in range(2):
                last = M.matmul((S, X)[tt][:, ab, :], matrix[:, ab, tt * P:(tt + 1) * P], rows[:],
                                start=True, stop=True)
            return last

        def add_tile(tt):
            return V.tensor_tensor(acc[:, tt, :], acc[:, tt, :],
                                   (S, X)[tt][:].rearrange("p a b -> p (a b)"), ALU.add)

        at4 = AT.rearrange("p (n s) -> p n s", s=P)
        at2 = AT.rearrange("p (a t) -> p a t", t=T)

        for eng, counts in ((pe, (up_done, act_T, down_done, weighted_T, scattered)),
                            (act, (act_copied, y_copied, scatter_copied)),
                            (dve, (activated, gated))):
            for n in counts:
                eng.engine.sem_inc(n.sem, 1)
                n.n += 1
        dve.after(slots, pool.done.now())
        m = choose(0, iota[:, 0:P], one_hot, False, built)
        pe.after(m, *ln1)
        m = gathered.add(gather())
        act.after(m)
        gather_copied.add(A.activation(xg[:], Xg[:], ACT.Copy))
        selected.add(select_bias(0))
        m = dve.after(k).do(V.reciprocal(st[:, :, 1:2], st[:, :, 1:2]))
        m = dve.after(m).do(V.tensor_tensor(gn[:], gts[:], st[:, :, 1:2].to_broadcast([P, TT, TOPK]), ALU.mult))
        dve.after(m)
        picks = [dve.do(V.tensor_tensor(gated_choice[:, tt], choice[:, tt],
                                        gn[:, tt, :].unsqueeze(2).to_broadcast([P, TOPK, NE]), ALU.mult))
                 for tt in range(TT)]
        m = dve.after(*picks).do(V.tensor_reduce(
            gate[:, :, 0:NE], gated_choice[:].rearrange("p t j e -> p t e j"), axis=AX.X, op=ALU.add))
        pe.after(m)
        for tt in range(TT):
            last = M.transpose(S[0:NE, 0, tt * P:(tt + 1) * P], gate[:, tt, 0:NE], self.ident[:])
        m = dve.after(pe.do(last)).do(V.tensor_copy(gT[0:NE, :], S[0:NE, 0, 0:T]))
        pe.after(m, biases)
        for tt, (ps, read) in enumerate(((S, hidden_read), (self.psA[:, 2:4, :], summed))):
            for half in range(2):
                last = M.matmul(ps[:, half, :], gT[:, tt * P:(tt + 1) * P],
                                bdown[:, half * 512:(half + 1) * 512], start=True, stop=True)
            dve.after(pe.do(last))
            read.add(V.scalar_tensor_tensor(acc[:, tt, :], self.x[:, tt, :], ALPHA,
                                            ps[:].rearrange("p a b -> p (a b)"), ALU.mult, ALU.add))
        pe.after(z, biases, slots)
        act.after(z)
        for eng in (pe, dve, act):
            eng.after(counted)
            eng.settle(self.settled)

        shares = {self.freed: 6, dve.done: 2, act.done: 1, gathered: 1, gather_copied: 1, up_done: 1,
                  selected: 1, hidden_read: 1, activated: 1, act_T: 1, act_copied: 1, down_done: 1,
                  y_copied: 1, weighted_T: 1, scatter_copied: 1, scattered: 2, summed: 2, built: 2, gated: 4,
                  px.done: 21, dx.done: 45, ax.done: 15, **{self.arrived[s]: 1 for s in order}}
        named = [n for n in shares if n not in (px.done, dx.done, ax.done, self.freed)]
        with Loop(nc, NE, shares) as e:
            marks = []
            for j, src in enumerate(sources(e)):
                self.sp.after((self.freed, self.freed.n - 5 + j, self.freed.loop))
                self.sp.settle(self.settled)
                marks.append(self.arrived[order[j]].add(nc.sync.dma_start(panel[j], src)))
            tokens = nc.values_load(cnt[0:1, bass.ds(e, 1)], min_val=0, max_val=T,
                                    engines=[x.engine.engine for x in (pe, dve, act)])
            dve.after(*(n.before_iteration() for n in (dve.done, selected, built, gated, hidden_read,
                                                       activated, summed, gathered)))
            m_built = choose(e + 1, iota[:, 0:P], one_hot, False, built)
            dve.after(weighted_T.before_iteration())
            for ab in range(2):
                m_gated = choose(e, iota_ab[:, ab, :], weighted[:, ab], True, gated)

            def dense_part(free):
                pe.after(gather_copied.before_iteration(), hidden_read.before_iteration(),
                         selected.before_iteration())
                m = {"up": up_done.add(up(xg, lambda j: marks[j], free))}
                pe.after(m_built, summed.before_iteration())
                m["gather"] = gathered.add(gather())
                pe.after(y_copied.before_iteration(), scatter_copied.before_iteration())
                m["s0"] = scattered.add(scatter_tile(0, scatter, y))
                pe.after((activated, activated.n + 1, activated.loop))
                m["act"] = act_T.add(transpose_activated(free))
                pe.after((gather_copied, gather_copied.n + 1, gather_copied.loop))
                m["s1"] = scattered.add(scatter_tile(1, scatter, y))
                pe.after((act_copied, act_copied.n + 1, act_copied.loop))
                m["down"] = down_done.add(down(lambda j: marks[4 + j], free))
                pe.after(m_gated)
                m["weighted"] = weighted_T.add(transpose_weighted(free))
                return m

            counts = (self.freed, up_done, gathered, scattered, act_T, down_done, weighted_T)
            state, waited = [n.n for n in counts], dict(pe.waited)
            with nc.tensor.If(tokens < SLOTS + 1):
                m = dense_part(self.freed)
            for n, v in zip(counts, state):
                n.n = v
            pe.waited = waited
            with nc.tensor.Else():
                m = dense_part(None)
            self.freed.n = state[0] + 6
            dve.after(act_T.before_iteration())
            activate(dve, act, m["up"], hidden_read, activated)
            selected.add(select_bias(e + 1))
            act.after(m["gather"], m["up"])
            gather_copied.add(A.activation(xg[:], Xg[:], ACT.Copy))
            act.after(m["act"], down_done.before_iteration())
            act_copied.add(A.activation(actT[:], at4, ACT.Copy))
            for tt in range(TT):
                dve.after(m[f"s{tt}"])
                summed.add(add_tile(tt))
            act.after(m["down"], m["s1"])
            y_copied.add(A.activation(y[:], DN, ACT.Copy))
            act.after(m["weighted"])
            scatter_copied.add(A.activation(scatter[:], at2, ACT.Copy))

            def free_after(base, mark, panels):
                if base == SLOTS:
                    px.after(mark).settle(self.settled)
                    with nc.tensor.If(tokens < 2 * SLOTS + 1):
                        nc.tensor.sem_inc(self.freed.sem, panels)

            def extra_pass(base):
                m = dx.do(V.tensor_scalar(ids[:], iota_ab[:], float(base), None, ALU.add))
                m = choose(e, iota[:, base:base + SLOTS], one_hot[:, :, 0:SLOTS], False, dx.done)
                m = px.after(m).do(gather())
                m = ax.after(m).do(A.activation(xg_x[:], Xg[:], ACT.Copy))
                px.after(dx.after(px.done.now()).do(select_bias(e)), m)
                m = px.do(up(xg_x, lambda j: None, None))
                free_after(base, m, 4)
                m = activate(dx, ax, m, dx.done, dx.done)
                m = px.after(m).do(transpose_activated())
                m = ax.after(m).do(A.activation(actT[:], at4, ACT.Copy))
                px.after(m)
                m = px.do(down(lambda j: None, None))
                free_after(base, m, 2)
                ax.after(m).do(A.activation(y_x[:], DN, ACT.Copy))
                dx.after(px.done.now(), dx.done.now())
                dx.do(select_bias(e + 1))
                for ab in range(2):
                    m = choose(e, ids[:, ab, :], weighted[:, ab], True, dx.done)
                m = px.after(m, ax.done.now()).do(transpose_weighted())
                m = ax.after(m).do(A.activation(scatter_x[:], at2, ACT.Copy))
                px.after(m, ax.done.now())
                for tt in range(TT):
                    m = px.do(scatter_tile(tt, scatter_x, y_x))
                    dx.after(m).do(add_tile(tt))

            over = (pe, dve, act)
            lines = (px, dx, ax)

            def passes(bases, condition, entry):
                kept = [dict(eng.waited) for eng in over + lines]
                start = [x.done.n for x in lines]
                branch = nc.If(condition)
                branch.__enter__()
                for eng in over:
                    eng.after(*entry)
                for eng, x in zip(over, lines):
                    x.waited = eng.waited
                for base in bases:
                    extra_pass(base)
                for eng in over:
                    eng.after(*(x.done.now() for x in lines))
                    eng.settle(self.settled)
                branch.__exit__(None, None, None)
                with nc.Else():
                    for eng, x, n in zip(over, lines, start):
                        eng.engine.sem_inc(x.done.sem, x.done.n - n)
                for eng, waited in zip(over + lines, kept):
                    eng.waited = waited

            entry = [n.now() for n in named]
            passes((SLOTS,), tokens > SLOTS, entry)
            passes((2 * SLOTS, 3 * SLOTS), tokens > 2 * SLOTS, [x.done.now() for x in lines] + entry)
            with nc.tensor.If(tokens > 2 * SLOTS):
                nc.tensor.sem_inc(self.freed.sem, 6)

        pe.after(y_copied.now(), scatter_copied.now(), gather_copied.now(), summed.now())
        s0 = scattered.add(scatter_tile(0, scatter, y))
        s1 = scattered.add(scatter_tile(1, scatter, y))
        dve.after(s0, summed.now())
        summed.add(add_tile(0))
        dve.after(s1)
        m = summed.add(add_tile(1))
        dve.after(m)
        out = self.layer_norm(acc, ln[:, 2, :], ln[:, 3, :], c)
        for tt in range(TT):
            self.sp.after(out[tt])
            self.stored.add(nc.sync.dma_start(self.out[0, tt * P:(tt + 1) * P, :], acc[:, tt, :]))
        self.sp.after(self.stored.now())


def build(nc, ctx, arrays, out):
    k = Kernel(nc, ctx, arrays, out)
    k.setup()
    k.griffin()
    k.mlp(0)
    k.fox()
    k.mlp(1)
    k.hybrid()
    k.moe()


_INS = [
    "x", "mix_norm", "mlp_norm", "mlp_w1", "mlp_w2", "lru_w_in", "lru_conv_w", "lru_conv_b", "lru_w_r",
    "lru_b_r", "lru_w_i", "lru_b_i", "lru_lambda", "lru_w_out", "fox_w_in", "fox_b_f", "fox_q_gain",
    "fox_k_gain", "fox_w_out", "w_in_2", "hgrn_lb_logits_2", "hgrn_norm_g_2", "w_branch_sb_2",
    "w_branch_hgrn_2", "w_out_2", "ln1_g_2", "ln1_b_2", "router_w_2", "router_b_2", "expert_w_up_2",
    "expert_b_up_2", "expert_w_down_2", "expert_b_down_2", "ln2_g_2", "ln2_b_2",
]


def kernel(**inputs):
    import concourse.bacc as _bacc
    import numpy as _np
    from concourse.bass_utils import run_bass_kernel_spmd as _run

    nc = _bacc.Bacc("TRN2", target_bir_lowering=False, num_devices=1)
    arrays, aps = {}, {}
    for name in _INS:
        a = _np.ascontiguousarray(inputs[name])
        arrays[f"in_{name}"] = a
        aps[name] = nc.dram_tensor(f"in_{name}", a.shape, mybir.dt.from_np(a.dtype), kind="ExternalInput").ap()
    out = nc.dram_tensor("out_x", (1, T, D), F32, kind="ExternalOutput").ap()
    with ExitStack() as ctx:
        build(nc, ctx, aps, out)
    r = _run(nc, [arrays], core_ids=[0])
    return r.results[0]["out_x"]
```
